# Optimizing a Trainium2 kernel written in Bass

```python
import math
import jax, jax.numpy as jnp
from jax import lax
import numpy as np

D_MODEL = 1024
BATCH = 1
SEQ = 512
DEPTH = 2

N_MIXERS = 2
N_MLA_LAYERS = (DEPTH + 1) // 2
N_MLSTM_LAYERS = DEPTH // 2

MLA_HEADS = 16
MLA_Q_RANK = 512
MLA_KV_RANK = 256
MLA_NOPE_DIM = 64
MLA_ROPE_DIM = 32
MLA_V_DIM = 64
MLA_QK_DIM = MLA_NOPE_DIM + MLA_ROPE_DIM
MLA_IN_DIM = MLA_Q_RANK + MLA_KV_RANK + MLA_ROPE_DIM
ROPE_THETA = 10000.0
ATTN_BLOCK = 128

MLSTM_HEADS = 8
MLSTM_QK_DIM = 64
MLSTM_V_DIM = 128
MLSTM_CONV = 4
MLSTM_CHUNK = 64
GATE_SOFTCAP = 15.0
MLSTM_QK_WIDTH = 2 * MLSTM_HEADS * MLSTM_QK_DIM
MLSTM_HV = MLSTM_HEADS * MLSTM_V_DIM
MLSTM_IN_DIM = MLSTM_QK_WIDTH + 2 * MLSTM_HV + 2 * MLSTM_HEADS

MLP_HIDDEN = 4 * D_MODEL
EPS = 1e-6

kernel_name = "mla_mlstm_interleaved_hybrid"

def rms_norm(x, g):
    xf = x.astype(jnp.float32)
    y = xf * lax.rsqrt(jnp.mean(xf * xf, axis=-1, keepdims=True) + EPS)
    return (y * g.astype(jnp.float32)).astype(x.dtype)

def softcap(x, cap):
    return cap * jnp.tanh(x / cap)

def rope_tables(positions, dim):
    inv = ROPE_THETA ** (-jnp.arange(0, dim, 2, dtype=jnp.float32) / dim)
    ang = positions.astype(jnp.float32)[..., None] * inv
    return jnp.cos(ang), jnp.sin(ang)

def apply_rope(x, cos, sin):
    xf = x.astype(jnp.float32)
    half = xf.shape[-1] // 2
    x1, x2 = xf[..., :half], xf[..., half:]
    out = jnp.concatenate([x1 * cos - x2 * sin, x1 * sin + x2 * cos], axis=-1)
    return out.astype(x.dtype)

def mla_mixer(u, cos, sin, w_in, g_q, g_kv, w_uq, w_ukv, w_o):
    B, S, _ = u.shape
    proj = u @ w_in
    c_q = proj[..., :MLA_Q_RANK]
    c_kv = proj[..., MLA_Q_RANK:MLA_Q_RANK + MLA_KV_RANK]
    k_r = proj[..., MLA_Q_RANK + MLA_KV_RANK:]
    q = (rms_norm(c_q, g_q) @ w_uq).reshape(B, S, MLA_HEADS, MLA_QK_DIM)
    q_n = q[..., :MLA_NOPE_DIM]
    q_r = apply_rope(q[..., MLA_NOPE_DIM:], cos[:, :, None, :], sin[:, :, None, :])
    kv = (rms_norm(c_kv, g_kv) @ w_ukv).reshape(B, S, MLA_HEADS, MLA_NOPE_DIM + MLA_V_DIM)
    k_n = kv[..., :MLA_NOPE_DIM]
    v = kv[..., MLA_NOPE_DIM:]
    k_r = apply_rope(k_r, cos, sin)
    scale = MLA_QK_DIM ** -0.5
    outs = []
    for blk in range(S // ATTN_BLOCK):
        q0 = blk * ATTN_BLOCK
        k_end = q0 + ATTN_BLOCK
        s = (jnp.einsum('bqhd,bkhd->bhqk', q_n[:, q0:k_end], k_n[:, :k_end])
             + jnp.einsum('bqhr,bkr->bhqk', q_r[:, q0:k_end], k_r[:, :k_end])).astype(jnp.float32) * scale
        q_idx = q0 + jnp.arange(ATTN_BLOCK)
        k_idx = jnp.arange(k_end)
        s = jnp.where(k_idx[None, :] <= q_idx[:, None], s, -jnp.inf)
        p = jax.nn.softmax(s, axis=-1).astype(v.dtype)
        outs.append(jnp.einsum('bhqk,bkhd->bqhd', p, v[:, :k_end]))
    o = jnp.concatenate(outs, axis=1).reshape(B, S, MLA_HEADS * MLA_V_DIM)
    return o @ w_o

def causal_depthwise_conv(x, w, b):
    C = x.shape[-1]
    y = lax.conv_general_dilated(x, w[:, None, :].astype(x.dtype), window_strides=(1,),
                                 padding=[(w.shape[0] - 1, 0)],
                                 dimension_numbers=('NWC', 'WIO', 'NWC'),
                                 feature_group_count=C)
    return y + b.astype(x.dtype)

def mlstm_chunkwise(q, k, v, ig, lf):
    B, S, H, DK = q.shape
    DV = v.shape[-1]
    L = MLSTM_CHUNK
    NC = S // L

    def to_chunks(a):
        a = a.astype(jnp.float32).reshape((B, NC, L, H) + a.shape[3:])
        return jnp.moveaxis(jnp.moveaxis(a, 1, 0), 3, 2)

    causal = jnp.tril(jnp.ones((L, L), dtype=bool))

    def step(carry, xs):
        C, n, m = carry
        qc, kc, vc, ic, fc = xs
        b = jnp.cumsum(fc, axis=-1)
        d = jnp.where(causal, b[..., :, None] - b[..., None, :] + ic[..., None, :], -jnp.inf)
        inter = b + m[..., None]
        m_t = jnp.maximum(inter, jnp.max(d, axis=-1))
        w_intra = jnp.exp(d - m_t[..., None])
        a_inter = jnp.exp(inter - m_t)
        s = jnp.einsum('bhjd,bhsd->bhjs', qc, kc) * w_intra
        num = (a_inter[..., None] * jnp.einsum('bhvd,bhjd->bhjv', C, qc)
               + jnp.einsum('bhjs,bhsv->bhjv', s, vc))
        den = a_inter * jnp.einsum('bhd,bhjd->bhj', n, qc) + jnp.sum(s, axis=-1)
        h = num / jnp.maximum(jnp.abs(den), jnp.exp(-m_t))[..., None]
        b_end = b[..., -1]
        g = b_end[..., None] - b + ic
        m_new = jnp.maximum(b_end + m, jnp.max(g, axis=-1))
        a_st = jnp.exp(b_end + m - m_new)
        w_st = jnp.exp(g - m_new[..., None])
        C_new = a_st[..., None, None] * C + jnp.einsum('bhs,bhsv,bhsd->bhvd', w_st, vc, kc)
        n_new = a_st[..., None] * n + jnp.einsum('bhs,bhsd->bhd', w_st, kc)
        return (C_new, n_new, m_new), h

    init = (jnp.zeros((B, H, DV, DK), jnp.float32),
            jnp.zeros((B, H, DK), jnp.float32),
            jnp.zeros((B, H), jnp.float32))
    _, hs = lax.scan(step, init, (to_chunks(q), to_chunks(k), to_chunks(v), to_chunks(ig), to_chunks(lf)))
    hs = jnp.moveaxis(jnp.moveaxis(hs, 2, 3), 0, 1)
    return hs.reshape(B, S, H, DV)

def mlstm_mixer(u, w_in, conv_w, conv_b, i_b, f_b, head_g, w_o):
    B, S, _ = u.shape
    H = MLSTM_HEADS
    proj = u @ w_in
    qk_pre = proj[..., :MLSTM_QK_WIDTH]
    v = proj[..., MLSTM_QK_WIDTH:MLSTM_QK_WIDTH + MLSTM_HV].reshape(B, S, H, MLSTM_V_DIM)
    o_pre = proj[..., MLSTM_QK_WIDTH + MLSTM_HV:MLSTM_QK_WIDTH + 2 * MLSTM_HV]
    i_pre = proj[..., MLSTM_QK_WIDTH + 2 * MLSTM_HV:MLSTM_QK_WIDTH + 2 * MLSTM_HV + H]
    f_pre = proj[..., MLSTM_QK_WIDTH + 2 * MLSTM_HV + H:]
    qk = jax.nn.silu(causal_depthwise_conv(qk_pre, conv_w, conv_b))
    q = qk[..., :H * MLSTM_QK_DIM].reshape(B, S, H, MLSTM_QK_DIM)
    k = qk[..., H * MLSTM_QK_DIM:].reshape(B, S, H, MLSTM_QK_DIM) * (MLSTM_QK_DIM ** -0.5)
    ig = softcap((i_pre + i_b).astype(jnp.float32), GATE_SOFTCAP)
    lf = jax.nn.log_sigmoid(softcap((f_pre + f_b).astype(jnp.float32), GATE_SOFTCAP))
    h = mlstm_chunkwise(q, k, v, ig, lf)
    h = rms_norm(h, head_g.reshape(H, MLSTM_V_DIM)).astype(u.dtype).reshape(B, S, MLSTM_HV)
    return (jax.nn.sigmoid(o_pre) * h) @ w_o

def squared_relu_mlp(u, w1, w2):
    a = jnp.maximum(u @ w1, 0)
    return (a * a) @ w2

def setup_inputs(seed: int = 0) -> dict:
    key = jax.random.key(seed)
    ks = iter(jax.random.split(key, 32))
    f32 = jnp.float32

    def w(shape, fan_in):
        return jax.random.normal(next(ks), shape, f32) * (fan_in ** -0.5)

    def gain(shape):
        return 1.0 + 0.02 * jax.random.normal(next(ks), shape, f32)

    x = jax.random.normal(next(ks), (BATCH, SEQ, D_MODEL), f32)
    offsets = jax.random.randint(next(ks), (BATCH, 1), 0, 4096, dtype=jnp.int32)
    positions = (offsets + jnp.arange(SEQ, dtype=jnp.int32)[None, :]).astype(jnp.int32)
    NA, NM = N_MLA_LAYERS, N_MLSTM_LAYERS
    f_bias = (jnp.linspace(3.0, 6.0, MLSTM_HEADS, dtype=f32)[None, :]
              + 0.1 * jax.random.normal(next(ks), (NM, MLSTM_HEADS), f32))
    return {
        "x": x,
        "positions": positions,
        "norm_mix_g": gain((DEPTH, D_MODEL)),
        "norm_mlp_g": gain((DEPTH, D_MODEL)),
        "final_g": gain((D_MODEL,)),
        "mla_w_in": w((NA, D_MODEL, MLA_IN_DIM), D_MODEL),
        "mla_q_norm_g": gain((NA, MLA_Q_RANK)),
        "mla_kv_norm_g": gain((NA, MLA_KV_RANK)),
        "mla_w_uq": w((NA, MLA_Q_RANK, MLA_HEADS * MLA_QK_DIM), MLA_Q_RANK),
        "mla_w_ukv": w((NA, MLA_KV_RANK, MLA_HEADS * (MLA_NOPE_DIM + MLA_V_DIM)), MLA_KV_RANK),
        "mla_w_o": w((NA, MLA_HEADS * MLA_V_DIM, D_MODEL), MLA_HEADS * MLA_V_DIM),
        "mlstm_w_in": w((NM, D_MODEL, MLSTM_IN_DIM), D_MODEL),
        "mlstm_conv_w": w((NM, MLSTM_CONV, MLSTM_QK_WIDTH), MLSTM_CONV),
        "mlstm_conv_b": 0.02 * jax.random.normal(next(ks), (NM, MLSTM_QK_WIDTH), f32),
        "mlstm_i_b": 0.1 * jax.random.normal(next(ks), (NM, MLSTM_HEADS), f32),
        "mlstm_f_b": f_bias,
        "mlstm_head_norm_g": gain((NM, MLSTM_HV)),
        "mlstm_w_o": w((NM, MLSTM_HV, D_MODEL), MLSTM_HV),
        "mlp_w1": w((DEPTH, D_MODEL, MLP_HIDDEN), D_MODEL),
        "mlp_w2": w((DEPTH, MLP_HIDDEN, D_MODEL), MLP_HIDDEN),
    }

def reference(x, positions, norm_mix_g, norm_mlp_g, final_g,
              mla_w_in, mla_q_norm_g, mla_kv_norm_g, mla_w_uq, mla_w_ukv, mla_w_o,
              mlstm_w_in, mlstm_conv_w, mlstm_conv_b, mlstm_i_b, mlstm_f_b, mlstm_head_norm_g, mlstm_w_o,
              mlp_w1, mlp_w2):
    cos, sin = rope_tables(positions, MLA_ROPE_DIM)
    h = x
    for layer in range(DEPTH):
        u = rms_norm(h, norm_mix_g[layer])
        j = layer // N_MIXERS
        if layer % N_MIXERS == 0:
            h = h + mla_mixer(u, cos, sin, mla_w_in[j], mla_q_norm_g[j], mla_kv_norm_g[j],
                              mla_w_uq[j], mla_w_ukv[j], mla_w_o[j])
        else:
            h = h + mlstm_mixer(u, mlstm_w_in[j], mlstm_conv_w[j], mlstm_conv_b[j], mlstm_i_b[j],
                                mlstm_f_b[j], mlstm_head_norm_g[j], mlstm_w_o[j])
        u = rms_norm(h, norm_mlp_g[layer])
        h = h + squared_relu_mlp(u, mlp_w1[layer], mlp_w2[layer])
    return rms_norm(h, final_g)


_drawn_inputs = setup_inputs


def setup_inputs(seed=0):
    import zlib

    import numpy as np

    out = dict(_drawn_inputs(seed))
    spreads = {}
    factors = {'norm_mix_g': 4.906,
     'final_g': 19.873,
     'mla_q_norm_g': 8.0,
     'mla_kv_norm_g': 8.0,
     'mlstm_conv_b': 188.161,
     'mlstm_i_b': 49.507,
     'mlstm_head_norm_g': 200.0,
     'norm_mlp_g': 8.0}
    for name, (base, spread) in spreads.items():
        noise = np.random.default_rng([zlib.crc32(name.encode()), seed]).standard_normal(out[name].shape)
        drawn = base * np.exp(spread * noise) if base else spread * noise
        out[name] = __import__('jax').numpy.asarray(drawn.astype(out[name].dtype))
    for name, factor in factors.items():
        out[name] = (out[name] * factor).astype(out[name].dtype)
    return out
```

```python
import numpy as np
import concourse.bass as bass
from concourse import mybir
from contextlib import ExitStack

F32 = mybir.dt.float32
F32R = mybir.dt.float32r
I32 = mybir.dt.int32
ALU = mybir.AluOpType
ACT = mybir.ActivationFunctionType
AX = mybir.AxisListType
ds = bass.ds

P = 128
S = 512
D = 1024
KD = D // P
TT = S // P
QRANK, KVRANK, NOPE, ROPE, VD = 512, 256, 64, 32, 64
QK = NOPE + ROPE
HEADS = 16
PAIRS = HEADS // 2
MH = 8
MPAIRS = MH // 2
CONV = 4
HID = 4096
QUARTERS = HID // D
CAP = 15.0
EPS = 1e-6
THETA = 10000.0
SCALE = QK ** -0.5
NEG = -1e30
MAGIC = 1.5 * 2.0 ** 23
TWO_PI_1 = 6.28125
TWO_PI_2 = float(np.float32(np.floor((2 * np.pi - 6.28125) * 2 ** 21) / 2 ** 21))
TWO_PI_3 = float(np.float32(2 * np.pi - 6.28125 - TWO_PI_2))
PI_IN = 3.1415925

G_MIX, G_MLP, G_FIN = 0, 16, 32
G_Q, G_KV = 40, 44
CONV_W, CONV_B, G_HEAD = 46, 78, 86
PCOLS = 94

N_KV, N_KR, N_Q = 0, 1, 2
N_PAIR = 4
N_WO = N_PAIR + 2 * PAIRS
N_MLP = [N_WO + 4, 0]
N_GATE = N_MLP[0] + 8 * QUARTERS
N_QK, N_V, N_O, N_WO2 = N_GATE + 1, N_GATE + 5, N_GATE + 9, N_GATE + 13
N_MLP[1] = N_GATE + 17

T_IN = KD
T_WO = T_IN + 8
T_MLP = [T_WO + 8, 0]
T_GATE = T_MLP[0] + 16 * QUARTERS
T_QK, T_V, T_O, T_WO2 = T_GATE + 1, T_GATE + 9, T_GATE + 17, T_GATE + 25
T_MLP[1] = T_GATE + 33
RING = 4
B_Q, B_KV, B_S, B_PT, B_PV = 0, 1, 2, 4, 6
B_ST, B_NUM, B_DEN, B_MS = 2, 4, 6, 7
B_OUT, B_BC, B_COL = 4, 6, 7

NORM_MIX0, NORM_KV, NORM_CQ, NORM_MLP0, NORM_MIX1, NORM_MLP1, NORM_FIN = range(7)
NORM_TILES = [KD, KVRANK // P, QRANK // P, KD, KD, KD, KD]


def adds_before(norm):
    return sum(n - 1 for n in NORM_TILES[:norm])


def strip_over(n, gemm_done, q_mm):
    if n < N_PAIR:
        return gemm_done, T_IN + 2 * n + 2
    if n < N_WO:
        return q_mm, n - N_PAIR + 1
    if n < N_GATE:
        return gemm_done, T_WO + 2 * (n - N_WO) + 2
    return gemm_done, T_GATE + 1 + 2 * (n - N_GATE)


def raw_count(n):
    return sum(48 if N_PAIR <= m < N_WO else 16 for m in range(n % 2, n + 1, 2))


def trunk(nc, a, out):
    ctx = ExitStack()
    with ctx:
        ctx.enter_context(nc.allow_non_contiguous_dma(reason="small parameters"))

        def sb(name, shape, dt=F32):
            return ctx.enter_context(nc.sbuf_tensor(name, shape, dt))

        def sem(name):
            return ctx.enter_context(nc.semaphore(name))

        h = sb("h", [P, KD, S])
        raw = [sb(f"raw{s}", [P, 2048]) for s in range(2)]
        whi = [sb(f"whi{s}", [P, 2048], F32R) for s in range(2)]
        wlo = [sb(f"wlo{s}", [P, 2048], F32R) for s in range(2)]
        xh = sb("xh", [P, KD, S], F32R)
        xl = sb("xl", [P, KD, S], F32R)
        uh = sb("uh", [P, KD, S], F32R)
        ul = sb("ul", [P, KD, S], F32R)
        ident = sb("ident", [P, P])
        ones = sb("ones", [P, P])
        mask_s = sb("mask_s", [P, P])
        mask_w = sb("mask_w", [P, P])
        identr = sb("identr", [P, P], F32R)
        onesr = sb("onesr", [P, 2], F32R)
        maskr = sb("maskr", [P, P], F32R)
        mhalf = sb("mhalf", [P, 8])
        prow = sb("prow", [PCOLS, P])
        pcol = sb("pcol", [P, PCOLS])
        acc = sb("acc", [P, S])
        sq = sb("sq", [P, 2, S])
        r_a = sb("r_a", [P, S])
        r_b = sb("r_b", [P, S])
        diag = sb("diag", [P, 2, S])
        var = sb("var", [P, 4])
        rcol = sb("rcol", [P, 4])
        rope_c = sb("rope_c", [P, 2])
        gate_b = sb("gate_b", [MH, 4])
        nmax = sb("nmax", [P, 4])
        rsum = sb("rsum", [P, 4])
        rinv = sb("rinv", [P, 4])
        gcol = sb("gcol", [P, TT * MH])
        encol = sb("encol", [P, MH * TT])
        dcp = sb("dcp", [P, 8])
        dd = sb("dd", [P, 8])
        var2 = sb("var2", [P, 8])
        rc2 = sb("rc2", [P, 8])
        top = nc.sbuf_base
        arena_bytes = 60 * 1024
        sb("arena", [P, arena_bytes // 4])
        top = (top + 31) // 32 * 32

        class Arena:
            def __init__(self, at=0):
                self.at = at

            def __call__(self, name, shape, dt=F32):
                size = 4 * int(np.prod(shape[1:]))
                t = nc.alloc_sbuf_tensor_at(name, shape, dt, offset=top + self.at)
                self.at += (size + 31) // 32 * 32
                assert self.at <= arena_bytes, (name, self.at)
                return t

        A = Arena()
        x_tok = Arena(0)("x_tok", [P, TT, D])
        ckv = A("ckv", [P, 2, S])
        cq = A("cq", [P, 4, S])
        krot = A("krot", [P, S])
        krot2 = A("krot2", [P, S])
        cqh = A("cqh", [P, 4, S], F32R)
        cql = A("cql", [P, 4, S], F32R)
        ckvh = A("ckvh", [P, 2, S], F32R)
        ckvl = A("ckvl", [P, 2, S], F32R)
        vh = A("vh", [P, TT, P], F32R)
        vl = A("vl", [P, TT, P], F32R)
        prob = A("prob", [P, 2, S])
        cos = A("cos", [P, S])
        sin = A("sin", [P, S])
        tab = A("tab", [P, S])
        qtmp = A("qtmp", [P, S])
        B = Arena(16 * 1024)
        pos_i = B("pos_i", [P, S], I32)
        ang = B("ang", [P, S])
        turn = B("turn", [P, S])
        pth, ptl = xh[:, 0:TT, :], xl[:, 0:TT, :]
        kh = [xh[:, 4 + e, :] for e in range(2)]
        kl = [xl[:, 4 + e, :] for e in range(2)]
        qh = [xh[:, 6 + e, :] for e in range(2)]
        ql = [xl[:, 6 + e, :] for e in range(2)]

        C = Arena()
        v_tok = C("v_tok", [P, TT, D])
        sg = C("sg", [P, MH, S])
        base = C.at
        qph = C("qph", [P, 2, S], F32R)
        qpl = C("qpl", [P, 2, S], F32R)
        mb = C("mb", [P, 2, S])
        md = C("md", [P, 2 * S])
        wt = C("wt", [P, 2, S])
        sw = C("sw", [P, 2, S])
        rb = C("rb", [P, 2, S])
        numsq = md[:, :].rearrange("p (e t) -> p e t", e=2)
        G = Arena(base)
        gi = G("gi", [MH, S])
        gf = G("gf", [MH, S])
        Fc = G("Fc", [MH, S])
        Gc = G("Gc", [MH, S])
        Mc = G("Mc", [MH, S])
        en = G("en", [MH, S])
        zrow = G("zrow", [MH, S])
        E = Arena(base + 16 * 1024)
        cpad = E("cpad", [P, S + CONV - 1])
        yc = E("yc", [P, 2, S])
        ys = E("ys", [P, 2, S])
        otmp = yc

        def flat(t):
            return t[:, :, :].rearrange("p k s -> p (k s)")

        TRI = [0, 512, 896, 1152]
        LEN = [512, 384, 256, 128]

        def swh(e, j):
            return flat(xh)[:, 1280 * e + TRI[j]:1280 * e + TRI[j] + LEN[j]]

        def swl(e, j):
            return flat(xl)[:, 1280 * e + TRI[j]:1280 * e + TRI[j] + LEN[j]]

        mkh, mkl = flat(xh)[:, 2560:3072], flat(xl)[:, 2560:3072]
        mvh = flat(xh)[:, 3072:4096].rearrange("p (t n) -> p t n", t=TT)
        mvl = flat(xl)[:, 3072:4096].rearrange("p (t n) -> p t n", t=TT)

        o_tok = Arena(0)("o_tok", [P, TT, D])
        hg = Arena(16 * 1024)("hg", [P, 2, S])

        m_dram = nc.dram_tensor("m_rows", (MH, S), F32).ap()
        ps = ctx.enter_context(nc.psum_tensor("ps", [P, 8, S], F32))

        def bank(b):
            return ps[:, b, :]

        x_in = [sem(f"x_in{i}") for i in range(2)]
        par_in = sem("par_in")
        pos_in = sem("pos_in")
        raw_full = [sem(f"raw_full{s}") for s in range(2)]
        whi_ready, wlo_ready = sem("whi_ready"), sem("wlo_ready")
        consts = sem("consts")
        par_t, par_ready = sem("par_t"), sem("par_ready")
        gemm_done, gemm_evac = sem("gemm_done"), sem("gemm_evac")
        xh_new, x_ready = sem("xh_new"), sem("x_ready")
        sq_new, acc_add = sem("sq_new"), sem("acc_add")
        stat_col, var_ready, rcol_ready = sem("stat_col"), sem("var_ready"), sem("rcol_ready")
        diag_ready, stat_bc, rbc_ready = sem("diag_ready"), sem("stat_bc"), sem("rbc_ready")
        dve_own = sem("dve_own")
        act_own = sem("act_own")
        pool_own = sem("pool_own")
        ang_ready, trig_ready = sem("ang_ready"), sem("trig_ready")
        kr_new, kr_hi, kr_lo = sem("kr_new"), sem("kr_hi"), sem("kr_lo")
        c_norm, c_hi, c_ready = sem("c_norm"), sem("c_hi"), sem("c_ready")
        q_mm, q_tab, q_hi, q_lo = sem("q_mm"), sem("q_tab"), sem("q_hi"), sem("q_lo")
        k_mm, k_hi, k_lo = sem("k_mm"), sem("k_hi"), sem("k_lo")
        v_mm, v_hi, v_lo = sem("v_mm"), sem("v_hi"), sem("v_lo")
        s_mm, s_max, s_exp, p_norm = sem("s_mm"), sem("s_max"), sem("s_exp"), sem("p_norm")
        t_mm, t_hi, t_lo = sem("t_mm"), sem("t_hi"), sem("t_lo")
        pv_mm, o_hi, o_lo = sem("pv_mm"), sem("o_hi"), sem("o_lo")
        a_new, u_hi, u_ready = sem("a_new"), sem("u_hi"), sem("u_ready")
        y_new, y_hi, y_lo = sem("y_new"), sem("y_hi"), sem("y_lo")
        sig_new, sg_ready = sem("sig_new"), sem("sg_ready")
        g_ln, g_m, g_en = sem("g_ln"), sem("g_m"), sem("g_en")
        m_out, mb_in = sem("m_out"), sem("mb_in")
        g_t, gcol_ready = sem("g_t"), sem("gcol_ready")
        md_ready, kq_ready, mv_hi, mv_lo = sem("md_ready"), sem("kq_ready"), sem("mv_hi"), sem("mv_lo")
        st_mm, w_exp, sw_mul, sw_hi, sw_lo = sem("st_mm"), sem("w_exp"), sem("sw_mul"), sem("sw_hi"), sem("sw_lo")
        num_mm, num_sq, ms_mm = sem("num_mm"), sem("num_sq"), sem("ms_mm")
        var2_ready, rc2_ready, diag2_ready = sem("var2_ready"), sem("rc2_ready"), sem("diag2_ready")
        bc2_mm, rb_ready, hn_ready, hs_ready = sem("bc2_mm"), sem("rb_ready"), sem("hn_ready"), sem("hs_ready")
        g_hi, g_ready = sem("g_hi"), sem("g_ready")
        hg_new, out_t, out_evac, out_ready, stored = (sem("hg_new"), sem("out_t"), sem("out_evac"),
                                                      sem("out_ready"), sem("stored"))

        def fixed(eng):
            eng.wait_ge(consts, 1)

        class Own:
            def __init__(self, eng, semaphore):
                self.eng, self.sem, self.n, self.loop = eng, semaphore, 0, None

            def link(self, ins):
                ins.then_inc(self.sem, 1)
                self.n += 1
                v = self.n if self.loop is None else self.loop[0] * self.loop[1] + self.n
                self.eng.wait_ge(self.sem, v)

            def enter(self, i, start, per):
                self.loop, self.at = (i, per), self.n
                self.n -= start * per

            def leave(self, start, end):
                i, per = self.loop
                assert self.n == self.at - start * per + per, (self.n - self.at + start * per, per)
                self.n, self.loop = self.at + (end - start) * per, None

        def full(t):
            return t[:, :].rearrange("p (k n) -> p k n", k=8)

        def kr_raw(t):
            return t[:, 0:8 * ROPE].rearrange("p (k n) -> p k n", k=8)

        def kr_split(t, which):
            return t[:, 1024 * which:1024 * which + 1024].rearrange("p (k r n) -> p k r n", k=8, r=4)

        def gate_raw(t):
            return t[:, 0:8 * 2 * MH].rearrange("p (k n) -> p k n", k=8)

        def pq_raw(t):
            return t[:, 0:4 * QK].rearrange("p (k n) -> p k n", k=4)

        def pkv_raw(t):
            return t[:, 4 * QK:4 * QK + 256].rearrange("p (k n) -> p k n", k=2)

        def pq(t):
            return t[:, 0:512].rearrange("p (k n) -> p k n", k=4)

        def pkv(t):
            return t[:, 512:768].rearrange("p (k n) -> p k n", k=2)

        def split_parts(n_kind, s):
            r, hi, lo = raw[s], whi[s], wlo[s]
            if n_kind == "full":
                return [(r[:, :], hi[:, :], lo[:, :])]
            if n_kind == "kr":
                half = ROPE // 2
                rr = kr_raw(r)
                parts = []
                for which, dst, src in ((0, 0, 0), (0, half, half), (1, 0, half), (1, half, 0)):
                    src_ap = rr[:, :, src:src + half].unsqueeze(2).broadcast_to([P, 8, 4, half])
                    parts.append((src_ap, kr_split(hi, which)[:, :, :, dst:dst + half],
                                  kr_split(lo, which)[:, :, :, dst:dst + half]))
                return parts
            if n_kind == "gate":
                return [(gate_raw(r)[:, :, MH * g:MH * g + MH], full(hi)[:, :, 32 * g:32 * g + MH],
                         full(lo)[:, :, 32 * g:32 * g + MH]) for g in range(2)]
            assert n_kind == "pair"
            half = ROPE // 2
            return [(pkv_raw(r), pkv(hi), pkv(lo)),
                    (pq_raw(r), pq(hi)[:, :, 0:QK], pq(lo)[:, :, 0:QK]),
                    (pq_raw(r)[:, :, NOPE + half:QK], pq(hi)[:, :, QK:QK + half], pq(lo)[:, :, QK:QK + half]),
                    (pq_raw(r)[:, :, NOPE:NOPE + half], pq(hi)[:, :, QK + half:P], pq(lo)[:, :, QK + half:P])]

        block = ctx.enter_context(nc.Block())

        @block.sync
        def _(sp):
            def slot_free(n, i=0, per=0):
                if n >= 2:
                    sp.wait_ge(wlo_ready, i * per + (n - 1))

            def load(n, src):
                slot_free(n)
                sp.dma_start(full(raw[n % 2]), src).then_inc(raw_full[n % 2], 16)

            def cols(w, c, width=256):
                return w[:, c:c + width].rearrange("(k p) n -> p k n", p=P)

            w_in = a["mla_w_in"][0]
            for i in range(2):
                sp.dma_start(x_tok[:, :, 512 * i:512 * i + 512],
                             a["x"][0, :, 512 * i:512 * i + 512].rearrange("(t p) n -> p t n", p=P)) \
                    .then_inc(x_in[i], 16)
            load(N_KV, cols(w_in, QRANK))
            sp.dma_start(kr_raw(raw[1]), cols(w_in, QRANK + KVRANK, ROPE)).then_inc(raw_full[1], 16)
            load(N_Q, cols(w_in, 0))
            load(N_Q + 1, cols(w_in, 256))

            def load_pair(p, n, head, kv, i, per):
                slot_free(n, i, per)
                s = n % 2
                sp.dma_start(pq_raw(raw[s]),
                             a["mla_w_uq"][0, :, ds(head * QK, QK)].rearrange("(k p) n -> p k n", p=P)) \
                    .then_inc(raw_full[s], 16)
                for k in range(2):
                    both = a["mla_w_ukv"][0, P * k:P * k + P, ds(p * 256, 256)].rearrange("p (e n) -> p e n", e=2)
                    sp.dma_start(pkv_raw(raw[s])[:, k, :].rearrange("p (e n) -> p e n", e=2),
                                 both[:, :, 64 * kv:64 * kv + 64]).then_inc(raw_full[s], 16)

            with sp.Fori(0, PAIRS) as p:
                load_pair(p, N_PAIR, p * 2, 0, p, 2)
                load_pair(p, N_PAIR + 1, p * 2 + 1, 1, p, 2)
            for j in range(4):
                load(N_WO + j, cols(a["mla_w_o"][0], 256 * j))

            def load_mlp(layer):
                n0 = N_MLP[layer]
                with sp.Fori(0, QUARTERS) as q:
                    for j in range(8):
                        n = n0 + j
                        slot_free(n, q, 8)
                        if j < 4:
                            src = a["mlp_w1"][layer, :, ds(q * D + 256 * j, 256)]
                        else:
                            src = a["mlp_w2"][layer, ds(q * D, D), 256 * (j - 4):256 * (j - 3)]
                        sp.dma_start(full(raw[n % 2]), src.rearrange("(k p) n -> p k n", p=P)) \
                            .then_inc(raw_full[n % 2], 16)

            load_mlp(0)
            w_in = a["mlstm_w_in"][0]
            slot_free(N_GATE)
            sp.dma_start(gate_raw(raw[N_GATE % 2]), cols(w_in, 3 * D, 2 * MH)).then_inc(raw_full[N_GATE % 2], 16)
            for j in range(4):
                load(N_QK + j, cols(w_in, 256 * j))
            sp.wait_ge(g_m, 1)
            sp.dma_start(m_dram, Mc[:, :]).then_inc(m_out, 16)
            for j in range(4):
                load(N_V + j, cols(w_in, D + 256 * j))
            for j in range(4):
                load(N_O + j, cols(w_in, 2 * D + 256 * j))
            for j in range(2):
                load(N_WO2 + j, cols(a["mlstm_w_o"][0], 256 * j))
            sp.wait_ge(m_out, 16)
            sp.wait_ge(gcol_ready, 2)
            for e in range(2):
                sp.dma_start(mb[:, e, :], m_dram[e:e + 1, :].broadcast_to([P, S])).then_inc(mb_in, 16)
            with sp.Fori(1, MPAIRS) as pr:
                sp.wait_ge(w_exp, pr * 8)
                for e in range(2):
                    sp.dma_start(mb[:, e, :], m_dram[ds(pr * 2 + e, 1), :].broadcast_to([P, S])) \
                        .then_inc(mb_in, 16)
            for j in range(2, 4):
                load(N_WO2 + j, cols(a["mlstm_w_o"][0], 256 * j))
            load_mlp(1)
            for t in range(TT):
                sp.wait_ge(out_ready, t + 1)
                sp.dma_start(out[0, P * t:P * t + P, :], o_tok[:, t, :]).then_inc(stored, 16)
            sp.wait_ge(stored, 16 * TT)

        @block.gpsimd
        def _(pool):
            own = Own(pool, pool_own)
            g = nc.gpsimd
            g.memset(ones[:], 1.0)
            g.memset(mhalf[:], -0.5)
            g.memset(mask_s[:], 0.0)
            g.memset(mask_w[:], 0.0)
            own.link(g.memset(ident[:], 0.0))
            g.affine_select(out=ident[:], in_=ident[:], compare_op=ALU.not_equal, fill=1.0, base=0,
                            pattern=[[-1, P]], channel_multiplier=1)
            g.affine_select(out=mask_s[:], in_=mask_s[:], compare_op=ALU.is_ge, fill=NEG, base=0,
                            pattern=[[-1, P]], channel_multiplier=1)
            own.link(g.affine_select(out=mask_w[:], in_=mask_w[:], compare_op=ALU.is_ge, fill=-NEG, base=0,
                                     pattern=[[1, P]], channel_multiplier=-1))
            g.tensor_copy(onesr[:], ones[:, 0:2])
            g.tensor_copy(identr[:], ident[:])
            g.tensor_copy(maskr[:], mask_s[:]).then_inc(consts, 1)

            def norm_adds(norm):
                first = sum(NORM_TILES[:norm])
                for m in range(1, NORM_TILES[norm]):
                    k = adds_before(norm) + m - 1
                    pool.wait_ge(sq_new, first + m + 1)
                    if m > 1:
                        pool.wait_ge(acc_add, k)
                    g.tensor_tensor(acc[:], acc[:], sq[:, k % 2, :], ALU.add).then_inc(acc_add, 1)

            def norm_pow(norm):
                pool.wait_ge(var_ready, norm + 1)
                g.tensor_tensor(rcol[:], var[:], mhalf[:, 0:4], ALU.pow).then_inc(rcol_ready, 1)

            norm_adds(NORM_MIX0)
            norm_pow(NORM_MIX0)
            norm_adds(NORM_KV)
            norm_pow(NORM_KV)
            norm_adds(NORM_CQ)
            norm_pow(NORM_CQ)

            def low_q(e, waits):
                pool.wait_ge(q_hi, waits)
                g.tensor_tensor(ql[e], qtmp[:], qh[e].bitcast(F32), ALU.subtract).then_inc(q_lo, 1)

            low_q(0, 1)
            with pool.Fori(0, PAIRS - 1) as p:
                low_q(1, p * 2 + 2)
                low_q(0, p * 2 + 3)
            low_q(1, HEADS)

            def low_hidden(layer, q, lead, per):
                for j in range(8):
                    pool.wait_ge(u_hi, q * per + (lead + j + 1))
                    g.tensor_tensor(ul[:, j, :], sq[:, j % 2, :], uh[:, j, :].bitcast(F32), ALU.subtract) \
                        .then_inc(u_ready, 1)

            def mlp(layer):
                norm_adds(NORM_MLP0 if layer == 0 else NORM_MLP1)
                norm_pow(NORM_MLP0 if layer == 0 else NORM_MLP1)
                with pool.Fori(0, QUARTERS) as q:
                    low_hidden(layer, q, 8 * QUARTERS * layer, 8)

            mlp(0)
            norm_adds(NORM_MIX1)
            norm_pow(NORM_MIX1)
            for m in range(8):
                pool.wait_ge(y_hi, m + 1)
                g.tensor_tensor(ul[:, m, :], ys[:, m % 2, :], uh[:, m, :].bitcast(F32), ALU.subtract) \
                    .then_inc(y_lo, 1)
            for m in range(8):
                pool.wait_ge(sig_new, m + 1)
                g.tensor_scalar(sg[:, m, :], sg[:, m, :], pcol[:, G_HEAD + m:G_HEAD + m + 1], None, ALU.mult) \
                    .then_inc(sg_ready, 1)
            pool.wait_ge(gcol_ready, 2)
            pool.wait_ge(m_out, 16)
            pool.wait_ge(sg_ready, MH)
            for e in range(2):
                o = 64 * (1 - e)
                g.memset(qph[o:o + 64, e, :].bitcast(F32), 0.0)
                own.link(g.memset(qpl[o:o + 64, e, :].bitcast(F32), 0.0))
            with pool.Fori(0, MPAIRS) as pr:
                own.enter(pr, 0, 2)
                g.tensor_copy(mkh, uh[:, ds(pr + 4, 1), :].rearrange("p a s -> p (a s)").bitcast(F32))
                own.link(g.tensor_copy(mkl, ul[:, ds(pr + 4, 1), :].rearrange("p a s -> p (a s)").bitcast(F32)))
                fixed(pool)
                for e in range(2):
                    o = 64 * e
                    g.tensor_copy(qph[o:o + 64, e, :],
                                  uh[o:o + 64, ds(pr, 1), :].rearrange("p a s -> p (a s)").bitcast(F32))
                    last = g.tensor_copy(qpl[o:o + 64, e, :],
                                         ul[o:o + 64, ds(pr, 1), :].rearrange("p a s -> p (a s)").bitcast(F32))
                    if e == 0:
                        own.link(last)
                        fixed(pool)
                last.then_inc(kq_ready, 1)
                pool.wait_ge(kq_ready, pr + 1)
                for e in range(2):
                    for j in range(TT):
                        z = 4 * e + j
                        pool.wait_ge(sw_hi, pr * 8 + z + 1)
                        g.tensor_tensor(swl(e, j), sw[:, z % 2, 0:LEN[j]], swh(e, j).bitcast(F32),
                                        ALU.subtract).then_inc(sw_lo, 1)
                pool.wait_ge(var2_ready, pr + 1)
                g.tensor_tensor(rc2[:], var2[:], mhalf[:], ALU.pow).then_inc(rc2_ready, 1)
                own.leave(0, MPAIRS)
            mlp(1)
            norm_adds(NORM_FIN)
            norm_pow(NORM_FIN)

        @block.scalar
        def _(act):
            own = Own(act, act_own)
            sc = nc.scalar
            for at, src in ((G_MIX, a["norm_mix_g"].rearrange("l (m p) -> (l m) p", p=P)),
                            (G_MLP, a["norm_mlp_g"].rearrange("l (m p) -> (l m) p", p=P)),
                            (G_FIN, a["final_g"].rearrange("(m p) -> m p", p=P)),
                            (G_Q, a["mla_q_norm_g"].rearrange("l (m p) -> (l m) p", p=P)),
                            (G_KV, a["mla_kv_norm_g"].rearrange("l (m p) -> (l m) p", p=P)),
                            (CONV_W, a["mlstm_conv_w"].rearrange("l c (m p) -> (l c m) p", p=P)),
                            (CONV_B, a["mlstm_conv_b"].rearrange("l (m p) -> (l m) p", p=P)),
                            (G_HEAD, a["mlstm_head_norm_g"].rearrange("l (m p) -> (l m) p", p=P))):
                act.dma_start(prow[at:at + src.shape[0], :], src).then_inc(par_in, 16)
            act.dma_start(rope_c[:], a["rope_const"]).then_inc(pos_in, 16)
            act.dma_start(pos_i[:], a["positions"].broadcast_to([P, S])).then_inc(pos_in, 16)
            act.dma_start(gate_b[:, 0:1], a["mlstm_i_b"].rearrange("l h -> h l")).then_inc(pos_in, 16)
            act.dma_start(gate_b[:, 1:2], a["mlstm_f_b"].rearrange("l h -> h l")).then_inc(pos_in, 16)

            def split(n, kind="full", i=0, over=0, arrived=0):
                act.wait_ge(raw_full[n % 2], i * arrived + raw_count(n))
                if n >= 2:
                    which, value = strip_over(n - 2, gemm_done, q_mm)
                    act.wait_ge(which, i * over + value)
                parts = split_parts(kind, n % 2)
                for src, hi, _ in parts:
                    last = sc.copy(hi, src)
                last.then_inc(whi_ready, 1)

            def square(norm, m, src):
                if m == 0:
                    if norm:
                        act.wait_ge(stat_col, norm)
                    sc.activation(acc[:], src, ACT.Square).then_inc(sq_new, 1)
                else:
                    k = adds_before(norm) + m - 1
                    if k >= 2:
                        act.wait_ge(acc_add, k - 1)
                    sc.activation(sq[:, k % 2, :], src, ACT.Square).then_inc(sq_new, 1)

            def update(t0, norm, gain, m):
                act.wait_ge(gemm_evac, t0 + m + 1)
                square(norm, m, h[:, m, :])
                sc.activation(xh[:, m, :], h[:, m, :], ACT.Copy, scale=pcol[:, gain + m:gain + m + 1]) \
                    .then_inc(xh_new, 1)

            act.wait_ge(ang_ready, 1)
            sc.activation(sin[:], ang[:], ACT.Sin, scale=rope_c[:, 1:2]).then_inc(trig_ready, 1)
            sc.activation(cos[:], turn[:], ACT.Sin).then_inc(trig_ready, 1)

            act.wait_ge(par_ready, 1)
            for m in range(KD):
                if m == 4:
                    split(N_KV)
                update(0, NORM_MIX0, G_MIX, m)
            split(N_KR, "kr")
            split(N_Q)
            for m in range(2):
                act.wait_ge(gemm_evac, T_IN + m + 1)
                square(NORM_KV, m, ckv[:, m, :])
            split(N_Q + 1)

            def c_high(n_before, src, hi, gain, tiles):
                for m in range(tiles):
                    act.wait_ge(c_norm, n_before + m + 1)
                    sc.activation(hi[:, m, :], src[:, m, :], ACT.Copy, scale=pcol[:, gain + m:gain + m + 1]) \
                        .then_inc(c_hi, 1)

            c_high(0, ckv, ckvh, G_KV, 2)
            split(N_PAIR, "pair")
            for m in range(4):
                act.wait_ge(gemm_evac, T_IN + 4 + m + 1)
                square(NORM_CQ, m, cq[:, m, :])
            split(N_PAIR + 1, "pair")
            act.wait_ge(kr_new, 1)
            for e in range(2):
                sc.copy(kh[e][64:128, :], krot[64:128, :]).then_inc(kr_hi, 1)

            def k_high(i, lead):
                act.wait_ge(k_mm, i + (lead + 1))
                for e in range(2):
                    last = sc.copy(kh[e][0:64, :], ps[64 * e:64 * e + 64, B_KV, :])
                last.then_inc(k_hi, 1)

            def q_high(e, i, lead):
                act.wait_ge(q_tab, i * 2 + (lead + 1))
                sc.copy(qh[e], qtmp[:]).then_inc(q_hi, 1)

            def exp(i, lead, b):
                w = P * (b + 1)
                s = 4 * lead + b
                act.wait_ge(s_max, i * 8 + (s + 1))
                if s >= 2:
                    act.wait_ge(t_mm, i * 8 + (s - 1))
                sc.activation(prob[:, b % 2, 0:w], ps[:, B_S + b % 2, 0:w], ACT.Exp, bias=nmax[:, b:b + 1],
                              accum_out=rsum[:, b:b + 1]).then_inc(s_exp, 1)

            def pt_high(i, lead, b):
                s = 4 * lead + b
                act.wait_ge(t_mm, i * 8 + (s + 1))
                sc.copy(pth[:, 0:b + 1, P * b:P * b + P],
                        ps[:, B_PT + b % 2, 0:P * (b + 1)].rearrange("p (j q) -> p j q", q=P)).then_inc(t_hi, 1)

            def o_high(i, e):
                act.wait_ge(pv_mm, i * 2 + (e + 1))
                fixed(act)
                sc.copy(uh[64 * e:64 * e + 64, ds(i, 1), :].rearrange("p a s -> p (a s)"),
                        ps[64 * e:64 * e + 64, B_PV + e, :]).then_inc(o_hi, 1)

            k_high(0, 0)
            c_high(2, cq, cqh, G_Q, 4)
            q_high(0, 0, 0)
            exp(0, 0, 0)
            exp(0, 0, 1)

            def attention(i, last=False):
                act.wait_ge(v_mm, i + 1)
                sc.copy(vh[:, :, :], ps[:, B_KV, :].rearrange("p (t n) -> p t n", t=TT)).then_inc(v_hi, 1)
                if not last:
                    split(N_PAIR + 2, "pair", i, 2, 48)
                pt_high(i, 0, 0)
                exp(i, 0, 2)
                pt_high(i, 0, 1)
                exp(i, 0, 3)
                q_high(1, i, 1)
                pt_high(i, 0, 2)
                pt_high(i, 0, 3)
                if not last:
                    split(N_PAIR + 3, "pair", i, 2, 48)
                exp(i, 1, 0)
                exp(i, 1, 1)
                o_high(i, 0)
                pt_high(i, 1, 0)
                exp(i, 1, 2)
                pt_high(i, 1, 1)
                exp(i, 1, 3)
                if not last:
                    k_high(i, 1)
                    q_high(0, i, 2)
                pt_high(i, 1, 2)
                pt_high(i, 1, 3)
                if not last:
                    exp(i, 2, 0)
                    exp(i, 2, 1)
                o_high(i, 1)

            with act.Fori(0, PAIRS - 1) as i:
                attention(i)
            attention(PAIRS - 1, last=True)

            def residual_stage(n0, t0, norm, gain):
                for j in range(4):
                    split(n0 + j + 1)
                    for m in (2 * j, 2 * j + 1):
                        update(t0, norm, gain, m)

            split(N_WO)
            residual_stage(N_WO, T_WO, NORM_MLP0, G_MLP)

            def final_tile(m):
                act.wait_ge(gemm_evac, T_MLP[1] + 16 * QUARTERS - 8 + m + 1)
                square(NORM_FIN, m, h[:, m, :])
                if m >= 2:
                    act.wait_ge(out_t, m - 1)
                sc.activation(hg[:, m % 2, :], h[:, m, :], ACT.Copy, scale=pcol[:, G_FIN + m:G_FIN + m + 1]) \
                    .then_inc(hg_new, 1)

            def final_evac(m):
                act.wait_ge(out_t, m + 1)
                sc.copy(o_tok[:, :, P * m:P * m + P],
                        ps[:, B_OUT + m % 2, :].rearrange("p (t n) -> p t n", t=TT)).then_inc(out_evac, 1)

            def mlp_quarter(layer, i, q, last=False):
                n0 = N_MLP[layer] + 8 * q
                for j in range(4):
                    split(n0 + j + 1, "full", i, 16, 64)
                    for m in (2 * j, 2 * j + 1):
                        act.wait_ge(a_new, i * 8 + (8 * QUARTERS * layer + 8 * q + m + 1))
                        sc.copy(uh[:, m, :], sq[:, m % 2, :]).then_inc(u_hi, 1)
                for j in range(4):
                    if not last:
                        split(n0 + j + 5, "full", i, 16, 64)
                    elif j < 3:
                        split(n0 + j + 5)
                    elif layer == 0:
                        split(n0 + 8, "gate")
                    if last:
                        for m in (2 * j, 2 * j + 1):
                            if layer == 0:
                                update(T_MLP[0] + 16 * QUARTERS - 8, NORM_MIX1, G_MIX + 8, m)
                            else:
                                final_tile(m)
                                if m:
                                    final_evac(m - 1)

            def mlp(layer):
                with act.Fori(0, QUARTERS - 1) as i:
                    mlp_quarter(layer, i, 0)
                mlp_quarter(layer, 0, QUARTERS - 1, last=True)

            mlp(0)

            split(N_QK)
            act.wait_ge(gemm_evac, T_GATE + 1)
            sc.activation(gi[:], gi[:], ACT.Tanh, bias=gate_b[:, 2:3], scale=1.0 / CAP)
            own.link(sc.activation(gf[:], gf[:], ACT.Tanh, bias=gate_b[:, 3:4], scale=1.0 / CAP))
            own.link(sc.activation(gf[:], gf[:], ACT.Exp, scale=-CAP))
            sc.activation(gf[:], gf[:], ACT.Ln, bias=1.0).then_inc(g_ln, 1)
            for j in range(4):
                split(N_QK + j + 1)
                for m in (2 * j, 2 * j + 1):
                    act.wait_ge(y_new, m + 1)
                    if m >= 2:
                        act.wait_ge(y_lo, m - 1)
                    own.link(sc.activation(ys[:, m % 2, :], yc[:, m % 2, :], ACT.Silu))
                    sc.copy(uh[:, m, :], ys[:, m % 2, :]).then_inc(y_hi, 1)
                if j == 0:
                    act.wait_ge(g_m, 1)
                    sc.activation(en[:], en[:], ACT.Exp, scale=-1.0).then_inc(g_en, 1)
            for j in range(4):
                split(N_V + j + 1)
            for j in range(4):
                split(N_O + j + 1)
                for m in (2 * j, 2 * j + 1):
                    act.wait_ge(gemm_evac, T_O + m + 1)
                    sc.activation(sg[:, m, :], otmp[:, m % 2, :], ACT.Sigmoid).then_inc(sig_new, 1)
            with act.Fori(0, MPAIRS) as pr:
                sc.copy(mvh, v_tok[:, :, ds(pr * 256, 256)]).then_inc(mv_hi, 1)
                act.wait_ge(mb_in, pr * 32 + 32)
                act.wait_ge(md_ready, pr + 1)

                def weights(e, j):
                    z = 4 * e + j
                    if z >= 2:
                        act.wait_ge(sw_mul, pr * 8 + z - 1)
                    fixed(act)
                    bias = gcol[:, ds(pr * 2 + (MH * j + e), 1)]
                    last = sc.activation(wt[:, z % 2, 0:P], md[:, (e * TT + j) * P:(e * TT + j + 1) * P],
                                         ACT.Exp, bias=bias, scale=-1.0)
                    if j < TT - 1:
                        last = sc.activation(wt[:, z % 2, P:LEN[j]], mb[:, e, P * (j + 1):S], ACT.Exp,
                                             bias=bias, scale=-1.0)
                    last.then_inc(w_exp, 1)

                def high(e, j):
                    z = 4 * e + j
                    act.wait_ge(sw_mul, pr * 8 + z + 1)
                    sc.copy(swh(e, j), sw[:, z % 2, 0:LEN[j]]).then_inc(sw_hi, 1)

                order = [(e, j) for e in range(2) for j in range(TT)]
                for z in range(9):
                    if z < 8:
                        weights(*order[z])
                    if z:
                        high(*order[z - 1])
                for e in range(2):
                    act.wait_ge(num_mm, pr * 2 + e + 1)
                    sc.activation(numsq[:, e, :], ps[:, B_NUM + e, :], ACT.Square).then_inc(num_sq, 1)
                for e in range(2):
                    act.wait_ge(bc2_mm, pr * 2 + e + 1)
                    sc.copy(rb[:, e, :], bank(e)).then_inc(rb_ready, 1)
                for e in range(2):
                    act.wait_ge(hs_ready, pr * 2 + e + 1)
                    fixed(act)
                    sc.copy(uh[:, ds(pr + 4 * e, 1), :].rearrange("p a s -> p (a s)"), rb[:, e, :]) \
                        .then_inc(g_hi, 1)
            residual_stage(N_WO2, T_WO2, NORM_MLP1, G_MLP + 8)
            mlp(1)
            final_evac(KD - 1)

        @block.vector
        def _(dve):
            own = Own(dve, dve_own)
            v = nc.vector

            def split(n, kind="full", i=0, per=0):
                dve.wait_ge(whi_ready, i * per + (n + 1))
                for src, hi, lo in split_parts(kind, n % 2):
                    last = v.tensor_tensor(lo, src, hi.bitcast(F32), ALU.subtract)
                last.then_inc(wlo_ready, 1)

            def low(t_lo_, src, hi, gain=None):
                if gain is None:
                    return v.tensor_tensor(t_lo_, src, hi.bitcast(F32), ALU.subtract)
                return v.scalar_tensor_tensor(out=t_lo_, in0=src, scalar=gain, in1=hi.bitcast(F32),
                                              op0=ALU.mult, op1=ALU.subtract)

            def x_low(group, gain, m):
                dve.wait_ge(xh_new, 8 * group + m + 1)
                low(xl[:, m, :], h[:, m, :], xh[:, m, :], pcol[:, gain + m:gain + m + 1]).then_inc(x_ready, 1)

            def stat_diag(norm, width):
                dve.wait_ge(stat_col, norm + 1)
                v.tensor_scalar(var[:], ps[:, B_COL, 0:4], 1.0 / width, EPS, ALU.mult, ALU.add) \
                    .then_inc(var_ready, 1)
                dve.wait_ge(rcol_ready, norm + 1)
                for t in range(TT):
                    last = v.tensor_scalar(diag[:, 0, P * t:P * t + P], ident[:], rcol[:, t:t + 1], None,
                                           ALU.mult)
                last.then_inc(diag_ready, 1)

            def stat_row(norm, r):
                dve.wait_ge(stat_bc, norm + 1)
                v.tensor_copy(r[:], bank(B_BC)).then_inc(rbc_ready, 1)
                dve.wait_ge(rbc_ready, norm + 1)

            dve.wait_ge(pos_in, 64)
            own.link(v.tensor_copy(ang[:], pos_i[:]))
            own.link(v.tensor_scalar(ang[:], ang[:], rope_c[:, 0:1], None, ALU.mult))
            own.link(v.tensor_scalar(turn[:], ang[:], 1.0 / (2 * np.pi), MAGIC, ALU.mult, ALU.add))
            own.link(v.tensor_scalar(turn[:], turn[:], MAGIC, None, ALU.subtract))
            for part in (TWO_PI_1, TWO_PI_2, TWO_PI_3):
                own.link(v.scalar_tensor_tensor(out=ang[:], in0=turn[:], scalar=-part, in1=ang[:],
                                                op0=ALU.mult, op1=ALU.add))
            own.link(v.tensor_scalar(ang[:], ang[:], PI_IN, -PI_IN, ALU.min, ALU.max))
            own.link(v.tensor_scalar(turn[:], ang[:], np.pi / 2, -2 * np.pi, ALU.is_gt, ALU.mult))
            own.link(v.scalar_tensor_tensor(out=turn[:], in0=ang[:], scalar=np.pi / 2, in1=turn[:],
                                            op0=ALU.add, op1=ALU.add))
            own.link(v.tensor_scalar(turn[:], turn[:], PI_IN, -PI_IN, ALU.min, ALU.max))
            v.tensor_scalar(gate_b[:, 2:4], gate_b[:, 0:2], 1.0 / CAP, None, ALU.mult).then_inc(ang_ready, 1)
            v.memset(tab[0:64, :], SCALE)
            dve.wait_ge(par_t, 1)
            v.tensor_copy(pcol[:], ps[:, B_COL, 0:PCOLS]).then_inc(par_ready, 1)
            dve.wait_ge(par_ready, 1)
            dve.wait_ge(trig_ready, 2)
            v.tensor_scalar(tab[64:96, :], cos[64:96, :], SCALE, None, ALU.mult)
            own.link(v.tensor_scalar(tab[96:128, :], sin[96:128, :], SCALE, None, ALU.mult))

            for m in range(KD):
                if m == 5:
                    split(N_KV)
                dve.wait_ge(gemm_done, m + 1)
                v.tensor_copy(h[:, m, :], bank(m % RING)).then_inc(gemm_evac, 1)
                if m:
                    x_low(0, G_MIX, m - 1)
            x_low(0, G_MIX, KD - 1)
            split(N_KR, "kr")
            stat_diag(NORM_MIX0, D)
            stat_row(NORM_MIX0, r_a)

            def scaled(t, dst, r):
                dve.wait_ge(gemm_done, t + 1)
                return v.tensor_tensor(dst, bank(t % RING), r[:], ALU.mult)

            for m in range(2):
                scaled(T_IN + m, ckv[:, m, :], r_a).then_inc(gemm_evac, 1)
            split(N_Q)
            dve.wait_ge(gemm_done, T_IN + 3)
            v.tensor_tensor(krot[:], bank((T_IN + 2) % RING), cos[:], ALU.mult).then_inc(gemm_evac, 1)
            dve.wait_ge(gemm_done, T_IN + 4)
            v.tensor_tensor(krot2[:], bank((T_IN + 3) % RING), sin[:], ALU.mult).then_inc(gemm_evac, 1)
            dve.wait_ge(gemm_evac, T_IN + 4)
            own.link(v.tensor_tensor(krot[:], krot[:], krot2[:], ALU.add))
            v.tensor_tensor(krot[:], krot[:], r_a[:], ALU.mult).then_inc(kr_new, 1)
            split(N_Q + 1)
            stat_diag(NORM_KV, KVRANK)
            scaled(T_IN + 4, cq[:, 0, :], r_a).then_inc(gemm_evac, 1)
            stat_row(NORM_KV, r_b)

            def normed(before, c, hi, lo, gain, tiles):
                for m in range(tiles):
                    v.tensor_tensor(c[:, m, :], c[:, m, :], r_b[:], ALU.mult).then_inc(c_norm, 1)
                for m in range(tiles):
                    dve.wait_ge(c_hi, before + m + 1)
                    low(lo[:, m, :], c[:, m, :], hi[:, m, :], pcol[:, gain + m:gain + m + 1]).then_inc(c_ready, 1)

            dve.wait_ge(gemm_evac, T_IN + 2)
            normed(0, ckv, ckvh, ckvl, G_KV, 2)
            scaled(T_IN + 5, cq[:, 1, :], r_a).then_inc(gemm_evac, 1)
            split(N_PAIR, "pair")
            scaled(T_IN + 6, cq[:, 2, :], r_a).then_inc(gemm_evac, 1)
            scaled(T_IN + 7, cq[:, 3, :], r_a).then_inc(gemm_evac, 1)
            stat_diag(NORM_CQ, QRANK)
            split(N_PAIR + 1, "pair")
            for e in range(2):
                dve.wait_ge(kr_hi, e + 1)
                low(kl[e][64:128, :], krot[64:128, :], kh[e][64:128, :]).then_inc(kr_lo, 1)

            def k_low(i, lead):
                dve.wait_ge(k_hi, i + (lead + 1))
                for e in range(2):
                    last = low(kl[e][0:64, :], ps[64 * e:64 * e + 64, B_KV, :], kh[e][0:64, :])
                last.then_inc(k_lo, 1)

            def q_table(i, lead):
                dve.wait_ge(q_mm, i * 2 + (lead + 1))
                if lead:
                    dve.wait_ge(q_lo, i * 2 + lead)
                v.tensor_tensor(qtmp[:], bank(B_Q), tab[:], ALU.mult).then_inc(q_tab, 1)

            def row_max(i, lead, b):
                dve.wait_ge(s_mm, i * 8 + (4 * lead + b + 1))
                v.tensor_reduce(nmax[:, b:b + 1], ps[:, B_S + b % 2, 0:P * (b + 1)], op=ALU.max, axis=AX.X,
                                negate=True).then_inc(s_max, 1)

            def normalise(i, lead, b):
                dve.wait_ge(s_exp, i * 8 + (4 * lead + b + 1))
                own.link(v.reciprocal(rinv[:, b:b + 1], rsum[:, b:b + 1]))
                w = P * (b + 1)
                v.tensor_scalar(prob[:, b % 2, 0:w], prob[:, b % 2, 0:w], rinv[:, b:b + 1], None, ALU.mult) \
                    .then_inc(p_norm, 1)

            def pt_low(i, lead, b):
                dve.wait_ge(t_hi, i * 8 + (4 * lead + b + 1))
                part = slice(P * b, P * b + P)
                low(ptl[:, 0:b + 1, part], ps[:, B_PT + b % 2, 0:P * (b + 1)].rearrange("p (j q) -> p j q", q=P),
                    pth[:, 0:b + 1, part]).then_inc(t_lo, 1)

            def o_low(i, e):
                dve.wait_ge(o_hi, i * 2 + (e + 1))
                rows = slice(64 * e, 64 * e + 64)
                low(ul[rows, ds(i, 1), :].rearrange("p a s -> p (a s)"), ps[rows, B_PV + e, :],
                    uh[rows, ds(i, 1), :].rearrange("p a s -> p (a s)")).then_inc(o_lo, 1)

            k_low(0, 0)
            stat_row(NORM_CQ, r_b)
            normed(2, cq, cqh, cql, G_Q, 4)
            q_table(0, 0)
            row_max(0, 0, 0)
            row_max(0, 0, 1)
            normalise(0, 0, 0)
            normalise(0, 0, 1)

            def attention(i, last=False):
                dve.wait_ge(v_hi, i + 1)
                low(vl[:, :, :], ps[:, B_KV, :].rearrange("p (t n) -> p t n", t=TT), vh[:, :, :]) \
                    .then_inc(v_lo, 1)
                if not last:
                    split(N_PAIR + 2, "pair", i, 2)
                pt_low(i, 0, 0)
                row_max(i, 0, 2)
                pt_low(i, 0, 1)
                normalise(i, 0, 2)
                row_max(i, 0, 3)
                q_table(i, 1)
                normalise(i, 0, 3)
                pt_low(i, 0, 2)
                pt_low(i, 0, 3)
                if not last:
                    split(N_PAIR + 3, "pair", i, 2)
                row_max(i, 1, 0)
                row_max(i, 1, 1)
                normalise(i, 1, 0)
                normalise(i, 1, 1)
                o_low(i, 0)
                pt_low(i, 1, 0)
                row_max(i, 1, 2)
                pt_low(i, 1, 1)
                normalise(i, 1, 2)
                row_max(i, 1, 3)
                if not last:
                    k_low(i, 1)
                    q_table(i, 2)
                normalise(i, 1, 3)
                pt_low(i, 1, 2)
                pt_low(i, 1, 3)
                if not last:
                    row_max(i, 2, 0)
                    row_max(i, 2, 1)
                    normalise(i, 2, 0)
                    normalise(i, 2, 1)
                o_low(i, 1)

            with dve.Fori(0, PAIRS - 1) as i:
                own.enter(i, 0, 8)
                attention(i)
                own.leave(0, PAIRS - 1)
            attention(PAIRS - 1, last=True)

            def onto_residual(t, m, i=0, per=0):
                dve.wait_ge(gemm_done, i * per + (t + 1))
                return v.tensor_tensor(h[:, m, :], bank(t % RING), h[:, m, :], ALU.add)

            def residual_stage(n0, t0, group, gain):
                for j in range(4):
                    split(n0 + j + 1)
                    for m in (2 * j, 2 * j + 1):
                        onto_residual(t0 + m, m).then_inc(gemm_evac, 1)
                        if m:
                            x_low(group, gain, m - 1)
                x_low(group, gain, KD - 1)

            split(N_WO)
            residual_stage(N_WO, T_WO, 1, G_MLP)

            def mlp_quarter(layer, i, q, first=False, last=False):
                n0, t0 = N_MLP[layer] + 8 * q, T_MLP[layer] + 16 * q
                u0 = 8 * QUARTERS * layer + 8 * q
                for j in range(4):
                    split(n0 + j + 1, "full", i, 8)
                    if first and j == 0:
                        norm = NORM_MLP0 if layer == 0 else NORM_MLP1
                        stat_diag(norm, D)
                        stat_row(norm, r_a)
                    for m in (2 * j, 2 * j + 1):
                        dve.wait_ge(gemm_done, i * 16 + (t0 + m + 1))
                        v.tensor_tensor(diag[:, m % 2, :], bank((t0 + m) % RING), r_a[:], ALU.mult) \
                            .then_inc(gemm_evac, 1)
                        dve.wait_ge(gemm_evac, i * 16 + (t0 + m + 1))
                        if u0 or m > 1 or not first:
                            dve.wait_ge(u_ready, i * 8 + (u0 + max(m - 1, 0)))
                        v.scalar_tensor_tensor(out=sq[:, m % 2, :], in0=diag[:, m % 2, :], scalar=0.0,
                                               in1=diag[:, m % 2, :], op0=ALU.max, op1=ALU.mult) \
                            .then_inc(a_new, 1)
                for j in range(4):
                    if not last:
                        split(n0 + j + 5, "full", i, 8)
                    elif j < 3:
                        split(n0 + j + 5)
                    elif layer == 0:
                        split(n0 + 8, "gate")
                    for m in (2 * j, 2 * j + 1):
                        onto_residual(t0 + 8 + m, m, i, 16).then_inc(gemm_evac, 1)
                        if last and layer == 0 and m:
                            x_low(2, G_MIX + 8, m - 1)
                if last and layer == 0:
                    x_low(2, G_MIX + 8, KD - 1)

            def mlp(layer):
                mlp_quarter(layer, 0, 0, first=True)
                with dve.Fori(1, QUARTERS - 1) as i:
                    mlp_quarter(layer, i, 0)
                mlp_quarter(layer, 0, QUARTERS - 1, last=True)

            mlp(0)

            split(N_QK)
            stat_diag(NORM_MIX1, D)
            stat_row(NORM_MIX1, r_a)
            v.memset(zrow[:], 0.0)
            v.memset(cpad[:, 0:CONV - 1], 0.0)
            dve.wait_ge(gemm_done, T_GATE + 1)
            b = bank(T_GATE % RING)
            own.link(v.tensor_tensor(gi[:], b[0:MH, :], r_a[0:MH, :], ALU.mult))
            v.tensor_tensor(gf[:], b[32:32 + MH, :], r_a[32:32 + MH, :], ALU.mult).then_inc(gemm_evac, 1)

            def gates():
                dve.wait_ge(g_ln, 1)
                own.link(v.tensor_tensor_scan(Fc[:], gf[:], zrow[:], 0.0, ALU.add, ALU.add))
                own.link(v.scalar_tensor_tensor(out=Gc[:], in0=gi[:], scalar=CAP, in1=Fc[:], op0=ALU.mult,
                                                op1=ALU.add))
                own.link(v.tensor_tensor_scan(Mc[:], Gc[:], Gc[:], 0.0, ALU.max, ALU.max))
                v.tensor_tensor(en[:], Mc[:], Fc[:], ALU.subtract).then_inc(g_m, 1)

            def gate_columns():
                dve.wait_ge(g_t, 1)
                v.tensor_copy(gcol[:], ps[:, 5, 0:32]).then_inc(gcol_ready, 1)
                v.tensor_copy(encol[:, :].rearrange("p (e j) -> p e j", e=MH),
                              ps[:, 5, 32:64].rearrange("p (j e) -> p e j", e=MH)).then_inc(gcol_ready, 1)

            def conv(m):
                if m:
                    dve.wait_ge(y_new, m)
                scaled(T_QK + m, cpad[:, CONV - 1:CONV - 1 + S], r_a).then_inc(gemm_evac, 1)
                if m >= 2:
                    dve.wait_ge(y_hi, m - 1)
                dve.wait_ge(gemm_evac, T_QK + m + 1)
                w = [pcol[:, CONV_W + 8 * c + m:CONV_W + 8 * c + m + 1] for c in range(CONV)]
                y = yc[:, m % 2, :]
                own.link(v.tensor_scalar(y, cpad[:, 0:S], w[0], pcol[:, CONV_B + m:CONV_B + m + 1],
                                         ALU.mult, ALU.add))
                for c in range(1, CONV):
                    ins = v.scalar_tensor_tensor(out=y, in0=cpad[:, c:c + S], scalar=w[c], in1=y,
                                                 op0=ALU.mult, op1=ALU.add)
                    if c < CONV - 1:
                        own.link(ins)
                ins.then_inc(y_new, 1)

            for j in range(4):
                split(N_QK + j + 1)
                conv(2 * j)
                if j == 0:
                    gates()
                if j == 2:
                    gate_columns()
                conv(2 * j + 1)
            for j in range(4):
                split(N_V + j + 1)
                for i in range(2):
                    t = T_V + 2 * j + i
                    dve.wait_ge(gemm_done, t + 1)
                    for half in range(2):
                        tt = 2 * i + half
                        last = v.tensor_scalar(v_tok[:, tt, 256 * j:256 * j + 256],
                                               ps[:, t % RING, 256 * half:256 * half + 256],
                                               rcol[:, tt:tt + 1], None, ALU.mult)
                    last.then_inc(gemm_evac, 1)
            for j in range(4):
                split(N_O + j + 1)
                for m in (2 * j, 2 * j + 1):
                    if m < 2:
                        dve.wait_ge(y_hi, 8)
                    else:
                        dve.wait_ge(sig_new, m - 1)
                    scaled(T_O + m, otmp[:, m % 2, :], r_a).then_inc(gemm_evac, 1)

            dve.wait_ge(sg_ready, MH)
            with dve.Fori(0, MPAIRS) as pr:
                own.enter(pr, 0, 4)
                dve.wait_ge(mv_hi, pr + 1)
                low(mvl, v_tok[:, :, ds(pr * 256, 256)], mvh).then_inc(mv_lo, 1)
                dve.wait_ge(mb_in, pr * 32 + 32)
                v.tensor_tensor(md[:, :].rearrange("p (b q) -> p b q", q=P),
                                mb[:, :, :].rearrange("p e (j q) -> p (e j) q", q=P),
                                mask_w[:].unsqueeze(1).broadcast_to([P, 2 * TT, P]), ALU.add) \
                    .then_inc(md_ready, 1)
                for z in range(8):
                    n = LEN[z % 4]
                    dve.wait_ge(st_mm, pr * 8 + z + 1)
                    dve.wait_ge(w_exp, pr * 8 + z + 1)
                    if z >= 2:
                        dve.wait_ge(sw_lo, pr * 8 + z - 1)
                    v.scalar_tensor_tensor(out=sw[:, z % 2, 0:n], in0=ps[:, B_ST + z % 2, 0:n],
                                           scalar=float(64 ** -0.5), in1=wt[:, z % 2, 0:n],
                                           op0=ALU.mult, op1=ALU.mult).then_inc(sw_mul, 1)
                dve.wait_ge(num_mm, pr * 2 + 2)
                own.link(v.tensor_copy(dcp[:], ps[:, B_DEN, 0:16].rearrange("p (a n) -> p a n", n=2)[:, :, 0]))
                own.link(v.scalar_tensor_tensor(out=dd[:], in0=dcp[:], scalar=-1.0, in1=dcp[:],
                                                op0=ALU.mult, op1=ALU.max))
                own.link(v.tensor_tensor(dd[:], dd[:], encol[:, ds(pr * 8, 8)], ALU.max))
                own.link(v.scalar_tensor_tensor(out=dd[:], in0=dd[:], scalar=EPS, in1=dd[:],
                                                op0=ALU.mult, op1=ALU.mult))
                dve.wait_ge(ms_mm, pr * 2 + 2)
                v.scalar_tensor_tensor(out=var2[:], in0=ps[:, B_MS, 0:8], scalar=1.0 / P, in1=dd[:],
                                       op0=ALU.mult, op1=ALU.add).then_inc(var2_ready, 1)
                dve.wait_ge(rc2_ready, pr + 1)
                for e in range(2):
                    v.tensor_tensor(diag[:, e, :].rearrange("p (t q) -> p t q", q=P),
                                    ident[:].unsqueeze(1).broadcast_to([P, TT, P]),
                                    rc2[:, 4 * e:4 * e + 4].unsqueeze(2).broadcast_to([P, TT, P]),
                                    ALU.mult).then_inc(diag2_ready, 1)
                for e in range(2):
                    dve.wait_ge(rb_ready, pr * 2 + e + 1)
                    v.tensor_tensor(rb[:, e, :], ps[:, B_NUM + e, :], rb[:, e, :], ALU.mult) \
                        .then_inc(hn_ready, 1)
                for e in range(2):
                    dve.wait_ge(hn_ready, pr * 2 + e + 1)
                    v.tensor_tensor(rb[:, e, :], rb[:, e, :],
                                    sg[:, ds(pr * 2 + e, 1), :].rearrange("p a s -> p (a s)"), ALU.mult) \
                        .then_inc(hs_ready, 1)
                for e in range(2):
                    dve.wait_ge(g_hi, pr * 2 + e + 1)
                    low(ul[:, ds(pr + 4 * e, 1), :].rearrange("p a s -> p (a s)"), rb[:, e, :],
                        uh[:, ds(pr + 4 * e, 1), :].rearrange("p a s -> p (a s)")).then_inc(g_ready, 1)
                own.leave(0, MPAIRS)
            residual_stage(N_WO2, T_WO2, 3, G_MLP + 8)
            mlp(1)
            dve.wait_ge(stat_col, NORM_FIN + 1)
            v.tensor_scalar(var[:], ps[:, B_COL, 0:4], 1.0 / D, EPS, ALU.mult, ALU.add).then_inc(var_ready, 1)
            dve.wait_ge(rcol_ready, NORM_FIN + 1)
            dve.wait_ge(out_evac, KD)
            for t in range(TT):
                v.tensor_scalar(o_tok[:, t, :], o_tok[:, t, :], rcol[:, t:t + 1], None, ALU.mult) \
                    .then_inc(out_ready, 1)

        @block.tensor
        def _(pe):
            mm, tr = nc.tensor.matmul, nc.tensor.transpose

            def product(o, pairs, wait=None):
                for k, ((ah, al), (bh, bl)) in enumerate(pairs):
                    if wait is not None:
                        wait(k)
                    first, last = k == 0, k == len(pairs) - 1
                    mm(o, ah, bl, start=first, stop=False)
                    mm(o, ah, bh, start=False, stop=False)
                    ins = mm(o, al, bh, start=False, stop=last)
                return ins

            def free_bank(t, i=0, per=0):
                if t >= RING:
                    pe.wait_ge(gemm_evac, i * per + (t - RING + 1))

            def strip_ready(n, i=0, per=0):
                pe.wait_ge(wlo_ready, i * per + (n + 1))

            def tile(t, n, c, rh, rl, wait=None, i=0, per=0, kinds=full, width=P, order=None):
                free_bank(t, i, per)
                s = n % 2
                ks = range(8)
                o = ps[0:width, t % RING, :]
                order = order or (lambda k: k)
                return product(o, [((full(whi[s])[:, k, c:c + width], full(wlo[s])[:, k, c:c + width]),
                                    (rh[:, order(k), :], rl[:, order(k), :])) for k in ks], wait) \
                    .then_inc(gemm_done, 1)

            def stat_sum(norm):
                pe.wait_ge(acc_add, adds_before(norm + 1))
                for t in range(TT):
                    last = mm(ps[:, B_COL, t:t + 1], acc[:, P * t:P * t + P], ones[:, 0:1], start=True, stop=True)
                last.then_inc(stat_col, 1)

            def stat_spread(norm):
                pe.wait_ge(diag_ready, norm + 1)
                if norm:
                    pe.wait_ge(rbc_ready, norm)
                mm(bank(B_BC), ones[:], diag[:, 0, :], start=True, stop=True).then_inc(stat_bc, 1)

            pe.wait_ge(consts, 1)
            pe.wait_ge(par_in, 128)
            tr(ps[:, B_COL, 0:PCOLS], prow[:, :], ident[0:PCOLS, 0:PCOLS]).then_inc(par_t, 1)
            for m in range(KD):
                pe.wait_ge(x_in[m // 4], 16)
                free_bank(m)
                for t in range(TT):
                    last = tr(ps[:, m % RING, P * t:P * t + P], x_tok[:, t, P * m:P * m + P], ident[:])
                last.then_inc(gemm_done, 1)

            def x_wait(group):
                return lambda k: pe.wait_ge(x_ready, 8 * group + k + 1)

            strip_ready(N_KV)
            tile(T_IN, N_KV, 0, xh, xl, x_wait(0))
            stat_sum(NORM_MIX0)
            tile(T_IN + 1, N_KV, P, xh, xl)
            stat_spread(NORM_MIX0)
            strip_ready(N_KR)
            for which in range(2):
                t = T_IN + 2 + which
                free_bank(t)
                s = N_KR % 2
                wh = kr_split(whi[s], which).rearrange("p k r n -> p k (r n)")
                wl = kr_split(wlo[s], which).rearrange("p k r n -> p k (r n)")
                product(bank(t % RING), [((wh[:, k, :], wl[:, k, :]), (xh[:, k, :], xl[:, k, :]))
                                         for k in range(8)]).then_inc(gemm_done, 1)
            strip_ready(N_Q)
            tile(T_IN + 4, N_Q, 0, xh, xl)
            stat_sum(NORM_KV)
            tile(T_IN + 5, N_Q, P, xh, xl)
            stat_spread(NORM_KV)
            strip_ready(N_Q + 1)
            tile(T_IN + 6, N_Q + 1, 0, xh, xl)
            tile(T_IN + 7, N_Q + 1, P, xh, xl)
            stat_sum(NORM_CQ)

            def k_product(s, wait=None):
                product(bank(B_KV), [((pkv(whi[s])[:, k, :], pkv(wlo[s])[:, k, :]), (ckvh[:, k, :], ckvl[:, k, :]))
                                     for k in range(2)], wait).then_inc(k_mm, 1)

            def q_product(s, wait=None):
                product(bank(B_Q), [((pq(whi[s])[:, k, :], pq(wlo[s])[:, k, :]), (cqh[:, k, :], cql[:, k, :]))
                                    for k in range(4)], wait).then_inc(q_mm, 1)

            def v_product(i, s):
                pe.wait_ge(k_lo, i + 1)
                for t in range(TT):
                    part = slice(P * t, P * t + P)
                    last = product(ps[:, B_KV, part], [((ckvh[:, k, part], ckvl[:, k, part]),
                                                        (pkv(whi[s])[:, k, :], pkv(wlo[s])[:, k, :]))
                                                       for k in range(2)])
                last.then_inc(v_mm, 1)

            def scores(i, lead, b):
                e = lead % 2
                s = 4 * lead + b
                if s >= 2:
                    pe.wait_ge(s_exp, i * 8 + (s - 1))
                if b == 0:
                    pe.wait_ge(q_lo, i * 2 + (lead + 1))
                    if e == 0:
                        pe.wait_ge(k_lo, i + (lead // 2 + 1))
                w = P * (b + 1)
                o = ps[:, B_S + b % 2, 0:w]
                part = slice(P * b, P * b + P)
                mm(o, qh[e][:, part], kl[e][:, 0:w], start=True, stop=False)
                mm(o, qh[e][:, part], kh[e][:, 0:w], start=False, stop=False)
                mm(o, ql[e][:, part], kh[e][:, 0:w], start=False, stop=False)
                mm(ps[:, B_S + b % 2, P * b:w], identr[:], maskr[:], start=False, stop=True).then_inc(s_mm, 1)

            def turn_p(i, lead, b):
                s = 4 * lead + b
                pe.wait_ge(p_norm, i * 8 + (s + 1))
                if b >= 2:
                    pe.wait_ge(t_lo, i * 8 + (s - 1))
                for j in range(b + 1):
                    last = tr(ps[:, B_PT + b % 2, P * j:P * j + P], prob[:, b % 2, P * j:P * j + P], ident[:])
                last.then_inc(t_mm, 1)

            def weigh(i, e):
                pe.wait_ge(t_lo, i * 8 + 4 * e + 4)
                pe.wait_ge(v_lo, i + 1)
                for j in range(TT):
                    o = ps[:, B_PV + e, P * j:S]
                    mm(o, vh[:, j, :], ptl[:, j, P * j:S], start=(j == 0), stop=False)
                    mm(o, vh[:, j, :], pth[:, j, P * j:S], start=False, stop=False)
                    last = mm(o, vl[:, j, :], pth[:, j, P * j:S], start=False, stop=(j == TT - 1))
                last.then_inc(pv_mm, 1)

            pe.wait_ge(gemm_evac, T_IN + 8)
            strip_ready(N_PAIR)
            k_product(0, lambda k: pe.wait_ge(c_ready, k + 1))
            stat_spread(NORM_CQ)
            q_product(0, lambda k: pe.wait_ge(c_ready, 2 + k + 1))
            pe.wait_ge(kr_lo, 2)
            scores(0, 0, 0)
            scores(0, 0, 1)

            def attention(i, last=False):
                strip_ready(N_PAIR + 1, i, 2)
                v_product(i, (N_PAIR + 1) % 2)
                turn_p(i, 0, 0)
                scores(i, 0, 2)
                turn_p(i, 0, 1)
                scores(i, 0, 3)
                pe.wait_ge(q_tab, i * 2 + 1)
                q_product((N_PAIR + 1) % 2)
                turn_p(i, 0, 2)
                turn_p(i, 0, 3)
                scores(i, 1, 0)
                scores(i, 1, 1)
                weigh(i, 0)
                turn_p(i, 1, 0)
                scores(i, 1, 2)
                turn_p(i, 1, 1)
                scores(i, 1, 3)
                if not last:
                    strip_ready(N_PAIR + 2, i, 2)
                    pe.wait_ge(v_lo, i + 1)
                    k_product(N_PAIR % 2)
                    pe.wait_ge(q_tab, i * 2 + 2)
                    q_product(N_PAIR % 2)
                turn_p(i, 1, 2)
                turn_p(i, 1, 3)
                if not last:
                    scores(i, 2, 0)
                    scores(i, 2, 1)
                weigh(i, 1)

            with pe.Fori(0, PAIRS - 1) as i:
                attention(i)
            attention(PAIRS - 1, last=True)

            def four_strips(n0, t0, rh, rl, wait=None, order=None):
                for j in range(4):
                    strip_ready(n0 + j)
                    for m in range(2):
                        tile(t0 + 2 * j + m, n0 + j, P * m, rh, rl, wait if j + m == 0 else None, order=order)

            four_strips(N_WO, T_WO, uh, ul, lambda k: pe.wait_ge(o_lo, 2 * k + 2))

            def mlp_quarter(layer, i, q, first=False, last=False):
                n0, t0 = N_MLP[layer] + 8 * q, T_MLP[layer] + 16 * q
                u0 = 8 * QUARTERS * layer + 8 * q
                norm = NORM_MLP0 if layer == 0 else NORM_MLP1
                for j in range(4):
                    strip_ready(n0 + j, i, 8)
                    for m in range(2):
                        tile(t0 + 2 * j + m, n0 + j, P * m, xh, xl,
                             x_wait(1 + 2 * layer) if first and j + m == 0 else None, i, 16)
                        if first and j == 0:
                            (stat_sum, stat_spread)[m](norm)
                for j in range(4):
                    strip_ready(n0 + 4 + j, i, 8)
                    for m in range(2):
                        tile(t0 + 8 + 2 * j + m, n0 + 4 + j, P * m, uh, ul,
                             (lambda k: pe.wait_ge(u_ready, i * 8 + (u0 + k + 1))) if j + m == 0 else None, i, 16)
                        if last and layer == 1 and 2 * j + m:
                            turn_out(2 * j + m - 1)

            def turn_out(m):
                pe.wait_ge(hg_new, m + 1)
                if m >= 2:
                    pe.wait_ge(out_evac, m - 1)
                for t in range(TT):
                    ins = tr(ps[:, B_OUT + m % 2, P * t:P * t + P], hg[:, m % 2, P * t:P * t + P], ident[:])
                ins.then_inc(out_t, 1)

            def mlp(layer):
                mlp_quarter(layer, 0, 0, first=True)
                with pe.Fori(1, QUARTERS - 1) as i:
                    mlp_quarter(layer, i, 0)
                mlp_quarter(layer, 0, QUARTERS - 1, last=True)

            mlp(0)

            strip_ready(N_GATE)
            tile(T_GATE, N_GATE, 0, xh, xl, x_wait(2), width=32 + MH)
            stat_sum(NORM_MIX1)
            for j in range(4):
                strip_ready(N_QK + j)
                for m in range(2):
                    tile(T_QK + 2 * j + m, N_QK + j, P * m, xh, xl)
                    if j + m == 0:
                        stat_spread(NORM_MIX1)
                if j == 1:
                    pe.wait_ge(g_m, 1)
                    pe.wait_ge(g_en, 1)
                    for c, row in ((0, Gc), (32, en)):
                        for t in range(TT):
                            last = tr(ps[:, 5, c + MH * t:c + MH * t + MH], row[:, P * t:P * t + P],
                                      ident[0:MH, 0:MH])
                    last.then_inc(g_t, 1)
            for j in range(4):
                strip_ready(N_V + j)
                s = (N_V + j) % 2
                for i in range(2):
                    t = T_V + 2 * j + i
                    free_bank(t)
                    for half in range(2):
                        part = slice(P * (2 * i + half), P * (2 * i + half) + P)
                        last = product(ps[:, t % RING, 256 * half:256 * half + 256],
                                       [((xh[:, k, part], xl[:, k, part]), (full(whi[s])[:, k, :], full(wlo[s])[:, k, :]))
                                        for k in range(8)])
                    last.then_inc(gemm_done, 1)
            four_strips(N_O, T_O, xh, xl)

            pe.wait_ge(gemm_evac, T_WO2)
            pe.wait_ge(y_lo, 8)
            with pe.Fori(0, MPAIRS) as pr:
                pe.wait_ge(kq_ready, pr + 1)
                for e in range(2):
                    for j in range(TT):
                        z = 4 * e + j
                        if z >= 2:
                            pe.wait_ge(sw_mul, pr * 8 + z - 1)
                        o = ps[:, B_ST + z % 2, 0:LEN[j]]
                        part = slice(P * j, P * j + P)
                        product(o, [((mkh[:, part], mkl[:, part]), (qph[:, e, P * j:S], qpl[:, e, P * j:S]))]) \
                            .then_inc(st_mm, 1)
                for e in range(2):
                    pe.wait_ge(sw_lo, pr * 8 + 4 * e + 4)
                    for b in range(TT):
                        o = ps[:, B_DEN, 2 * (TT * e + b):2 * (TT * e + b) + 2]
                        for j in range(b + 1):
                            part = slice(P * (b - j), P * (b - j) + P)
                            mm(o, swh(e, j)[:, part], onesr[:], start=(j == 0), stop=False)
                            mm(o, swl(e, j)[:, part], onesr[:], start=False, stop=(j == b))
                    pe.wait_ge(mv_lo, pr + 1)
                    for j in range(TT):
                        o = ps[:, B_NUM + e, P * j:S]
                        part = slice(P * e, P * e + P)
                        mm(o, mvh[:, j, part], swl(e, j), start=(j == 0), stop=False)
                        mm(o, mvh[:, j, part], swh(e, j), start=False, stop=False)
                        last = mm(o, mvl[:, j, part], swh(e, j), start=False, stop=(j == TT - 1))
                    last.then_inc(num_mm, 1)
                for e in range(2):
                    pe.wait_ge(num_sq, pr * 2 + e + 1)
                    for b in range(TT):
                        last = mm(ps[:, B_MS, TT * e + b:TT * e + b + 1], numsq[:, e, P * b:P * b + P],
                                  ones[:, 0:1], start=True, stop=True)
                    last.then_inc(ms_mm, 1)
                for e in range(2):
                    pe.wait_ge(diag2_ready, pr * 2 + e + 1)
                    mm(bank(e), ones[:], diag[:, e, :], start=True, stop=True).then_inc(bc2_mm, 1)
            pe.wait_ge(rb_ready, MH)
            four_strips(N_WO2, T_WO2, uh, ul, lambda k: pe.wait_ge(g_ready, k + 1),
                        order=lambda k: k // 2 + 4 * (k % 2))
            mlp(1)
            stat_sum(NORM_FIN)
            turn_out(KD - 1)


_INS = ["x", "positions", "norm_mix_g", "norm_mlp_g", "final_g",
        "mla_w_in", "mla_q_norm_g", "mla_kv_norm_g", "mla_w_uq", "mla_w_ukv", "mla_w_o",
        "mlstm_w_in", "mlstm_conv_w", "mlstm_conv_b", "mlstm_i_b", "mlstm_f_b", "mlstm_head_norm_g", "mlstm_w_o",
        "mlp_w1", "mlp_w2"]


def kernel(**inputs):
    import numpy as _np
    import concourse.bacc as _bacc
    from concourse import mybir as _mybir
    from concourse.bass_utils import run_bass_kernel_spmd as _run

    nc = _bacc.Bacc("TRN2", target_bir_lowering=False, num_devices=1)
    arrays, args = {}, {}
    for name in _INS:
        arr = _np.ascontiguousarray(inputs[name])
        arrays[f"in_{name}"] = arr
        args[name] = nc.dram_tensor(f"in_{name}", arr.shape, _mybir.dt.from_np(arr.dtype), kind="ExternalInput").ap()
    half = ROPE // 2
    lane = _np.arange(P) % ROPE
    freq = _np.float32(THETA) ** (-_np.arange(0, ROPE, 2, dtype=_np.float32) / _np.float32(ROPE))
    rope = _np.stack([freq[lane % half], _np.where(lane < half, -1.0, 1.0)], axis=1).astype(_np.float32)
    arrays["rope_const"] = rope
    args["rope_const"] = nc.dram_tensor("rope_const", rope.shape, _mybir.dt.float32, kind="ExternalInput").ap()
    out = nc.dram_tensor("out_h", (1, S, D), _mybir.dt.float32, kind="ExternalOutput").ap()
    trunk(nc, args, out)
    r = _run(nc, [arrays], core_ids=[0])
    return r.results[0]["out_h"]
```

```python
import numpy as np
import concourse.bass as bass
from concourse import mybir
from contextlib import ExitStack

F32 = mybir.dt.float32
F32R = mybir.dt.float32r
I32 = mybir.dt.int32
ALU = mybir.AluOpType
ACT = mybir.ActivationFunctionType
AX = mybir.AxisListType
ds = bass.ds

P = 128
S = 512
D = 1024
KD = D // P
TT = S // P
QRANK, KVRANK, NOPE, ROPE, VD = 512, 256, 64, 32, 64
QK = NOPE + ROPE
HEADS = 16
PAIRS = HEADS // 2
MH = 8
MPAIRS = MH // 2
CONV = 4
HID = 4096
QUARTERS = HID // D
CAP = 15.0
EPS = 1e-6
THETA = 10000.0
SCALE = QK ** -0.5
NEG = -1e30
MAGIC = 1.5 * 2.0 ** 23
TWO_PI_1 = 6.28125
TWO_PI_2 = float(np.float32(np.floor((2 * np.pi - 6.28125) * 2 ** 21) / 2 ** 21))
TWO_PI_3 = float(np.float32(2 * np.pi - 6.28125 - TWO_PI_2))
PI_IN = 3.1415925

G_MIX, G_MLP, G_FIN = 0, 16, 32
G_Q, G_KV = 40, 44
CONV_W, CONV_B, G_HEAD = 46, 78, 86
PCOLS = 94

N_KV, N_KR, N_Q = 0, 1, 2
N_VA = 4
N_PAIR = 5
N_WO = N_PAIR + 2 * PAIRS
N_MLP = [N_WO + 4, 0]
N_GATE = N_MLP[0] + 8 * QUARTERS
N_QK, N_V, N_O, N_WO2 = N_GATE + 1, N_GATE + 5, N_GATE + 9, N_GATE + 13
N_MLP[1] = N_GATE + 17

T_IN = KD
T_VA = T_IN + 8
T_WO = T_VA + 8
T_MLP = [T_WO + 8, 0]
T_GATE = T_MLP[0] + 16 * QUARTERS
T_QK, T_V, T_O, T_WO2 = T_GATE + 1, T_GATE + 9, T_GATE + 17, T_GATE + 25
T_MLP[1] = T_GATE + 33
RING = 4
B_Q, B_KV, B_S, B_PT, B_PV = 0, 1, 2, 4, 6
B_ST, B_NUM, B_BCH, B_STAT = 4, (3, 7), 0, 6
B_OUT, B_BC, B_COL = 4, 6, 7

NORM_MIX0, NORM_KV, NORM_CQ, NORM_MLP0, NORM_MIX1, NORM_MLP1, NORM_FIN = range(7)
NORM_TILES = [KD, KVRANK // P, QRANK // P, KD, KD, KD, KD]


def adds_before(norm):
    return sum(n - 1 for n in NORM_TILES[:norm])


def strip_over(n, gemm_done, q_mm):
    if n < N_VA:
        return gemm_done, T_IN + 2 * n + 2
    if n == N_VA:
        return gemm_done, T_VA + 8
    if n < N_WO:
        return q_mm, n - N_PAIR + 1
    if n < N_GATE:
        return gemm_done, T_WO + 2 * (n - N_WO) + 2
    return gemm_done, T_GATE + 1 + 2 * (n - N_GATE)


def raw_count(n):
    return sum(48 if m in range(N_PAIR, N_WO, 2) else 32 if m == N_VA else 16 for m in range(n % 2, n + 1, 2))


def trunk(nc, a, out):
    ctx = ExitStack()
    with ctx:
        ctx.enter_context(nc.allow_non_contiguous_dma(reason="small parameters"))

        def sb(name, shape, dt=F32):
            return ctx.enter_context(nc.sbuf_tensor(name, shape, dt))

        def sem(name):
            return ctx.enter_context(nc.semaphore(name))

        h = sb("h", [P, KD, S])
        raw = [sb(f"raw{s}", [P, 2048]) for s in range(2)]
        whi = [sb(f"whi{s}", [P, 2048], F32R) for s in range(2)]
        wlo = [sb(f"wlo{s}", [P, 2048], F32R) for s in range(2)]
        xh = sb("xh", [P, KD, S], F32R)
        xl = sb("xl", [P, KD, S], F32R)
        uh_at = (nc.sbuf_base + 31) // 32 * 32
        uh = sb("uh", [P, KD, S], F32R)
        ul = sb("ul", [P, KD, S], F32R)
        ident = sb("ident", [P, P])
        ones = sb("ones", [P, P])
        mask_s = sb("mask_s", [P, P])
        mask_w = sb("mask_w", [P, P])
        identr = sb("identr", [P, P], F32R)
        onesr = sb("onesr", [P, 2], F32R)
        maskr = sb("maskr", [P, P], F32R)
        mhalf = sb("mhalf", [P, 8])
        prow = sb("prow", [PCOLS, P])
        pcol = sb("pcol", [P, PCOLS])
        acc = sb("acc", [P, S])
        sq = sb("sq", [P, 2, S])
        r_a = sb("r_a", [P, S])
        r_b = sb("r_b", [P, S])
        diag = sb("diag", [P, 2, S])
        var = sb("var", [P, 4])
        rcol = sb("rcol", [P, 4])
        rope_c = sb("rope_c", [P, 2])
        gate_b = sb("gate_b", [MH, 4])
        nmax = sb("nmax", [P, 4])
        rsum = sb("rsum", [P, 4])
        rinv = sb("rinv", [P, 4])
        gcol = sb("gcol", [P, TT * MH])
        encol = sb("encol", [P, MH * TT])
        stat = sb("stat", [P, 2, 12])
        dd = sb("dd", [P, 8])
        var2 = sb("var2", [P, 8])
        rc2 = sb("rc2", [P, 8])
        top = nc.sbuf_base
        arena_bytes = 60 * 1024
        sb("arena", [P, arena_bytes // 4])
        top = (top + 31) // 32 * 32

        class Arena:
            def __init__(self, at=0):
                self.at = at

            def __call__(self, name, shape, dt=F32):
                size = 4 * int(np.prod(shape[1:]))
                t = nc.alloc_sbuf_tensor_at(name, shape, dt, offset=top + self.at)
                self.at += (size + 31) // 32 * 32
                assert self.at <= arena_bytes, (name, self.at)
                return t

        A = Arena()
        x_tok = Arena(0)("x_tok", [P, TT, D])
        cq = A("cq", [P, 4, S])
        ckv = A("ckv", [P, 2, S])
        krot = A("krot", [P, S])
        krot2 = A("krot2", [P, S])
        cqh = A("cqh", [P, 4, S], F32R)
        cql = A("cql", [P, 4, S], F32R)
        ckvh = A("ckvh", [P, 2, S], F32R)
        ckvl = A("ckvl", [P, 2, S], F32R)
        vh = A("vh", [P, TT, P], F32R)
        vl = A("vl", [P, TT, P], F32R)
        prob = A("prob", [P, 2, S])
        cos = A("cos", [P, S])
        sin = A("sin", [P, S])
        tab = A("tab", [P, S])
        qtmp = A("qtmp", [P, S])
        B = Arena(16 * 1024)
        pos_i = B("pos_i", [P, S], I32)
        ang = B("ang", [P, S])
        turn = B("turn", [P, S])
        pt_b = [Arena(8192 * part)(f"pt_b{part}", [P, TT, S], F32R) for part in range(2)]
        pth = [xh[:, 0:TT, :], pt_b[0][:, :, :]]
        ptl = [xl[:, 0:TT, :], pt_b[1][:, :, :]]
        kh = [xh[:, 4 + e, :] for e in range(2)]
        kl = [xl[:, 4 + e, :] for e in range(2)]
        qh = [xh[:, 6 + e, :] for e in range(2)]
        ql = [xl[:, 6 + e, :] for e in range(2)]

        v_all = nc.alloc_sbuf_tensor_at("v_all", [P, PAIRS, S], F32, offset=uh_at)

        def v_slot(i):
            return v_all[:, ds(i, 1), :].rearrange("p a s -> p (a s)").rearrange("p (t n) -> p t n", t=TT)

        C = Arena()
        v_tok = C("v_tok", [P, TT, D])
        sg = C("sg", [P, MH, S])
        base = C.at
        mb = C("mb", [P, 2, S])
        md = C("md", [P, 2, S])
        wt = C("wt", [P, 2, S])
        sw = C("sw", [P, 2, S])
        rb = C("rb", [P, 2, S])
        mkh = C("mkh", [P, 2, S], F32R)
        mkl = C("mkl", [P, 2, S], F32R)
        numsq = rb
        G = Arena(base)
        gi = G("gi", [MH, S])
        gf = G("gf", [MH, S])
        Fc = G("Fc", [MH, S])
        Gc = G("Gc", [MH, S])
        Mc = G("Mc", [MH, S])
        en = G("en", [MH, S])
        zrow = G("zrow", [MH, S])
        E = Arena(base + 16 * 1024)
        yc = E("yc", [P, 2, S])
        cpad = E("cpad", [P, S + CONV - 1])
        ys = E("ys", [P, 2, S])
        otmp = yc

        def flat(t):
            return t[:, :, :].rearrange("p k s -> p (k s)")

        TRI = [0, 512, 896, 1152]
        LEN = [512, 384, 256, 128]

        def swh(e, j):
            return flat(xh)[:, 1280 * e + TRI[j]:1280 * e + TRI[j] + LEN[j]]

        def swl(e, j):
            return flat(xl)[:, 1280 * e + TRI[j]:1280 * e + TRI[j] + LEN[j]]

        mvh = flat(xh)[:, 3072:4096].rearrange("p (t n) -> p t n", t=TT)
        mvl = flat(xl)[:, 3072:4096].rearrange("p (t n) -> p t n", t=TT)

        o_tok = Arena(0)("o_tok", [P, TT, D])
        hg = Arena(16 * 1024)("hg", [P, 2, S])

        m_dram = nc.dram_tensor("m_rows", (MH, S), F32).ap()
        ps = ctx.enter_context(nc.psum_tensor("ps", [P, 8, S], F32))

        def bank(b):
            return ps[:, b, :]

        x_in = [sem(f"x_in{i}") for i in range(2)]
        par_in = sem("par_in")
        pos_in = sem("pos_in")
        raw_full = [sem(f"raw_full{s}") for s in range(2)]
        whi_ready, wlo_ready = sem("whi_ready"), sem("wlo_ready")
        consts = sem("consts")
        par_t, par_ready = sem("par_t"), sem("par_ready")
        gemm_done, gemm_evac = sem("gemm_done"), sem("gemm_evac")
        xh_new, x_ready = sem("xh_new"), sem("x_ready")
        sq_new, acc_add = sem("sq_new"), sem("acc_add")
        stat_col, var_ready, rcol_ready = sem("stat_col"), sem("var_ready"), sem("rcol_ready")
        diag_ready, stat_bc, rbc_ready = sem("diag_ready"), sem("stat_bc"), sem("rbc_ready")
        dve_own = sem("dve_own")
        act_own = sem("act_own")
        pool_own = sem("pool_own")
        ang_ready, trig_ready = sem("ang_ready"), sem("trig_ready")
        kr_new, kr_hi, kr_lo = sem("kr_new"), sem("kr_hi"), sem("kr_lo")
        c_norm, c_hi, c_ready = sem("c_norm"), sem("c_hi"), sem("c_ready")
        q_mm, q_tab, q_hi, q_lo = sem("q_mm"), sem("q_tab"), sem("q_hi"), sem("q_lo")
        k_mm, k_hi, k_lo = sem("k_mm"), sem("k_hi"), sem("k_lo")
        v_hi, v_lo = sem("v_hi"), sem("v_lo")
        s_mm, s_max, s_exp, p_norm = sem("s_mm"), sem("s_max"), sem("s_exp"), sem("p_norm")
        t_mm, t_hi, t_lo = sem("t_mm"), sem("t_hi"), sem("t_lo")
        pv_mm, o_hi, o_lo = sem("pv_mm"), sem("o_hi"), sem("o_lo")
        a_new, u_hi, u_ready = sem("a_new"), sem("u_hi"), sem("u_ready")
        y_new, y_hi, y_lo = sem("y_new"), sem("y_hi"), sem("y_lo")
        sig_new, sg_ready = sem("sig_new"), sem("sg_ready")
        g_ln, g_m, g_en = sem("g_ln"), sem("g_m"), sem("g_en")
        m_out, mb_in = sem("m_out"), [sem(f"mb_in{e}") for e in range(2)]
        g_t, gcol_ready = sem("g_t"), sem("gcol_ready")
        md_ready, mk_ready, mv_hi, mv_lo = sem("md_ready"), sem("mk_ready"), sem("mv_hi"), sem("mv_lo")
        st_mm, w_exp, sw_mul, sw_hi, sw_lo = sem("st_mm"), sem("w_exp"), sem("sw_mul"), sem("sw_hi"), sem("sw_lo")
        num_mm, num_sq, ms_mm, stat_read = sem("num_mm"), sem("num_sq"), sem("ms_mm"), sem("stat_read")
        var2_ready, rc2_ready, diag2_ready = sem("var2_ready"), sem("rc2_ready"), sem("diag2_ready")
        bc2_mm, rb_ready, hs_ready = sem("bc2_mm"), sem("rb_ready"), sem("hs_ready")
        g_hi, g_ready = sem("g_hi"), sem("g_ready")
        hg_new, out_t, out_evac, out_ready, stored = (sem("hg_new"), sem("out_t"), sem("out_evac"),
                                                      sem("out_ready"), sem("stored"))

        def fixed(eng):
            eng.wait_ge(consts, 1)

        class Own:
            def __init__(self, eng, semaphore):
                self.eng, self.sem, self.n, self.loop = eng, semaphore, 0, None

            def link(self, ins):
                ins.then_inc(self.sem, 1)
                self.n += 1
                v = self.n if self.loop is None else self.loop[0] * self.loop[1] + self.n
                self.eng.wait_ge(self.sem, v)

            def enter(self, i, start, per):
                self.loop, self.at = (i, per), self.n
                self.n -= start * per

            def leave(self, start, end):
                i, per = self.loop
                assert self.n == self.at - start * per + per, (self.n - self.at + start * per, per)
                self.n, self.loop = self.at + (end - start) * per, None

        def full(t):
            return t[:, :].rearrange("p (k n) -> p k n", k=8)

        def kr_raw(t):
            return t[:, 0:8 * ROPE].rearrange("p (k n) -> p k n", k=8)

        def kr_split(t, which):
            return t[:, 1024 * which:1024 * which + 1024].rearrange("p (k r n) -> p k r n", k=8, r=4)

        def gate_raw(t):
            return t[:, 0:8 * 2 * MH].rearrange("p (k n) -> p k n", k=8)

        def pq_raw(t):
            return t[:, 0:4 * QK].rearrange("p (k n) -> p k n", k=4)

        def pkv_raw(t):
            return t[:, 4 * QK:4 * QK + 256].rearrange("p (k n) -> p k n", k=2)

        def pq(t):
            return t[:, 0:512].rearrange("p (k n) -> p k n", k=4)

        def pkv(t):
            return t[:, 512:768].rearrange("p (k n) -> p k n", k=2)

        def split_parts(n_kind, s):
            r, hi, lo = raw[s], whi[s], wlo[s]
            if n_kind == "full":
                return [(r[:, :], hi[:, :], lo[:, :])]
            if n_kind == "kr":
                half = ROPE // 2
                rr = kr_raw(r)
                parts = []
                for which, dst, src in ((0, 0, 0), (0, half, half), (1, 0, half), (1, half, 0)):
                    src_ap = rr[:, :, src:src + half].unsqueeze(2).broadcast_to([P, 8, 4, half])
                    parts.append((src_ap, kr_split(hi, which)[:, :, :, dst:dst + half],
                                  kr_split(lo, which)[:, :, :, dst:dst + half]))
                return parts
            if n_kind == "gate":
                return [(gate_raw(r)[:, :, MH * g:MH * g + MH], full(hi)[:, :, 32 * g:32 * g + MH],
                         full(lo)[:, :, 32 * g:32 * g + MH]) for g in range(2)]
            assert n_kind in ("kq", "q")
            half = ROPE // 2
            parts = [(pkv_raw(r), pkv(hi), pkv(lo))] if n_kind == "kq" else []
            return parts + [(pq_raw(r), pq(hi)[:, :, 0:QK], pq(lo)[:, :, 0:QK]),
                    (pq_raw(r)[:, :, NOPE + half:QK], pq(hi)[:, :, QK:QK + half], pq(lo)[:, :, QK:QK + half]),
                    (pq_raw(r)[:, :, NOPE:NOPE + half], pq(hi)[:, :, QK + half:P], pq(lo)[:, :, QK + half:P])]

        block = ctx.enter_context(nc.Block())

        @block.sync
        def _(sp):
            def slot_free(n, i=0, per=0):
                if n >= 2:
                    sp.wait_ge(wlo_ready, i * per + (n - 1))

            def load(n, src):
                slot_free(n)
                sp.dma_start(full(raw[n % 2]), src).then_inc(raw_full[n % 2], 16)

            def cols(w, c, width=256):
                return w[:, c:c + width].rearrange("(k p) n -> p k n", p=P)

            w_in = a["mla_w_in"][0]
            for i in range(2):
                sp.dma_start(x_tok[:, :, 512 * i:512 * i + 512],
                             a["x"][0, :, 512 * i:512 * i + 512].rearrange("(t p) n -> p t n", p=P)) \
                    .then_inc(x_in[i], 16)
            load(N_KV, cols(w_in, QRANK))
            sp.dma_start(kr_raw(raw[1]), cols(w_in, QRANK + KVRANK, ROPE)).then_inc(raw_full[1], 16)
            load(N_Q, cols(w_in, 0))
            load(N_Q + 1, cols(w_in, 256))
            slot_free(N_VA)
            for k in range(2):
                kv_heads = a["mla_w_ukv"][0, P * k:P * k + P, :].rearrange("p (h n) -> p h n", h=HEADS)
                sp.dma_start(raw[N_VA % 2][:, 1024 * k:1024 * k + 1024].rearrange("p (h n) -> p h n", h=HEADS),
                             kv_heads[:, :, NOPE:NOPE + VD]).then_inc(raw_full[N_VA % 2], 16)

            def load_head(p, n, head, with_k):
                slot_free(n, p, 2)
                s = n % 2
                sp.dma_start(pq_raw(raw[s]),
                             a["mla_w_uq"][0, :, ds(head * QK, QK)].rearrange("(k p) n -> p k n", p=P)) \
                    .then_inc(raw_full[s], 16)
                for k in range(2) if with_k else ():
                    both = a["mla_w_ukv"][0, P * k:P * k + P, ds(p * 256, 256)].rearrange("p (e n) -> p e n", e=2)
                    sp.dma_start(pkv_raw(raw[s])[:, k, :].rearrange("p (e n) -> p e n", e=2),
                                 both[:, :, 0:NOPE]).then_inc(raw_full[s], 16)

            with sp.Fori(0, PAIRS) as p:
                load_head(p, N_PAIR, p * 2, True)
                load_head(p, N_PAIR + 1, p * 2 + 1, False)
            for j in range(4):
                load(N_WO + j, cols(a["mla_w_o"][0], 256 * j))

            def load_mlp(layer):
                n0 = N_MLP[layer]
                with sp.Fori(0, QUARTERS) as q:
                    for j in range(8):
                        n = n0 + j
                        slot_free(n, q, 8)
                        if j < 4:
                            src = a["mlp_w1"][layer, :, ds(q * D + 256 * j, 256)]
                        else:
                            src = a["mlp_w2"][layer, ds(q * D, D), 256 * (j - 4):256 * (j - 3)]
                        sp.dma_start(full(raw[n % 2]), src.rearrange("(k p) n -> p k n", p=P)) \
                            .then_inc(raw_full[n % 2], 16)

            load_mlp(0)
            w_in = a["mlstm_w_in"][0]
            slot_free(N_GATE)
            sp.dma_start(gate_raw(raw[N_GATE % 2]), cols(w_in, 3 * D, 2 * MH)).then_inc(raw_full[N_GATE % 2], 16)
            for j in range(4):
                load(N_QK + j, cols(w_in, 256 * j))
            sp.wait_ge(g_m, 1)
            sp.dma_start(m_dram, Mc[:, :]).then_inc(m_out, 16)
            for j in range(4):
                load(N_V + j, cols(w_in, D + 256 * j))
            sp.wait_ge(m_out, 16)
            sp.wait_ge(gcol_ready, 2)
            for e in range(2):
                sp.dma_start(mb[:, e, :], m_dram[e:e + 1, :].broadcast_to([P, S])).then_inc(mb_in[e], 16)
            for j in range(4):
                load(N_O + j, cols(w_in, 2 * D + 256 * j))
            for j in range(2):
                load(N_WO2 + j, cols(a["mlstm_w_o"][0], 256 * j))
            with sp.Fori(1, MPAIRS) as pr:
                for e in range(2):
                    sp.wait_ge(w_exp, pr * 8 + (4 * e - 4))
                    sp.dma_start(mb[:, e, :], m_dram[ds(pr * 2 + e, 1), :].broadcast_to([P, S])) \
                        .then_inc(mb_in[e], 16)
            for j in range(2, 4):
                load(N_WO2 + j, cols(a["mlstm_w_o"][0], 256 * j))
            load_mlp(1)
            for t in range(TT):
                sp.wait_ge(out_ready, t + 1)
                sp.dma_start(out[0, P * t:P * t + P, :], o_tok[:, t, :]).then_inc(stored, 16)
            sp.wait_ge(stored, 16 * TT)

        @block.gpsimd
        def _(pool):
            own = Own(pool, pool_own)
            g = nc.gpsimd
            g.memset(ones[:], 1.0)
            g.memset(mhalf[:], -0.5)
            g.memset(mask_s[:], 0.0)
            g.memset(mask_w[:], 0.0)
            own.link(g.memset(ident[:], 0.0))
            g.affine_select(out=ident[:], in_=ident[:], compare_op=ALU.not_equal, fill=1.0, base=0,
                            pattern=[[-1, P]], channel_multiplier=1)
            g.affine_select(out=mask_s[:], in_=mask_s[:], compare_op=ALU.is_ge, fill=NEG, base=0,
                            pattern=[[-1, P]], channel_multiplier=1)
            own.link(g.affine_select(out=mask_w[:], in_=mask_w[:], compare_op=ALU.is_ge, fill=-NEG, base=0,
                                     pattern=[[1, P]], channel_multiplier=-1))
            g.tensor_copy(onesr[:], ones[:, 0:2])
            g.tensor_copy(identr[:], ident[:])
            g.tensor_copy(maskr[:], mask_s[:]).then_inc(consts, 1)

            def norm_adds(norm):
                first = sum(NORM_TILES[:norm])
                for m in range(1, NORM_TILES[norm]):
                    k = adds_before(norm) + m - 1
                    pool.wait_ge(sq_new, first + m + 1)
                    if m > 1:
                        pool.wait_ge(acc_add, k)
                    g.tensor_tensor(acc[:], acc[:], sq[:, k % 2, :], ALU.add).then_inc(acc_add, 1)

            def norm_pow(norm):
                pool.wait_ge(var_ready, norm + 1)
                g.tensor_tensor(rcol[:], var[:], mhalf[:, 0:4], ALU.pow).then_inc(rcol_ready, 1)

            norm_adds(NORM_MIX0)
            norm_pow(NORM_MIX0)
            norm_adds(NORM_KV)
            norm_pow(NORM_KV)
            norm_adds(NORM_CQ)
            norm_pow(NORM_CQ)

            def head_low(n, kind, p=0):
                pool.wait_ge(whi_ready, p * 2 + (n + 1))
                for src, hi, lo in split_parts(kind, n % 2):
                    last = g.tensor_tensor(lo, src, hi.bitcast(F32), ALU.subtract)
                last.then_inc(wlo_ready, 1)

            pool.wait_ge(wlo_ready, N_PAIR)
            with pool.Fori(0, PAIRS) as p:
                head_low(N_PAIR, "kq", p)
                head_low(N_PAIR + 1, "q", p)

            def low_hidden(layer, q, lead, per):
                for j in range(8):
                    pool.wait_ge(u_hi, q * per + (lead + j + 1))
                    g.tensor_tensor(ul[:, j, :], sq[:, j % 2, :], uh[:, j, :].bitcast(F32), ALU.subtract) \
                        .then_inc(u_ready, 1)

            def mlp(layer):
                norm_adds(NORM_MLP0 if layer == 0 else NORM_MLP1)
                norm_pow(NORM_MLP0 if layer == 0 else NORM_MLP1)
                with pool.Fori(0, QUARTERS) as q:
                    low_hidden(layer, q, 8 * QUARTERS * layer, 8)

            mlp(0)
            norm_adds(NORM_MIX1)
            norm_pow(NORM_MIX1)
            for m in range(8):
                pool.wait_ge(y_hi, m + 1)
                g.tensor_tensor(ul[:, m, :], ys[:, m % 2, :], uh[:, m, :].bitcast(F32), ALU.subtract) \
                    .then_inc(y_lo, 1)
            def k_copy(i, lead):
                e, pair = lead % 2, i + lead // 2
                rows = slice(64 * e, 64 * e + 64)
                fixed(pool)
                if lead > 1:
                    pool.wait_ge(st_mm, i * 8 + (4 * lead - 4))
                g.tensor_copy(mkh[rows, e, :], uh[rows, ds(pair + 4, 1), :].rearrange("p a s -> p (a s)").bitcast(F32))
                own.link(g.tensor_copy(mkl[rows, e, :],
                                       ul[rows, ds(pair + 4, 1), :].rearrange("p a s -> p (a s)").bitcast(F32)))
                g.nop().then_inc(mk_ready, 1)

            def head_parts(i, lead, first=False, copy=True):
                for j in range(TT):
                    z = 4 * lead + j
                    pool.wait_ge(sw_hi, i * 8 + (z + 1))
                    g.tensor_tensor(swl(lead % 2, j), sw[:, z % 2, 0:LEN[j]], swh(lead % 2, j).bitcast(F32),
                                    ALU.subtract).then_inc(sw_lo, 1)
                if not first:
                    head_pow(i, lead - 1)
                if copy:
                    if first:
                        pool.wait_ge(sw_lo, TT)
                    else:
                        pool.wait_ge(rc2_ready, i * 2 + lead)
                    k_copy(i, lead + 2)

            def head_pow(i, lead):
                c = slice(4 * (lead % 2), 4 * (lead % 2) + 4)
                pool.wait_ge(var2_ready, i * 2 + (lead + 1))
                g.tensor_tensor(rc2[:, c], var2[:, c], mhalf[:, 0:4], ALU.pow).then_inc(rc2_ready, 1)

            pool.wait_ge(y_lo, 8)
            for e in range(2):
                rows = slice(64 * (1 - e), 64 * (1 - e) + 64)
                g.memset(mkh[rows, e, :].bitcast(F32), 0.0)
                own.link(g.memset(mkl[rows, e, :].bitcast(F32), 0.0))
                k_copy(0, e)
            for m in range(8):
                pool.wait_ge(sig_new, m + 1)
                g.tensor_scalar(sg[:, m, :], sg[:, m, :], pcol[:, G_HEAD + m:G_HEAD + m + 1], None, ALU.mult) \
                    .then_inc(sg_ready, 1)
            head_parts(0, 0, first=True)
            with pool.Fori(0, MPAIRS - 2) as i:
                own.enter(i, 0, 2)
                head_parts(i, 1)
                head_parts(i, 2)
                own.leave(0, MPAIRS - 2)
            head_parts(MPAIRS - 2, 1)
            head_parts(MPAIRS - 2, 2, copy=False)
            head_parts(MPAIRS - 1, 1, copy=False)
            head_pow(MPAIRS - 1, 1)
            mlp(1)
            norm_adds(NORM_FIN)
            norm_pow(NORM_FIN)

        @block.scalar
        def _(act):
            own = Own(act, act_own)
            sc = nc.scalar
            for at, src in ((G_MIX, a["norm_mix_g"].rearrange("l (m p) -> (l m) p", p=P)),
                            (G_MLP, a["norm_mlp_g"].rearrange("l (m p) -> (l m) p", p=P)),
                            (G_FIN, a["final_g"].rearrange("(m p) -> m p", p=P)),
                            (G_Q, a["mla_q_norm_g"].rearrange("l (m p) -> (l m) p", p=P)),
                            (G_KV, a["mla_kv_norm_g"].rearrange("l (m p) -> (l m) p", p=P)),
                            (CONV_W, a["mlstm_conv_w"].rearrange("l c (m p) -> (l c m) p", p=P)),
                            (CONV_B, a["mlstm_conv_b"].rearrange("l (m p) -> (l m) p", p=P)),
                            (G_HEAD, a["mlstm_head_norm_g"].rearrange("l (m p) -> (l m) p", p=P))):
                act.dma_start(prow[at:at + src.shape[0], :], src).then_inc(par_in, 16)
            act.dma_start(rope_c[:], a["rope_const"]).then_inc(pos_in, 16)
            act.dma_start(pos_i[:], a["positions"].broadcast_to([P, S])).then_inc(pos_in, 16)
            act.dma_start(gate_b[:, 0:1], a["mlstm_i_b"].rearrange("l h -> h l")).then_inc(pos_in, 16)
            act.dma_start(gate_b[:, 1:2], a["mlstm_f_b"].rearrange("l h -> h l")).then_inc(pos_in, 16)

            def split(n, kind="full", i=0, over=0, arrived=0):
                act.wait_ge(raw_full[n % 2], i * arrived + raw_count(n))
                if n >= 2:
                    which, value = strip_over(n - 2, gemm_done, q_mm)
                    act.wait_ge(which, i * over + value)
                parts = split_parts(kind, n % 2)
                for src, hi, _ in parts:
                    last = sc.copy(hi, src)
                last.then_inc(whi_ready, 1)

            def square(norm, m, src):
                if m == 0:
                    if norm:
                        act.wait_ge(stat_col, norm)
                    sc.activation(acc[:], src, ACT.Square).then_inc(sq_new, 1)
                else:
                    k = adds_before(norm) + m - 1
                    if k >= 2:
                        act.wait_ge(acc_add, k - 1)
                    sc.activation(sq[:, k % 2, :], src, ACT.Square).then_inc(sq_new, 1)

            def update(t0, norm, gain, m):
                act.wait_ge(gemm_evac, t0 + m + 1)
                square(norm, m, h[:, m, :])
                sc.activation(xh[:, m, :], h[:, m, :], ACT.Copy, scale=pcol[:, gain + m:gain + m + 1]) \
                    .then_inc(xh_new, 1)

            act.wait_ge(ang_ready, 1)
            sc.activation(sin[:], ang[:], ACT.Sin, scale=rope_c[:, 1:2]).then_inc(trig_ready, 1)
            sc.activation(cos[:], turn[:], ACT.Sin).then_inc(trig_ready, 1)

            act.wait_ge(par_ready, 1)
            for m in range(KD):
                if m == 4:
                    split(N_KV)
                update(0, NORM_MIX0, G_MIX, m)
            split(N_KR, "kr")
            split(N_Q)
            for m in range(2):
                act.wait_ge(gemm_evac, T_IN + m + 1)
                square(NORM_KV, m, ckv[:, m, :])
            split(N_Q + 1)

            def c_high(n_before, src, hi, gain, tiles):
                for m in range(tiles):
                    act.wait_ge(c_norm, n_before + m + 1)
                    sc.activation(hi[:, m, :], src[:, m, :], ACT.Copy, scale=pcol[:, gain + m:gain + m + 1]) \
                        .then_inc(c_hi, 1)

            c_high(0, ckv, ckvh, G_KV, 2)
            split(N_VA)
            for m in range(4):
                act.wait_ge(gemm_evac, T_IN + 4 + m + 1)
                square(NORM_CQ, m, cq[:, m, :])
            split(N_PAIR, "kq")
            act.wait_ge(kr_new, 1)
            for e in range(2):
                sc.copy(kh[e][64:128, :], krot[64:128, :]).then_inc(kr_hi, 1)

            def k_high(e, i, lead):
                act.wait_ge(k_mm, i + (lead + 1))
                if e and lead:
                    act.wait_ge(s_mm, i * 8 + 8)
                sc.copy(kh[e][0:64, :], ps[64 * e:64 * e + 64, B_KV, :]).then_inc(k_hi, 1)

            def q_high(e, i, lead):
                act.wait_ge(q_tab, i * 2 + (lead + 1))
                sc.copy(qh[e], qtmp[:]).then_inc(q_hi, 1)

            def exp(i, lead, b):
                w = P * (b + 1)
                s = 4 * lead + b
                act.wait_ge(s_max, i * 8 + (s + 1))
                if s >= 2:
                    act.wait_ge(t_mm, i * 8 + (s - 1))
                sc.activation(prob[:, b % 2, 0:w], ps[:, B_S + b % 2, 0:w], ACT.Exp, bias=nmax[:, b:b + 1],
                              accum_out=rsum[:, b:b + 1]).then_inc(s_exp, 1)

            def pt_high(i, lead, b):
                s = 4 * lead + b
                act.wait_ge(t_mm, i * 8 + (s + 1))
                sc.copy(pth[lead % 2][:, 0:b + 1, P * b:P * b + P],
                        ps[:, B_PT + b % 2, 0:P * (b + 1)].rearrange("p (j q) -> p j q", q=P)).then_inc(t_hi, 1)

            def o_high(i, lead):
                e, pair = lead % 2, i + lead // 2
                fixed(act)
                act.wait_ge(pv_mm, i * 2 + (lead + 1))
                sc.copy(uh[64 * e:64 * e + 64, ds(pair, 1), :].rearrange("p a s -> p (a s)"),
                        ps[64 * e:64 * e + 64, B_PV + e, :]).then_inc(o_hi, 1)

            c_high(2, cq, cqh, G_Q, 4)
            for e in range(2):
                k_high(e, 0, 0)
            split(N_PAIR + 1, "q")
            q_high(0, 0, 0)
            exp(0, 0, 0)
            exp(0, 0, 1)

            def attention(i, first=False, last=False):
                pt_high(i, 0, 0)
                exp(i, 0, 2)
                if last:
                    split(N_WO)
                else:
                    split(N_PAIR + 2, "kq", i, 2, 48)
                pt_high(i, 0, 1)
                q_high(1, i, 1)
                exp(i, 0, 3)
                pt_high(i, 0, 2)
                exp(i, 1, 0)
                if not first:
                    o_high(i, -1)
                sc.copy(vh[:, :, :], v_slot(i)).then_inc(v_hi, 1)
                pt_high(i, 0, 3)
                exp(i, 1, 1)
                if not last:
                    k_high(0, i, 1)
                pt_high(i, 1, 0)
                exp(i, 1, 2)
                if not last:
                    q_high(0, i, 2)
                pt_high(i, 1, 1)
                exp(i, 1, 3)
                if last:
                    split(N_WO + 1)
                else:
                    split(N_PAIR + 3, "q", i, 2, 16)
                    k_high(1, i, 1)
                pt_high(i, 1, 2)
                if not last:
                    exp(i, 2, 0)
                pt_high(i, 1, 3)
                if not last:
                    exp(i, 2, 1)
                o_high(i, 0)

            attention(0, first=True)
            with act.Fori(1, PAIRS - 1) as i:
                attention(i)
            attention(PAIRS - 1, last=True)
            o_high(PAIRS, -1)

            def residual_stage(n0, t0, norm, gain):
                for j in range(4):
                    if j:
                        split(n0 + j + 1)
                    for m in (2 * j, 2 * j + 1):
                        update(t0, norm, gain, m)

            residual_stage(N_WO, T_WO, NORM_MLP0, G_MLP)

            def final_tile(m):
                act.wait_ge(gemm_evac, T_MLP[1] + 16 * QUARTERS - 8 + m + 1)
                square(NORM_FIN, m, h[:, m, :])
                if m >= 2:
                    act.wait_ge(out_t, m - 1)
                sc.activation(hg[:, m % 2, :], h[:, m, :], ACT.Copy, scale=pcol[:, G_FIN + m:G_FIN + m + 1]) \
                    .then_inc(hg_new, 1)

            def final_evac(m):
                act.wait_ge(out_t, m + 1)
                sc.copy(o_tok[:, :, P * m:P * m + P],
                        ps[:, B_OUT + m % 2, :].rearrange("p (t n) -> p t n", t=TT)).then_inc(out_evac, 1)

            def mlp_quarter(layer, i, q, last=False):
                n0 = N_MLP[layer] + 8 * q
                for j in range(4):
                    split(n0 + j + 1, "full", i, 16, 64)
                    for m in (2 * j, 2 * j + 1):
                        act.wait_ge(a_new, i * 8 + (8 * QUARTERS * layer + 8 * q + m + 1))
                        sc.copy(uh[:, m, :], sq[:, m % 2, :]).then_inc(u_hi, 1)
                for j in range(4):
                    if not last:
                        split(n0 + j + 5, "full", i, 16, 64)
                    elif j < 3:
                        split(n0 + j + 5)
                    elif layer == 0:
                        split(n0 + 8, "gate")
                    if last:
                        for m in (2 * j, 2 * j + 1):
                            if layer == 0:
                                update(T_MLP[0] + 16 * QUARTERS - 8, NORM_MIX1, G_MIX + 8, m)
                            else:
                                final_tile(m)
                                if m:
                                    final_evac(m - 1)

            def mlp(layer):
                with act.Fori(0, QUARTERS - 1) as i:
                    mlp_quarter(layer, i, 0)
                mlp_quarter(layer, 0, QUARTERS - 1, last=True)

            mlp(0)

            split(N_QK)
            act.wait_ge(gemm_evac, T_GATE + 1)
            sc.activation(gi[:], gi[:], ACT.Tanh, bias=gate_b[:, 2:3], scale=1.0 / CAP)
            own.link(sc.activation(gf[:], gf[:], ACT.Tanh, bias=gate_b[:, 3:4], scale=1.0 / CAP))
            own.link(sc.activation(gf[:], gf[:], ACT.Exp, scale=-CAP))
            sc.activation(gf[:], gf[:], ACT.Ln, bias=1.0).then_inc(g_ln, 1)
            for j in range(4):
                split(N_QK + j + 1)
                for m in (2 * j, 2 * j + 1):
                    act.wait_ge(y_new, m + 1)
                    if m >= 2:
                        act.wait_ge(y_lo, m - 1)
                    own.link(sc.activation(ys[:, m % 2, :], yc[:, m % 2, :], ACT.Silu))
                    sc.copy(uh[:, m, :], ys[:, m % 2, :]).then_inc(y_hi, 1)
                if j == 0:
                    act.wait_ge(g_m, 1)
                    sc.activation(en[:], en[:], ACT.Exp, scale=-1.0).then_inc(g_en, 1)
            for j in range(4):
                split(N_V + j + 1)
            for j in range(4):
                split(N_O + j + 1)
                for m in (2 * j, 2 * j + 1):
                    act.wait_ge(gemm_evac, T_O + m + 1)
                    sc.activation(sg[:, m, :], otmp[:, m % 2, :], ACT.Sigmoid).then_inc(sig_new, 1)
            def weights(i, lead, j):
                z, e, pair = 4 * lead + j, lead % 2, i + lead // 2
                fixed(act)
                if j == 0:
                    act.wait_ge(mb_in[e], pair * 16 + 16)
                    act.wait_ge(md_ready, i * 2 + (lead + 1))
                if z >= 2:
                    act.wait_ge(sw_mul, i * 8 + (z - 1))
                bias = gcol[:, ds(pair * 2 + (MH * j + e), 1)]
                last = sc.activation(wt[:, z % 2, 0:P], md[:, e, P * j:P * j + P], ACT.Exp, bias=bias, scale=-1.0)
                if j < TT - 1:
                    last = sc.activation(wt[:, z % 2, P:LEN[j]], mb[:, e, P * (j + 1):S], ACT.Exp,
                                         bias=bias, scale=-1.0)
                last.then_inc(w_exp, 1)

            def high(i, lead, j):
                z = 4 * lead + j
                act.wait_ge(sw_mul, i * 8 + (z + 1))
                sc.copy(swh(lead % 2, j), sw[:, z % 2, 0:LEN[j]]).then_inc(sw_hi, 1)

            def v_high(i, lead):
                e, pair = lead % 2, i + lead // 2
                sc.copy(mvh[:, :, P * e:P * e + P], v_tok[:, :, ds(pair * 256 + P * e, P)]).then_inc(mv_hi, 1)

            def square_num(i, lead):
                e = lead % 2
                act.wait_ge(num_mm, i * 2 + (lead + 1))
                sc.activation(numsq[:, e, :], bank(B_NUM[e]), ACT.Square).then_inc(num_sq, 1)

            def gated_high(i, lead):
                e, pair = lead % 2, i + lead // 2
                fixed(act)
                act.wait_ge(hs_ready, i * 2 + (lead + 1))
                sc.copy(uh[:, ds(pair + 4 * e, 1), :].rearrange("p a s -> p (a s)"), rb[:, e, :]) \
                    .then_inc(g_hi, 1)

            def head_step(i, lead, first=False, last=False):
                high(i, lead, 3)
                if not last:
                    weights(i, lead + 1, 0)
                    weights(i, lead + 1, 1)
                    high(i, lead + 1, 0)
                    v_high(i, lead + 1)
                    weights(i, lead + 1, 2)
                    high(i, lead + 1, 1)
                else:
                    act.wait_ge(g_ready, MH - 2)
                square_num(i, lead)
                if not last:
                    weights(i, lead + 1, 3)
                    high(i, lead + 1, 2)
                if not first:
                    gated_high(i, lead - 1)

            weights(0, 0, 0)
            weights(0, 0, 1)
            act.wait_ge(gemm_done, T_O + 8)
            high(0, 0, 0)
            v_high(0, 0)
            weights(0, 0, 2)
            high(0, 0, 1)
            weights(0, 0, 3)
            high(0, 0, 2)
            head_step(0, 0, first=True)
            with act.Fori(0, MPAIRS - 1) as i:
                head_step(i, 1)
                head_step(i, 2)
            split(N_WO2 + 1)
            head_step(MPAIRS - 1, 1, last=True)
            gated_high(MPAIRS - 1, 1)
            residual_stage(N_WO2, T_WO2, NORM_MLP1, G_MLP + 8)
            mlp(1)
            final_evac(KD - 1)

        @block.vector
        def _(dve):
            own = Own(dve, dve_own)
            v = nc.vector

            def split(n, kind="full", i=0, per=0):
                dve.wait_ge(whi_ready, i * per + (n + 1))
                for src, hi, lo in split_parts(kind, n % 2):
                    last = v.tensor_tensor(lo, src, hi.bitcast(F32), ALU.subtract)
                last.then_inc(wlo_ready, 1)

            def low(t_lo_, src, hi, gain=None):
                if gain is None:
                    return v.tensor_tensor(t_lo_, src, hi.bitcast(F32), ALU.subtract)
                return v.scalar_tensor_tensor(out=t_lo_, in0=src, scalar=gain, in1=hi.bitcast(F32),
                                              op0=ALU.mult, op1=ALU.subtract)

            def x_low(group, gain, m):
                dve.wait_ge(xh_new, 8 * group + m + 1)
                low(xl[:, m, :], h[:, m, :], xh[:, m, :], pcol[:, gain + m:gain + m + 1]).then_inc(x_ready, 1)

            def stat_diag(norm, width):
                dve.wait_ge(stat_col, norm + 1)
                v.tensor_scalar(var[:], ps[:, B_COL, 0:4], 1.0 / width, EPS, ALU.mult, ALU.add) \
                    .then_inc(var_ready, 1)
                dve.wait_ge(rcol_ready, norm + 1)
                for t in range(TT):
                    last = v.tensor_scalar(diag[:, 0, P * t:P * t + P], ident[:], rcol[:, t:t + 1], None,
                                           ALU.mult)
                last.then_inc(diag_ready, 1)

            def stat_row(norm, r):
                dve.wait_ge(stat_bc, norm + 1)
                v.tensor_copy(r[:], bank(B_BC)).then_inc(rbc_ready, 1)
                dve.wait_ge(rbc_ready, norm + 1)

            dve.wait_ge(pos_in, 64)
            own.link(v.tensor_copy(ang[:], pos_i[:]))
            own.link(v.tensor_scalar(ang[:], ang[:], rope_c[:, 0:1], None, ALU.mult))
            own.link(v.tensor_scalar(turn[:], ang[:], 1.0 / (2 * np.pi), MAGIC, ALU.mult, ALU.add))
            own.link(v.tensor_scalar(turn[:], turn[:], MAGIC, None, ALU.subtract))
            for part in (TWO_PI_1, TWO_PI_2, TWO_PI_3):
                own.link(v.scalar_tensor_tensor(out=ang[:], in0=turn[:], scalar=-part, in1=ang[:],
                                                op0=ALU.mult, op1=ALU.add))
            own.link(v.tensor_scalar(ang[:], ang[:], PI_IN, -PI_IN, ALU.min, ALU.max))
            own.link(v.tensor_scalar(turn[:], ang[:], np.pi / 2, -2 * np.pi, ALU.is_gt, ALU.mult))
            own.link(v.scalar_tensor_tensor(out=turn[:], in0=ang[:], scalar=np.pi / 2, in1=turn[:],
                                            op0=ALU.add, op1=ALU.add))
            own.link(v.tensor_scalar(turn[:], turn[:], PI_IN, -PI_IN, ALU.min, ALU.max))
            v.tensor_scalar(gate_b[:, 2:4], gate_b[:, 0:2], 1.0 / CAP, None, ALU.mult).then_inc(ang_ready, 1)
            v.memset(tab[0:64, :], SCALE)
            dve.wait_ge(par_t, 1)
            v.tensor_copy(pcol[:], ps[:, B_COL, 0:PCOLS]).then_inc(par_ready, 1)
            dve.wait_ge(par_ready, 1)
            dve.wait_ge(trig_ready, 2)
            v.tensor_scalar(tab[64:96, :], cos[64:96, :], SCALE, None, ALU.mult)
            own.link(v.tensor_scalar(tab[96:128, :], sin[96:128, :], SCALE, None, ALU.mult))

            for m in range(KD):
                if m == 5:
                    split(N_KV)
                dve.wait_ge(gemm_done, m + 1)
                v.tensor_copy(h[:, m, :], bank(m % RING)).then_inc(gemm_evac, 1)
                if m:
                    x_low(0, G_MIX, m - 1)
            x_low(0, G_MIX, KD - 1)
            split(N_KR, "kr")
            stat_diag(NORM_MIX0, D)
            stat_row(NORM_MIX0, r_a)

            def scaled(t, dst, r):
                dve.wait_ge(gemm_done, t + 1)
                return v.tensor_tensor(dst, bank(t % RING), r[:], ALU.mult)

            for m in range(2):
                scaled(T_IN + m, ckv[:, m, :], r_a).then_inc(gemm_evac, 1)
            split(N_Q)
            dve.wait_ge(gemm_done, T_IN + 3)
            v.tensor_tensor(krot[:], bank((T_IN + 2) % RING), cos[:], ALU.mult).then_inc(gemm_evac, 1)
            dve.wait_ge(gemm_done, T_IN + 4)
            v.tensor_tensor(krot2[:], bank((T_IN + 3) % RING), sin[:], ALU.mult).then_inc(gemm_evac, 1)
            dve.wait_ge(gemm_evac, T_IN + 4)
            own.link(v.tensor_tensor(krot[:], krot[:], krot2[:], ALU.add))
            v.tensor_tensor(krot[:], krot[:], r_a[:], ALU.mult).then_inc(kr_new, 1)
            split(N_Q + 1)
            stat_diag(NORM_KV, KVRANK)
            scaled(T_IN + 4, cq[:, 0, :], r_a).then_inc(gemm_evac, 1)
            stat_row(NORM_KV, r_b)

            dve.wait_ge(gemm_evac, T_IN + 2)
            for m in range(2):
                v.tensor_tensor(ckv[:, m, :], ckv[:, m, :], r_b[:], ALU.mult).then_inc(c_norm, 1)
            for m in range(2):
                dve.wait_ge(c_hi, m + 1)
                low(ckvl[:, m, :], ckv[:, m, :], ckvh[:, m, :], pcol[:, G_KV + m:G_KV + m + 1]).then_inc(c_ready, 1)
            scaled(T_IN + 5, cq[:, 1, :], r_a).then_inc(gemm_evac, 1)
            split(N_VA)
            scaled(T_IN + 6, cq[:, 2, :], r_a).then_inc(gemm_evac, 1)
            scaled(T_IN + 7, cq[:, 3, :], r_a).then_inc(gemm_evac, 1)
            stat_diag(NORM_CQ, QRANK)

            def v_evac(t):
                half, tt = t // TT, t % TT
                dve.wait_ge(gemm_done, T_VA + t + 1)
                v.tensor_copy(v_all[:, 4 * half:4 * half + 4, P * tt:P * tt + P],
                              bank((T_VA + t) % RING).rearrange("p (m n) -> p m n", n=P)).then_inc(gemm_evac, 1)

            for t in range(4):
                v_evac(t)
            stat_row(NORM_CQ, r_b)
            for m in range(4):
                v.tensor_tensor(cq[:, m, :], cq[:, m, :], r_b[:], ALU.mult).then_inc(c_norm, 1)
            for m in range(4):
                v_evac(4 + m)
                dve.wait_ge(c_hi, 2 + m + 1)
                low(cql[:, m, :], cq[:, m, :], cqh[:, m, :], pcol[:, G_Q + m:G_Q + m + 1]).then_inc(c_ready, 1)
            for e in range(2):
                dve.wait_ge(kr_hi, e + 1)
                low(kl[e][64:128, :], krot[64:128, :], kh[e][64:128, :]).then_inc(kr_lo, 1)

            def k_low(e, i, lead):
                dve.wait_ge(k_hi, i * 2 + (2 * lead + e + 1))
                low(kl[e][0:64, :], ps[64 * e:64 * e + 64, B_KV, :], kh[e][0:64, :]).then_inc(k_lo, 1)

            def q_table(i, lead):
                dve.wait_ge(q_mm, i * 2 + (lead + 1))
                if lead:
                    dve.wait_ge(q_lo, i * 2 + lead)
                v.tensor_tensor(qtmp[:], bank(B_Q), tab[:], ALU.mult).then_inc(q_tab, 1)

            def q_low(i, lead):
                dve.wait_ge(q_hi, i * 2 + (lead + 1))
                low(ql[lead % 2], qtmp[:], qh[lead % 2]).then_inc(q_lo, 1)

            def row_max(i, lead, b):
                dve.wait_ge(s_mm, i * 8 + (4 * lead + b + 1))
                v.tensor_reduce(nmax[:, b:b + 1], ps[:, B_S + b % 2, 0:P * (b + 1)], op=ALU.max, axis=AX.X,
                                negate=True).then_inc(s_max, 1)

            def normalise(i, lead, b):
                dve.wait_ge(s_exp, i * 8 + (4 * lead + b + 1))
                own.link(v.reciprocal(rinv[:, b:b + 1], rsum[:, b:b + 1]))
                w = P * (b + 1)
                v.tensor_scalar(prob[:, b % 2, 0:w], prob[:, b % 2, 0:w], rinv[:, b:b + 1], None, ALU.mult) \
                    .then_inc(p_norm, 1)

            def pt_low(i, lead, b):
                dve.wait_ge(t_hi, i * 8 + (4 * lead + b + 1))
                part, e = slice(P * b, P * b + P), lead % 2
                low(ptl[e][:, 0:b + 1, part], ps[:, B_PT + b % 2, 0:P * (b + 1)].rearrange("p (j q) -> p j q", q=P),
                    pth[e][:, 0:b + 1, part]).then_inc(t_lo, 1)

            def o_low(i, lead):
                e, pair = lead % 2, i + lead // 2
                dve.wait_ge(o_hi, i * 2 + (lead + 1))
                rows = slice(64 * e, 64 * e + 64)
                low(ul[rows, ds(pair, 1), :].rearrange("p a s -> p (a s)"), ps[rows, B_PV + e, :],
                    uh[rows, ds(pair, 1), :].rearrange("p a s -> p (a s)")).then_inc(o_lo, 1)

            for e in range(2):
                k_low(e, 0, 0)
            q_table(0, 0)
            q_low(0, 0)
            row_max(0, 0, 0)
            row_max(0, 0, 1)
            normalise(0, 0, 0)

            def attention(i, first=False, last=False):
                normalise(i, 0, 1)
                row_max(i, 0, 2)
                pt_low(i, 0, 0)
                if last:
                    dve.wait_ge(wlo_ready, N_WO)
                    split(N_WO)
                normalise(i, 0, 2)
                q_table(i, 1)
                row_max(i, 0, 3)
                pt_low(i, 0, 1)
                q_low(i, 1)
                normalise(i, 0, 3)
                row_max(i, 1, 0)
                pt_low(i, 0, 2)
                if not first:
                    o_low(i, -1)
                normalise(i, 1, 0)
                row_max(i, 1, 1)
                pt_low(i, 0, 3)
                dve.wait_ge(v_hi, i + 1)
                low(vl[:, :, :], v_slot(i), vh[:, :, :]).then_inc(v_lo, 1)
                if not last:
                    k_low(0, i, 1)
                normalise(i, 1, 1)
                row_max(i, 1, 2)
                pt_low(i, 1, 0)
                if not last:
                    q_table(i, 2)
                normalise(i, 1, 2)
                row_max(i, 1, 3)
                if not last:
                    q_low(i, 2)
                pt_low(i, 1, 1)
                if last:
                    split(N_WO + 1)
                normalise(i, 1, 3)
                if not last:
                    k_low(1, i, 1)
                    row_max(i, 2, 0)
                pt_low(i, 1, 2)
                if not last:
                    normalise(i, 2, 0)
                    row_max(i, 2, 1)
                pt_low(i, 1, 3)
                o_low(i, 0)

            attention(0, first=True)
            with dve.Fori(1, PAIRS - 1) as i:
                own.enter(i, 1, 8)
                attention(i)
                own.leave(1, PAIRS - 1)
            attention(PAIRS - 1, last=True)
            o_low(PAIRS, -1)

            def onto_residual(t, m, i=0, per=0):
                dve.wait_ge(gemm_done, i * per + (t + 1))
                return v.tensor_tensor(h[:, m, :], bank(t % RING), h[:, m, :], ALU.add)

            def residual_stage(n0, t0, group, gain):
                for j in range(4):
                    if j:
                        split(n0 + j + 1)
                    for m in (2 * j, 2 * j + 1):
                        onto_residual(t0 + m, m).then_inc(gemm_evac, 1)
                        if m:
                            x_low(group, gain, m - 1)
                x_low(group, gain, KD - 1)

            residual_stage(N_WO, T_WO, 1, G_MLP)

            def mlp_quarter(layer, i, q, first=False, last=False):
                n0, t0 = N_MLP[layer] + 8 * q, T_MLP[layer] + 16 * q
                u0 = 8 * QUARTERS * layer + 8 * q
                for j in range(4):
                    split(n0 + j + 1, "full", i, 8)
                    if first and j == 0:
                        norm = NORM_MLP0 if layer == 0 else NORM_MLP1
                        stat_diag(norm, D)
                        stat_row(norm, r_a)
                    for m in (2 * j, 2 * j + 1):
                        dve.wait_ge(gemm_done, i * 16 + (t0 + m + 1))
                        v.tensor_tensor(diag[:, m % 2, :], bank((t0 + m) % RING), r_a[:], ALU.mult) \
                            .then_inc(gemm_evac, 1)
                        dve.wait_ge(gemm_evac, i * 16 + (t0 + m + 1))
                        if u0 or m > 1 or not first:
                            dve.wait_ge(u_ready, i * 8 + (u0 + max(m - 1, 0)))
                        v.scalar_tensor_tensor(out=sq[:, m % 2, :], in0=diag[:, m % 2, :], scalar=0.0,
                                               in1=diag[:, m % 2, :], op0=ALU.max, op1=ALU.mult) \
                            .then_inc(a_new, 1)
                for j in range(4):
                    if not last:
                        split(n0 + j + 5, "full", i, 8)
                    elif j < 3:
                        split(n0 + j + 5)
                    elif layer == 0:
                        split(n0 + 8, "gate")
                    for m in (2 * j, 2 * j + 1):
                        onto_residual(t0 + 8 + m, m, i, 16).then_inc(gemm_evac, 1)
                        if last and layer == 0 and m:
                            x_low(2, G_MIX + 8, m - 1)
                if last and layer == 0:
                    x_low(2, G_MIX + 8, KD - 1)

            def mlp(layer):
                mlp_quarter(layer, 0, 0, first=True)
                with dve.Fori(1, QUARTERS - 1) as i:
                    mlp_quarter(layer, i, 0)
                mlp_quarter(layer, 0, QUARTERS - 1, last=True)

            mlp(0)

            split(N_QK)
            stat_diag(NORM_MIX1, D)
            stat_row(NORM_MIX1, r_a)
            v.memset(zrow[:], 0.0)
            v.memset(cpad[:, 0:CONV - 1], 0.0)
            dve.wait_ge(gemm_done, T_GATE + 1)
            b = bank(T_GATE % RING)
            own.link(v.tensor_tensor(gi[:], b[0:MH, :], r_a[0:MH, :], ALU.mult))
            v.tensor_tensor(gf[:], b[32:32 + MH, :], r_a[32:32 + MH, :], ALU.mult).then_inc(gemm_evac, 1)

            def gates():
                dve.wait_ge(g_ln, 1)
                own.link(v.tensor_tensor_scan(Fc[:], gf[:], zrow[:], 0.0, ALU.add, ALU.add))
                own.link(v.scalar_tensor_tensor(out=Gc[:], in0=gi[:], scalar=CAP, in1=Fc[:], op0=ALU.mult,
                                                op1=ALU.add))
                own.link(v.tensor_tensor_scan(Mc[:], Gc[:], Gc[:], 0.0, ALU.max, ALU.max))
                v.tensor_tensor(en[:], Mc[:], Fc[:], ALU.subtract).then_inc(g_m, 1)

            def gate_columns():
                dve.wait_ge(g_t, 1)
                v.tensor_copy(gcol[:], ps[:, 5, 0:32]).then_inc(gcol_ready, 1)
                v.tensor_copy(encol[:, :].rearrange("p (e j) -> p e j", e=MH),
                              ps[:, 5, 32:64].rearrange("p (j e) -> p e j", e=MH)).then_inc(gcol_ready, 1)

            def conv(m):
                if m:
                    dve.wait_ge(y_new, m)
                scaled(T_QK + m, cpad[:, CONV - 1:CONV - 1 + S], r_a).then_inc(gemm_evac, 1)
                if m >= 2:
                    dve.wait_ge(y_hi, m - 1)
                dve.wait_ge(gemm_evac, T_QK + m + 1)
                w = [pcol[:, CONV_W + 8 * c + m:CONV_W + 8 * c + m + 1] for c in range(CONV)]
                y = yc[:, m % 2, :]
                own.link(v.tensor_scalar(y, cpad[:, 0:S], w[0], pcol[:, CONV_B + m:CONV_B + m + 1],
                                         ALU.mult, ALU.add))
                for c in range(1, CONV):
                    ins = v.scalar_tensor_tensor(out=y, in0=cpad[:, c:c + S], scalar=w[c], in1=y,
                                                 op0=ALU.mult, op1=ALU.add)
                    if c < CONV - 1:
                        own.link(ins)
                ins.then_inc(y_new, 1)

            for j in range(4):
                split(N_QK + j + 1)
                conv(2 * j)
                if j == 0:
                    gates()
                if j == 2:
                    gate_columns()
                conv(2 * j + 1)
            for j in range(4):
                split(N_V + j + 1)
                for i in range(2):
                    t = T_V + 2 * j + i
                    dve.wait_ge(gemm_done, t + 1)
                    for half in range(2):
                        tt = 2 * i + half
                        last = v.tensor_scalar(v_tok[:, tt, 256 * j:256 * j + 256],
                                               ps[:, t % RING, 256 * half:256 * half + 256],
                                               rcol[:, tt:tt + 1], None, ALU.mult)
                    last.then_inc(gemm_evac, 1)
            for j in range(4):
                split(N_O + j + 1)
                for m in (2 * j, 2 * j + 1):
                    if m < 2:
                        dve.wait_ge(y_hi, 8)
                    else:
                        dve.wait_ge(sig_new, m - 1)
                    scaled(T_O + m, otmp[:, m % 2, :], r_a).then_inc(gemm_evac, 1)

            def masked(i, lead):
                e, pair = lead % 2, i + lead // 2
                dve.wait_ge(mb_in[e], pair * 16 + 16)
                v.tensor_tensor(md[:, e, :].rearrange("p (j q) -> p j q", q=P),
                                mb[:, e, :].rearrange("p (j q) -> p j q", q=P),
                                mask_w[:].unsqueeze(1).broadcast_to([P, TT, P]), ALU.add).then_inc(md_ready, 1)

            def weighted(i, lead, j):
                z, n = 4 * lead + j, LEN[j]
                dve.wait_ge(st_mm, i * 8 + (z + 1))
                dve.wait_ge(w_exp, i * 8 + (z + 1))
                if z >= 2:
                    dve.wait_ge(sw_lo, i * 8 + (z - 1))
                v.scalar_tensor_tensor(out=sw[:, z % 2, 0:n], in0=ps[:, B_ST + z % 2, 0:n],
                                       scalar=float(64 ** -0.5), in1=wt[:, z % 2, 0:n],
                                       op0=ALU.mult, op1=ALU.mult).then_inc(sw_mul, 1)

            def v_low(i, lead):
                e, pair = lead % 2, i + lead // 2
                dve.wait_ge(mv_hi, i * 2 + (lead + 1))
                part = mvh[:, :, P * e:P * e + P]
                low(mvl[:, :, P * e:P * e + P], v_tok[:, :, ds(pair * 256 + P * e, P)], part).then_inc(mv_lo, 1)

            def head_norm(i, lead):
                e, pair = lead % 2, i + lead // 2
                c = slice(4 * e, 4 * e + 4)
                dve.wait_ge(ms_mm, i * 2 + (lead + 1))
                v.tensor_copy(stat[:, e, :], ps[:, B_STAT, 0:12]).then_inc(stat_read, 1)
                dve.wait_ge(stat_read, i * 2 + (lead + 1))
                den = stat[:, e, 0:8].rearrange("p (a n) -> p a n", n=2)[:, :, 0]
                own.link(v.scalar_tensor_tensor(out=dd[:, c], in0=den, scalar=-1.0, in1=den,
                                                op0=ALU.mult, op1=ALU.max))
                own.link(v.tensor_tensor(dd[:, c], dd[:, c], encol[:, ds(pair * 8 + 4 * e, 4)], ALU.max))
                own.link(v.scalar_tensor_tensor(out=dd[:, c], in0=dd[:, c], scalar=EPS, in1=dd[:, c],
                                                op0=ALU.mult, op1=ALU.mult))
                v.scalar_tensor_tensor(out=var2[:, c], in0=stat[:, e, 8:12], scalar=1.0 / P, in1=dd[:, c],
                                       op0=ALU.mult, op1=ALU.add).then_inc(var2_ready, 1)
                dve.wait_ge(rc2_ready, i * 2 + (lead + 1))
                v.tensor_tensor(diag[:, e, :].rearrange("p (t q) -> p t q", q=P),
                                ident[:].unsqueeze(1).broadcast_to([P, TT, P]),
                                rc2[:, c].unsqueeze(2).broadcast_to([P, TT, P]), ALU.mult).then_inc(diag2_ready, 1)

            def gated(i, lead):
                e, pair = lead % 2, i + lead // 2
                dve.wait_ge(bc2_mm, i * 2 + (lead + 1))
                v.tensor_tensor(rb[:, e, :], bank(B_BCH),
                                sg[:, ds(pair * 2 + e, 1), :].rearrange("p a s -> p (a s)"), ALU.mult) \
                    .then_inc(rb_ready, 1)
                dve.wait_ge(rb_ready, i * 2 + (lead + 1))
                v.tensor_tensor(rb[:, e, :], rb[:, e, :], bank(B_NUM[e]), ALU.mult).then_inc(hs_ready, 1)

            def gated_low(i, lead):
                e, pair = lead % 2, i + lead // 2
                dve.wait_ge(g_hi, i * 2 + (lead + 1))
                low(ul[:, ds(pair + 4 * e, 1), :].rearrange("p a s -> p (a s)"), rb[:, e, :],
                    uh[:, ds(pair + 4 * e, 1), :].rearrange("p a s -> p (a s)")).then_inc(g_ready, 1)

            def head_step(i, lead, first=False, last=False):
                if not last:
                    masked(i, lead + 1)
                    weighted(i, lead + 1, 0)
                    weighted(i, lead + 1, 1)
                if not first:
                    head_norm(i, lead - 1)
                if not last:
                    v_low(i, lead + 1)
                if not first:
                    gated(i, lead - 1)
                if not last:
                    weighted(i, lead + 1, 2)
                    weighted(i, lead + 1, 3)
                if not first:
                    gated_low(i, lead - 1)

            masked(0, 0)
            weighted(0, 0, 0)
            weighted(0, 0, 1)
            v_low(0, 0)
            weighted(0, 0, 2)
            weighted(0, 0, 3)
            dve.wait_ge(sg_ready, MH)
            head_step(0, 0, first=True)
            with dve.Fori(0, MPAIRS - 1) as i:
                own.enter(i, 0, 6)
                head_step(i, 1)
                head_step(i, 2)
                own.leave(0, MPAIRS - 1)
            split(N_WO2 + 1)
            head_step(MPAIRS - 1, 1, last=True)
            head_norm(MPAIRS - 1, 1)
            gated(MPAIRS - 1, 1)
            gated_low(MPAIRS - 1, 1)
            residual_stage(N_WO2, T_WO2, 3, G_MLP + 8)
            mlp(1)
            dve.wait_ge(stat_col, NORM_FIN + 1)
            v.tensor_scalar(var[:], ps[:, B_COL, 0:4], 1.0 / D, EPS, ALU.mult, ALU.add).then_inc(var_ready, 1)
            dve.wait_ge(rcol_ready, NORM_FIN + 1)
            dve.wait_ge(out_evac, KD)
            for t in range(TT):
                v.tensor_scalar(o_tok[:, t, :], o_tok[:, t, :], rcol[:, t:t + 1], None, ALU.mult) \
                    .then_inc(out_ready, 1)

        @block.tensor
        def _(pe):
            mm, tr = nc.tensor.matmul, nc.tensor.transpose

            def product(o, pairs, wait=None):
                for k, ((ah, al), (bh, bl)) in enumerate(pairs):
                    if wait is not None:
                        wait(k)
                    first, last = k == 0, k == len(pairs) - 1
                    mm(o, ah, bl, start=first, stop=False)
                    mm(o, ah, bh, start=False, stop=False)
                    ins = mm(o, al, bh, start=False, stop=last)
                return ins

            def free_bank(t, i=0, per=0):
                if t >= RING:
                    pe.wait_ge(gemm_evac, i * per + (t - RING + 1))

            def strip_ready(n, i=0, per=0):
                pe.wait_ge(wlo_ready, i * per + (n + 1))

            def tile(t, n, c, rh, rl, wait=None, i=0, per=0, kinds=full, width=P, order=None):
                free_bank(t, i, per)
                s = n % 2
                ks = range(8)
                o = ps[0:width, t % RING, :]
                order = order or (lambda k: k)
                return product(o, [((full(whi[s])[:, k, c:c + width], full(wlo[s])[:, k, c:c + width]),
                                    (rh[:, order(k), :], rl[:, order(k), :])) for k in ks], wait) \
                    .then_inc(gemm_done, 1)

            def stat_sum(norm):
                pe.wait_ge(acc_add, adds_before(norm + 1))
                for t in range(TT):
                    last = mm(ps[:, B_COL, t:t + 1], acc[:, P * t:P * t + P], ones[:, 0:1], start=True, stop=True)
                last.then_inc(stat_col, 1)

            def stat_spread(norm):
                pe.wait_ge(diag_ready, norm + 1)
                if norm:
                    pe.wait_ge(rbc_ready, norm)
                mm(bank(B_BC), ones[:], diag[:, 0, :], start=True, stop=True).then_inc(stat_bc, 1)

            pe.wait_ge(consts, 1)
            pe.wait_ge(par_in, 128)
            tr(ps[:, B_COL, 0:PCOLS], prow[:, :], ident[0:PCOLS, 0:PCOLS]).then_inc(par_t, 1)
            for m in range(KD):
                pe.wait_ge(x_in[m // 4], 16)
                free_bank(m)
                for t in range(TT):
                    last = tr(ps[:, m % RING, P * t:P * t + P], x_tok[:, t, P * m:P * m + P], ident[:])
                last.then_inc(gemm_done, 1)

            def x_wait(group):
                return lambda k: pe.wait_ge(x_ready, 8 * group + k + 1)

            strip_ready(N_KV)
            tile(T_IN, N_KV, 0, xh, xl, x_wait(0))
            stat_sum(NORM_MIX0)
            tile(T_IN + 1, N_KV, P, xh, xl)
            stat_spread(NORM_MIX0)
            strip_ready(N_KR)
            for which in range(2):
                t = T_IN + 2 + which
                free_bank(t)
                s = N_KR % 2
                wh = kr_split(whi[s], which).rearrange("p k r n -> p k (r n)")
                wl = kr_split(wlo[s], which).rearrange("p k r n -> p k (r n)")
                product(bank(t % RING), [((wh[:, k, :], wl[:, k, :]), (xh[:, k, :], xl[:, k, :]))
                                         for k in range(8)]).then_inc(gemm_done, 1)
            strip_ready(N_Q)
            tile(T_IN + 4, N_Q, 0, xh, xl)
            stat_sum(NORM_KV)
            tile(T_IN + 5, N_Q, P, xh, xl)
            stat_spread(NORM_KV)
            strip_ready(N_Q + 1)
            tile(T_IN + 6, N_Q + 1, 0, xh, xl)
            tile(T_IN + 7, N_Q + 1, P, xh, xl)
            stat_sum(NORM_CQ)

            def k_product(s, wait=None):
                product(bank(B_KV), [((pkv(whi[s])[:, k, :], pkv(wlo[s])[:, k, :]), (ckvh[:, k, :], ckvl[:, k, :]))
                                     for k in range(2)], wait).then_inc(k_mm, 1)

            def q_half(half, s, wait=None):
                for k in (0, 1) if half == 0 else (2, 3):
                    if wait is not None:
                        wait(k)
                    ah, al, bh, bl = pq(whi[s])[:, k, :], pq(wlo[s])[:, k, :], cqh[:, k, :], cql[:, k, :]
                    mm(bank(B_Q), ah, bl, start=(k == 0), stop=False)
                    mm(bank(B_Q), ah, bh, start=False, stop=False)
                    last = mm(bank(B_Q), al, bh, start=False, stop=(k == 3))
                if half:
                    last.then_inc(q_mm, 1)

            def scores(i, lead, b):
                e = lead % 2
                s = 4 * lead + b
                if s >= 2:
                    pe.wait_ge(s_exp, i * 8 + (s - 1))
                if b == 0:
                    pe.wait_ge(q_lo, i * 2 + (lead + 1))
                    pe.wait_ge(k_lo, i * 2 + (lead + 1))
                w = P * (b + 1)
                o = ps[:, B_S + b % 2, 0:w]
                part = slice(P * b, P * b + P)
                mm(o, qh[e][:, part], kl[e][:, 0:w], start=True, stop=False)
                mm(o, qh[e][:, part], kh[e][:, 0:w], start=False, stop=False)
                mm(o, ql[e][:, part], kh[e][:, 0:w], start=False, stop=False)
                mm(ps[:, B_S + b % 2, P * b:w], identr[:], maskr[:], start=False, stop=True).then_inc(s_mm, 1)

            def turn_p(i, lead, b, first=False):
                s = 4 * lead + b
                pe.wait_ge(p_norm, i * 8 + (s + 1))
                if s >= 2 or not first:
                    pe.wait_ge(t_lo, i * 8 + (s - 1))
                for j in range(b + 1):
                    last = tr(ps[:, B_PT + b % 2, P * j:P * j + P], prob[:, b % 2, P * j:P * j + P], ident[:])
                last.then_inc(t_mm, 1)

            def weigh(i, lead, js=range(TT)):
                e = lead % 2
                if js[0] == 0:
                    pe.wait_ge(t_lo, i * 8 + (4 * lead + 4))
                    pe.wait_ge(v_lo, i + (lead // 2 + 1))
                for j in js:
                    o = ps[:, B_PV + e, P * j:S]
                    mm(o, vh[:, j, :], ptl[e][:, j, P * j:S], start=(j == 0), stop=False)
                    mm(o, vh[:, j, :], pth[e][:, j, P * j:S], start=False, stop=False)
                    last = mm(o, vl[:, j, :], pth[e][:, j, P * j:S], start=False, stop=(j == TT - 1))
                if js[-1] == TT - 1:
                    last.then_inc(pv_mm, 1)

            strip_ready(N_VA)
            pe.wait_ge(c_ready, 2)
            wv = [w[N_VA % 2][:, :].rearrange("p (k n) -> p k n", k=2) for w in (whi, wlo)]
            for t in range(8):
                half, part = t // TT, slice(P * (t % TT), P * (t % TT) + P)
                cols = slice(512 * half, 512 * half + 512)
                free_bank(T_VA + t)
                product(bank((T_VA + t) % RING), [((ckvh[:, k, part], ckvl[:, k, part]),
                                                   (wv[0][:, k, cols], wv[1][:, k, cols]))
                                                  for k in range(2)]).then_inc(gemm_done, 1)
                if t == 2:
                    stat_spread(NORM_CQ)
            pe.wait_ge(gemm_evac, T_VA + 8)
            strip_ready(N_PAIR)
            k_product(N_PAIR % 2)
            for half in range(2):
                q_half(half, N_PAIR % 2, lambda k: pe.wait_ge(c_ready, 2 + k + 1))
            pe.wait_ge(kr_lo, 2)
            scores(0, 0, 0)
            scores(0, 0, 1)
            strip_ready(N_PAIR + 1)
            pe.wait_ge(q_tab, 1)
            q_half(0, (N_PAIR + 1) % 2)

            def attention(i, first=False, last=False):
                turn_p(i, 0, 0, first)
                scores(i, 0, 2)
                q_half(1, (N_PAIR + 1) % 2)
                turn_p(i, 0, 1, first)
                scores(i, 0, 3)
                if not first:
                    weigh(i, -1)
                turn_p(i, 0, 2)
                scores(i, 1, 0)
                if not last:
                    strip_ready(N_PAIR + 2, i, 2)
                    pe.wait_ge(k_lo, i * 2 + 2)
                    k_product(N_PAIR % 2)
                else:
                    out_products(range(0, 2))
                turn_p(i, 0, 3)
                scores(i, 1, 1)
                if not last:
                    pe.wait_ge(q_tab, i * 2 + 2)
                    q_half(0, N_PAIR % 2)
                else:
                    out_products(range(2, 4))
                turn_p(i, 1, 0)
                scores(i, 1, 2)
                if not last:
                    q_half(1, N_PAIR % 2)
                else:
                    out_products(range(4, 5))
                turn_p(i, 1, 1)
                scores(i, 1, 3)
                weigh(i, 0, range(1))
                turn_p(i, 1, 2)
                if not last:
                    scores(i, 2, 0)
                weigh(i, 0, range(1, TT))
                if last:
                    out_products(range(5, 6))
                turn_p(i, 1, 3)
                if last:
                    out_products(range(6, 7))
                if not last:
                    scores(i, 2, 1)
                    strip_ready(N_PAIR + 3, i, 2)
                    pe.wait_ge(q_tab, i * 2 + 3)
                    q_half(0, (N_PAIR + 1) % 2)

            def side_by_side(n0, t0, ks, wait, order=lambda k: k):
                s = n0 % 2
                for k in ks:
                    if k == 0:
                        strip_ready(n0)
                        for m in range(2):
                            free_bank(t0 + m)
                    wait(k)
                    bh, bl = uh[:, order(k), :], ul[:, order(k), :]
                    for m in range(2):
                        c, o = slice(P * m, P * m + P), bank((t0 + m) % RING)
                        ah, al = full(whi[s])[:, k, c], full(wlo[s])[:, k, c]
                        mm(o, ah, bl, start=(k == 0), stop=False)
                        mm(o, ah, bh, start=False, stop=False)
                        last = mm(o, al, bh, start=False, stop=(k == KD - 1))
                        if k == KD - 1:
                            last.then_inc(gemm_done, 1)

            def out_products(ks):
                side_by_side(N_WO, T_WO, ks, lambda k: pe.wait_ge(o_lo, 2 * k + 2))

            attention(0, first=True)
            with pe.Fori(1, PAIRS - 1) as i:
                attention(i)
            attention(PAIRS - 1, last=True)

            def strips(n0, t0, js, rh, rl, order=None):
                for j in js:
                    strip_ready(n0 + j)
                    for m in range(2):
                        tile(t0 + 2 * j + m, n0 + j, P * m, rh, rl, order=order)

            weigh(PAIRS, -1)
            out_products(range(KD - 1, KD))
            strips(N_WO, T_WO, range(1, 4), uh, ul)

            def mlp_quarter(layer, i, q, first=False, last=False):
                n0, t0 = N_MLP[layer] + 8 * q, T_MLP[layer] + 16 * q
                u0 = 8 * QUARTERS * layer + 8 * q
                norm = NORM_MLP0 if layer == 0 else NORM_MLP1
                for j in range(4):
                    strip_ready(n0 + j, i, 8)
                    for m in range(2):
                        tile(t0 + 2 * j + m, n0 + j, P * m, xh, xl,
                             x_wait(1 + 2 * layer) if first and j + m == 0 else None, i, 16)
                        if first and j == 0:
                            (stat_sum, stat_spread)[m](norm)
                for j in range(4):
                    strip_ready(n0 + 4 + j, i, 8)
                    for m in range(2):
                        tile(t0 + 8 + 2 * j + m, n0 + 4 + j, P * m, uh, ul,
                             (lambda k: pe.wait_ge(u_ready, i * 8 + (u0 + k + 1))) if j + m == 0 else None, i, 16)
                        if last and layer == 1 and 2 * j + m:
                            turn_out(2 * j + m - 1)

            def turn_out(m):
                pe.wait_ge(hg_new, m + 1)
                if m >= 2:
                    pe.wait_ge(out_evac, m - 1)
                for t in range(TT):
                    ins = tr(ps[:, B_OUT + m % 2, P * t:P * t + P], hg[:, m % 2, P * t:P * t + P], ident[:])
                ins.then_inc(out_t, 1)

            def mlp(layer):
                mlp_quarter(layer, 0, 0, first=True)
                with pe.Fori(1, QUARTERS - 1) as i:
                    mlp_quarter(layer, i, 0)
                mlp_quarter(layer, 0, QUARTERS - 1, last=True)

            mlp(0)

            strip_ready(N_GATE)
            tile(T_GATE, N_GATE, 0, xh, xl, x_wait(2), width=32 + MH)
            stat_sum(NORM_MIX1)
            for j in range(4):
                strip_ready(N_QK + j)
                for m in range(2):
                    tile(T_QK + 2 * j + m, N_QK + j, P * m, xh, xl)
                    if j + m == 0:
                        stat_spread(NORM_MIX1)
                if j == 1:
                    pe.wait_ge(g_m, 1)
                    pe.wait_ge(g_en, 1)
                    for c, row in ((0, Gc), (32, en)):
                        for t in range(TT):
                            last = tr(ps[:, 5, c + MH * t:c + MH * t + MH], row[:, P * t:P * t + P],
                                      ident[0:MH, 0:MH])
                    last.then_inc(g_t, 1)
            for j in range(4):
                strip_ready(N_V + j)
                s = (N_V + j) % 2
                for i in range(2):
                    t = T_V + 2 * j + i
                    free_bank(t)
                    for half in range(2):
                        part = slice(P * (2 * i + half), P * (2 * i + half) + P)
                        last = product(ps[:, t % RING, 256 * half:256 * half + 256],
                                       [((xh[:, k, part], xl[:, k, part]), (full(whi[s])[:, k, :], full(wlo[s])[:, k, :]))
                                        for k in range(8)])
                    last.then_inc(gemm_done, 1)
            strips(N_O, T_O, range(4), xh, xl)

            def st_product(i, lead, js):
                e, pair = lead % 2, i + lead // 2
                for j in js:
                    z = 4 * lead + j
                    if z >= 2:
                        pe.wait_ge(sw_mul, i * 8 + (z - 1))
                    if j == 0:
                        pe.wait_ge(mk_ready, i * 2 + (lead + 1))
                    o = ps[:, B_ST + z % 2, 0:LEN[j]]
                    part = slice(P * j, P * j + P)
                    qt = [x[:, ds(pair, 1), P * j:S].rearrange("p a s -> p (a s)") for x in (uh, ul)]
                    product(o, [((mkh[:, e, part], mkl[:, e, part]), qt)]).then_inc(st_mm, 1)

            def numerator(i, lead, first=False):
                e = lead % 2
                pe.wait_ge(sw_lo, i * 8 + (4 * lead + 4))
                pe.wait_ge(mv_lo, i * 2 + (lead + 1))
                for j in range(TT):
                    o = ps[:, B_NUM[e], P * j:S]
                    part = slice(P * e, P * e + P)
                    mm(o, mvh[:, j, part], swl(e, j), start=(j == 0), stop=False)
                    mm(o, mvh[:, j, part], swh(e, j), start=False, stop=False)
                    last = mm(o, mvl[:, j, part], swh(e, j), start=False, stop=(j == TT - 1))
                if not first:
                    pe.wait_ge(stat_read, i * 2 + lead)
                for b in range(TT):
                    o = ps[:, B_STAT, 2 * b:2 * b + 2]
                    for j in range(b + 1):
                        part = slice(P * (b - j), P * (b - j) + P)
                        mm(o, swh(e, j)[:, part], onesr[:], start=(j == 0), stop=False)
                        last = mm(o, swl(e, j)[:, part], onesr[:], start=False, stop=(j == b))
                last.then_inc(num_mm, 1)

            def square_sum(i, lead):
                e = lead % 2
                pe.wait_ge(num_sq, i * 2 + (lead + 1))
                for b in range(TT):
                    last = mm(ps[:, B_STAT, 8 + b:9 + b], numsq[:, e, P * b:P * b + P], ones[:, 0:1],
                              start=True, stop=True)
                last.then_inc(ms_mm, 1)

            def norm_spread(i, lead, first=False):
                pe.wait_ge(diag2_ready, i * 2 + (lead + 1))
                if not first:
                    pe.wait_ge(rb_ready, i * 2 + lead)
                mm(bank(B_BCH), ones[:], diag[:, lead % 2, :], start=True, stop=True).then_inc(bc2_mm, 1)

            def out_products2(ks):
                side_by_side(N_WO2, T_WO2, ks, lambda k: pe.wait_ge(g_ready, k + 1), order=by_head)

            def by_head(k):
                return k // 2 + 4 * (k % 2)

            def head_step(i, lead, first=False, last=False, second=False):
                if not last:
                    st_product(i, lead + 1, (0, 1))
                if not first:
                    square_sum(i, lead - 1)
                numerator(i, lead, first)
                if last:
                    out_products2(range(0, 2))
                if not first:
                    norm_spread(i, lead - 1, second)
                if not last:
                    st_product(i, lead + 1, (2, 3))

            pe.wait_ge(y_lo, 8)
            st_product(0, 0, range(TT))
            pe.wait_ge(gemm_evac, T_WO2)
            head_step(0, 0, first=True)
            head_step(0, 1, second=True)
            head_step(0, 2)
            with pe.Fori(1, MPAIRS - 1) as i:
                head_step(i, 1)
                head_step(i, 2)
            head_step(MPAIRS - 1, 1, last=True)
            out_products2(range(2, 4))
            square_sum(MPAIRS - 1, 1)
            out_products2(range(4, 7))
            norm_spread(MPAIRS - 1, 1)
            out_products2(range(7, 8))
            pe.wait_ge(hs_ready, MH)
            strips(N_WO2, T_WO2, range(1, 4), uh, ul, by_head)
            mlp(1)
            stat_sum(NORM_FIN)
            turn_out(KD - 1)


_INS = ["x", "positions", "norm_mix_g", "norm_mlp_g", "final_g",
        "mla_w_in", "mla_q_norm_g", "mla_kv_norm_g", "mla_w_uq", "mla_w_ukv", "mla_w_o",
        "mlstm_w_in", "mlstm_conv_w", "mlstm_conv_b", "mlstm_i_b", "mlstm_f_b", "mlstm_head_norm_g", "mlstm_w_o",
        "mlp_w1", "mlp_w2"]


def kernel(**inputs):
    import numpy as _np
    import concourse.bacc as _bacc
    from concourse import mybir as _mybir
    from concourse.bass_utils import run_bass_kernel_spmd as _run

    nc = _bacc.Bacc("TRN2", target_bir_lowering=False, num_devices=1)
    arrays, args = {}, {}
    for name in _INS:
        arr = _np.ascontiguousarray(inputs[name])
        arrays[f"in_{name}"] = arr
        args[name] = nc.dram_tensor(f"in_{name}", arr.shape, _mybir.dt.from_np(arr.dtype), kind="ExternalInput").ap()
    half = ROPE // 2
    lane = _np.arange(P) % ROPE
    freq = _np.float32(THETA) ** (-_np.arange(0, ROPE, 2, dtype=_np.float32) / _np.float32(ROPE))
    rope = _np.stack([freq[lane % half], _np.where(lane < half, -1.0, 1.0)], axis=1).astype(_np.float32)
    arrays["rope_const"] = rope
    args["rope_const"] = nc.dram_tensor("rope_const", rope.shape, _mybir.dt.float32, kind="ExternalInput").ap()
    out = nc.dram_tensor("out_h", (1, S, D), _mybir.dt.float32, kind="ExternalOutput").ap()
    trunk(nc, args, out)
    r = _run(nc, [arrays], core_ids=[0])
    return r.results[0]["out_h"]
```

```python
import numpy as np
import concourse.bass as bass
from concourse import mybir
from contextlib import ExitStack

F32 = mybir.dt.float32
F32R = mybir.dt.float32r
I32 = mybir.dt.int32
ALU = mybir.AluOpType
ACT = mybir.ActivationFunctionType
AX = mybir.AxisListType
ds = bass.ds

P = 128
S = 512
D = 1024
KD = D // P
TT = S // P
QRANK, KVRANK, NOPE, ROPE, VD = 512, 256, 64, 32, 64
QK = NOPE + ROPE
HEADS = 16
PAIRS = HEADS // 2
MH = 8
MPAIRS = MH // 2
CONV = 4
HID = 4096
QUARTERS = HID // D
CAP = 15.0
EPS = 1e-6
THETA = 10000.0
SCALE = QK ** -0.5
NEG = -1e30
MAGIC = 1.5 * 2.0 ** 23
TWO_PI_1 = 6.28125
TWO_PI_2 = float(np.float32(np.floor((2 * np.pi - 6.28125) * 2 ** 21) / 2 ** 21))
TWO_PI_3 = float(np.float32(2 * np.pi - 6.28125 - TWO_PI_2))
PI_IN = 3.1415925

G_MIX, G_MLP, G_FIN = 0, 16, 32
G_Q, G_KV = 40, 44
CONV_W, CONV_B, G_HEAD = 46, 78, 86
PCOLS = 94

N_KV, N_KR, N_Q = 0, 1, 2
N_VA = 4
N_PAIR = 5
N_WO = N_PAIR + 2 * PAIRS
N_MLP = [N_WO + 4, 0]
N_GATE = N_MLP[0] + 8 * QUARTERS
N_QK, N_V, N_O, N_WO2 = N_GATE + 1, N_GATE + 5, N_GATE + 9, N_GATE + 13
N_MLP[1] = N_GATE + 17

T_IN = KD
T_VA = T_IN + 8
T_WO = T_VA + 8
T_MLP = [T_WO + 8, 0]
T_GATE = T_MLP[0] + 16 * QUARTERS
T_QK, T_V, T_O, T_WO2 = T_GATE + 1, T_GATE + 9, T_GATE + 17, T_GATE + 25
T_MLP[1] = T_GATE + 33
RING = 4
B_Q, B_KV, B_S, B_PT, B_PV = 0, 1, 2, 4, 6
B_ST, B_NUM, B_BCH, B_DEN, B_STAT = 4, (3, 7), 0, 2, 6
B_OUT, B_BC, B_COL = 4, 6, 7

NORM_MIX0, NORM_KV, NORM_CQ, NORM_MLP0, NORM_MIX1, NORM_MLP1, NORM_FIN = range(7)
NORM_TILES = [KD, KVRANK // P, QRANK // P, KD, KD, KD, KD]


def adds_before(norm):
    return sum(n - 1 for n in NORM_TILES[:norm])


def strip_over(n, gemm_done, q_mm):
    if n < N_VA:
        return gemm_done, T_IN + 2 * n + 2
    if n == N_VA:
        return gemm_done, T_VA + 8
    if n < N_WO:
        return q_mm, n - N_PAIR + 1
    if n < N_GATE:
        return gemm_done, T_WO + 2 * (n - N_WO) + 2
    return gemm_done, T_GATE + 1 + 2 * (n - N_GATE)


def raw_count(n):
    return sum(48 if m in range(N_PAIR, N_WO, 2) else 32 if m == N_VA else 16 for m in range(n % 2, n + 1, 2))


def trunk(nc, a, out):
    ctx = ExitStack()
    with ctx:
        ctx.enter_context(nc.allow_non_contiguous_dma(reason="small parameters"))

        def sb(name, shape, dt=F32):
            return ctx.enter_context(nc.sbuf_tensor(name, shape, dt))

        def sem(name):
            return ctx.enter_context(nc.semaphore(name))

        h = sb("h", [P, KD, S])
        raw = [sb(f"raw{s}", [P, 2048]) for s in range(2)]
        whi = [sb(f"whi{s}", [P, 2048], F32R) for s in range(2)]
        wlo = [sb(f"wlo{s}", [P, 2048], F32R) for s in range(2)]
        xh = sb("xh", [P, KD, S], F32R)
        xl = sb("xl", [P, KD, S], F32R)
        uh_at = (nc.sbuf_base + 31) // 32 * 32
        uh = sb("uh", [P, KD, S], F32R)
        ul = sb("ul", [P, KD, S], F32R)
        ident = sb("ident", [P, P])
        ones = sb("ones", [P, P])
        mask_s = sb("mask_s", [P, P])
        mask_w = sb("mask_w", [P, P])
        identr = sb("identr", [P, P], F32R)
        onesr = sb("onesr", [P, 2], F32R)
        maskr = sb("maskr", [P, P], F32R)
        mhalf = sb("mhalf", [P, 8])
        prow = sb("prow", [PCOLS, P])
        pcol = sb("pcol", [P, PCOLS])
        acc = sb("acc", [P, S])
        sq = sb("sq", [P, 2, S])
        r_a = sb("r_a", [P, S])
        r_b = sb("r_b", [P, S])
        diag = sb("diag", [P, 2, S])
        var = sb("var", [P, 4])
        rcol = sb("rcol", [P, 4])
        rope_c = sb("rope_c", [P, 2])
        gate_b = sb("gate_b", [MH, 4])
        nmax = sb("nmax", [P, 4])
        rsum = sb("rsum", [P, 4])
        rinv = sb("rinv", [P, 4])
        gcol = sb("gcol", [P, TT * MH])
        encol = sb("encol", [P, MH * TT])
        stat = sb("stat", [P, 2, 8])
        den_row = acc[0:1, :]
        dd = sb("dd", [P, 8])
        var2 = sb("var2", [P, 8])
        rc2 = sb("rc2", [P, 8])
        top = nc.sbuf_base
        arena_bytes = 60 * 1024
        sb("arena", [P, arena_bytes // 4])
        top = (top + 31) // 32 * 32

        class Arena:
            def __init__(self, at=0):
                self.at = at

            def __call__(self, name, shape, dt=F32):
                size = 4 * int(np.prod(shape[1:]))
                t = nc.alloc_sbuf_tensor_at(name, shape, dt, offset=top + self.at)
                self.at += (size + 31) // 32 * 32
                assert self.at <= arena_bytes, (name, self.at)
                return t

        A = Arena()
        x_tok = Arena(0)("x_tok", [P, TT, D])
        cq = A("cq", [P, 4, S])
        ckv = A("ckv", [P, 2, S])
        krot = A("krot", [P, S])
        krot2 = A("krot2", [P, S])
        cqh = A("cqh", [P, 4, S], F32R)
        cql = A("cql", [P, 4, S], F32R)
        ckvh = A("ckvh", [P, 2, S], F32R)
        ckvl = A("ckvl", [P, 2, S], F32R)
        vh = A("vh", [P, TT, P], F32R)
        vl = A("vl", [P, TT, P], F32R)
        prob = A("prob", [P, 2, S])
        cos = A("cos", [P, S])
        sin = A("sin", [P, S])
        tab = A("tab", [P, S])
        qtmp = A("qtmp", [P, S])
        B = Arena(16 * 1024)
        pos_i = B("pos_i", [P, S], I32)
        ang = B("ang", [P, S])
        turn = B("turn", [P, S])
        pt_b = [Arena(8192 * part)(f"pt_b{part}", [P, TT, S], F32R) for part in range(2)]
        pth = [xh[:, 0:TT, :], pt_b[0][:, :, :]]
        ptl = [xl[:, 0:TT, :], pt_b[1][:, :, :]]
        kh = [xh[:, 4 + e, :] for e in range(2)]
        kl = [xl[:, 4 + e, :] for e in range(2)]
        qh = [xh[:, 6 + e, :] for e in range(2)]
        ql = [xl[:, 6 + e, :] for e in range(2)]

        v_all = nc.alloc_sbuf_tensor_at("v_all", [P, PAIRS, S], F32, offset=uh_at)

        def v_slot(i):
            return v_all[:, ds(i, 1), :].rearrange("p a s -> p (a s)").rearrange("p (t n) -> p t n", t=TT)

        C = Arena()
        v_tok = C("v_tok", [P, TT, D])
        sg = C("sg", [P, MH, S])
        base = C.at
        mb = C("mb", [P, 2, S])
        md = C("md", [P, 2, S])
        wt = C("wt", [P, 2, S])
        sw = C("sw", [P, 2, S])
        rb = C("rb", [P, 2, S])
        mkh = C("mkh", [P, 2, S], F32R)
        mkl = C("mkl", [P, 2, S], F32R)
        numsq = rb
        G = Arena(base)
        gi = G("gi", [MH, S])
        gf = G("gf", [MH, S])
        Fc = G("Fc", [MH, S])
        Gc = G("Gc", [MH, S])
        Mc = G("Mc", [MH, S])
        en = G("en", [MH, S])
        zrow = G("zrow", [MH, S])
        E = Arena(base + 16 * 1024)
        yc = E("yc", [P, 2, S])
        cpad = E("cpad", [P, S + CONV - 1])
        ys = E("ys", [P, 2, S])
        otmp = yc

        def flat(t):
            return t[:, :, :].rearrange("p k s -> p (k s)")

        TRI = [0, 512, 896, 1152]
        LEN = [512, 384, 256, 128]

        def swh(e, j):
            return flat(xh)[:, 1280 * e + TRI[j]:1280 * e + TRI[j] + LEN[j]]

        def swl(e, j):
            return flat(xl)[:, 1280 * e + TRI[j]:1280 * e + TRI[j] + LEN[j]]

        mvh = flat(xh)[:, 3072:4096].rearrange("p (t n) -> p t n", t=TT)
        mvl = flat(xl)[:, 3072:4096].rearrange("p (t n) -> p t n", t=TT)

        o_tok = Arena(0)("o_tok", [P, TT, D])
        hg = Arena(16 * 1024)("hg", [P, 2, S])

        m_dram = nc.dram_tensor("m_rows", (MH, S), F32).ap()
        ps = ctx.enter_context(nc.psum_tensor("ps", [P, 8, S], F32))

        def bank(b):
            return ps[:, b, :]

        x_in = [sem(f"x_in{i}") for i in range(4)]
        par_in = sem("par_in")
        pos_in = sem("pos_in")
        raw_full = [sem(f"raw_full{s}") for s in range(2)]
        whi_ready, wlo_ready = sem("whi_ready"), sem("wlo_ready")
        consts = sem("consts")
        par_t, par_ready = sem("par_t"), sem("par_ready")
        gemm_done, gemm_evac = sem("gemm_done"), sem("gemm_evac")
        xh_new, x_ready = sem("xh_new"), sem("x_ready")
        sq_new, acc_add = sem("sq_new"), sem("acc_add")
        stat_col, var_ready, rcol_ready = sem("stat_col"), sem("var_ready"), sem("rcol_ready")
        diag_ready, stat_bc, rbc_ready = sem("diag_ready"), sem("stat_bc"), sem("rbc_ready")
        dve_own = sem("dve_own")
        act_own = sem("act_own")
        pool_own = sem("pool_own")
        ang_ready, trig_ready = sem("ang_ready"), sem("trig_ready")
        kr_new, kr_hi, kr_lo = sem("kr_new"), sem("kr_hi"), sem("kr_lo")
        c_norm, c_hi, c_ready = sem("c_norm"), sem("c_hi"), sem("c_ready")
        q_mm, q_tab, q_hi, q_lo = sem("q_mm"), sem("q_tab"), sem("q_hi"), sem("q_lo")
        k_mm, k_hi, k_lo = sem("k_mm"), sem("k_hi"), sem("k_lo")
        v_hi, v_lo = sem("v_hi"), sem("v_lo")
        s_mm, s_max, s_exp, p_norm = sem("s_mm"), sem("s_max"), sem("s_exp"), sem("p_norm")
        t_mm, t_hi, t_lo = sem("t_mm"), sem("t_hi"), sem("t_lo")
        pv_mm, o_hi, o_lo = sem("pv_mm"), sem("o_hi"), sem("o_lo")
        a_new, u_hi, u_ready = sem("a_new"), sem("u_hi"), sem("u_ready")
        y_new, y_hi, y_lo = sem("y_new"), sem("y_hi"), sem("y_lo")
        sig_new, sg_ready = sem("sig_new"), sem("sg_ready")
        g_ln, g_m, g_en = sem("g_ln"), sem("g_m"), sem("g_en")
        m_out, mb_in = sem("m_out"), [sem(f"mb_in{e}") for e in range(2)]
        g_t, gcol_ready = sem("g_t"), sem("gcol_ready")
        mk_zero, den_mm, den_read = sem("mk_zero"), sem("den_mm"), sem("den_read")
        md_ready, mk_ready, mv_hi, mv_lo = sem("md_ready"), sem("mk_ready"), sem("mv_hi"), sem("mv_lo")
        st_mm, w_exp, sw_mul, sw_hi, sw_lo = sem("st_mm"), sem("w_exp"), sem("sw_mul"), sem("sw_hi"), sem("sw_lo")
        num_mm, num_sq, ms_mm, stat_read = sem("num_mm"), sem("num_sq"), sem("ms_mm"), sem("stat_read")
        var2_ready, rc2_ready, diag2_ready = sem("var2_ready"), sem("rc2_ready"), sem("diag2_ready")
        bc2_mm, rb_ready, hs_ready = sem("bc2_mm"), sem("rb_ready"), sem("hs_ready")
        g_hi, g_ready = sem("g_hi"), sem("g_ready")
        hg_new, out_t, out_evac, out_ready, stored = (sem("hg_new"), sem("out_t"), sem("out_evac"),
                                                      sem("out_ready"), sem("stored"))

        def fixed(eng):
            eng.wait_ge(consts, 1)

        class Own:
            def __init__(self, eng, semaphore):
                self.eng, self.sem, self.n, self.loop = eng, semaphore, 0, None

            def link(self, ins):
                ins.then_inc(self.sem, 1)
                self.n += 1
                v = self.n if self.loop is None else self.loop[0] * self.loop[1] + self.n
                self.eng.wait_ge(self.sem, v)

            def enter(self, i, start, per):
                self.loop, self.at = (i, per), self.n
                self.n -= start * per

            def leave(self, start, end):
                i, per = self.loop
                assert self.n == self.at - start * per + per, (self.n - self.at + start * per, per)
                self.n, self.loop = self.at + (end - start) * per, None

        def full(t):
            return t[:, :].rearrange("p (k n) -> p k n", k=8)

        def kr_raw(t):
            return t[:, 0:8 * ROPE].rearrange("p (k n) -> p k n", k=8)

        def kr_split(t):
            return t[:, 0:1024].rearrange("p (k r n) -> p k r n", k=8, r=2)

        def gate_raw(t):
            return t[:, 0:8 * 2 * MH].rearrange("p (k n) -> p k n", k=8)

        def pq_raw(t):
            return t[:, 0:4 * QK].rearrange("p (k n) -> p k n", k=4)

        def pkv_raw(t):
            return t[:, 4 * QK:4 * QK + 256].rearrange("p (k n) -> p k n", k=2)

        def pq(t):
            return t[:, 0:512].rearrange("p (k n) -> p k n", k=4)

        def pkv(t):
            return t[:, 512:768].rearrange("p (k n) -> p k n", k=2)

        def split_parts(n_kind, s):
            r, hi, lo = raw[s], whi[s], wlo[s]
            if n_kind == "full":
                return [(r[:, :], hi[:, :], lo[:, :])]
            if n_kind in ("half 0", "half 1"):
                part = slice(0, 1024) if n_kind == "half 0" else slice(1024, 2048)
                return [(r[:, part], hi[:, part], lo[:, part])]
            if n_kind == "kr":
                half = ROPE // 2
                rr = kr_raw(r)
                parts = []
                for dst, src, n in ((0, 0, ROPE), (ROPE, half, half), (ROPE + half, 0, half)):
                    src_ap = rr[:, :, src:src + n].unsqueeze(2).broadcast_to([P, 8, 2, n])
                    parts.append((src_ap, kr_split(hi)[:, :, :, dst:dst + n], kr_split(lo)[:, :, :, dst:dst + n]))
                return parts
            if n_kind == "gate":
                return [(gate_raw(r)[:, :, MH * g:MH * g + MH], full(hi)[:, :, 32 * g:32 * g + MH],
                         full(lo)[:, :, 32 * g:32 * g + MH]) for g in range(2)]
            assert n_kind in ("kq", "q")
            half = ROPE // 2
            parts = [(pkv_raw(r), pkv(hi), pkv(lo))] if n_kind == "kq" else []
            return parts + [(pq_raw(r), pq(hi)[:, :, 0:QK], pq(lo)[:, :, 0:QK]),
                    (pq_raw(r)[:, :, NOPE + half:QK], pq(hi)[:, :, QK:QK + half], pq(lo)[:, :, QK:QK + half]),
                    (pq_raw(r)[:, :, NOPE:NOPE + half], pq(hi)[:, :, QK + half:P], pq(lo)[:, :, QK + half:P])]

        block = ctx.enter_context(nc.Block())

        @block.sync
        def _(sp):
            def slot_free(n, i=0, per=0):
                if n >= 2:
                    sp.wait_ge(wlo_ready, i * per + (n - 1))

            def load(n, src):
                slot_free(n)
                sp.dma_start(full(raw[n % 2]), src).then_inc(raw_full[n % 2], 16)

            def cols(w, c, width=256):
                return w[:, c:c + width].rearrange("(k p) n -> p k n", p=P)

            w_in = a["mla_w_in"][0]
            for i in range(4):
                sp.dma_start(x_tok[:, :, 256 * i:256 * i + 256],
                             a["x"][0, :, 256 * i:256 * i + 256].rearrange("(t p) n -> p t n", p=P)) \
                    .then_inc(x_in[i], 16)
            sp.wait_ge(par_in, 128)
            load(N_KV, cols(w_in, QRANK))
            sp.dma_start(kr_raw(raw[1]), cols(w_in, QRANK + KVRANK, ROPE)).then_inc(raw_full[1], 16)
            load(N_Q, cols(w_in, 0))
            load(N_Q + 1, cols(w_in, 256))
            slot_free(N_VA)
            for k in range(2):
                kv_heads = a["mla_w_ukv"][0, P * k:P * k + P, :].rearrange("p (h n) -> p h n", h=HEADS)
                sp.dma_start(raw[N_VA % 2][:, 1024 * k:1024 * k + 1024].rearrange("p (h n) -> p h n", h=HEADS),
                             kv_heads[:, :, NOPE:NOPE + VD]).then_inc(raw_full[N_VA % 2], 16)

            def load_head(p, n, head, with_k):
                slot_free(n, p, 2)
                s = n % 2
                sp.dma_start(pq_raw(raw[s]),
                             a["mla_w_uq"][0, :, ds(head * QK, QK)].rearrange("(k p) n -> p k n", p=P)) \
                    .then_inc(raw_full[s], 16)
                for k in range(2) if with_k else ():
                    both = a["mla_w_ukv"][0, P * k:P * k + P, ds(p * 256, 256)].rearrange("p (e n) -> p e n", e=2)
                    sp.dma_start(pkv_raw(raw[s])[:, k, :].rearrange("p (e n) -> p e n", e=2),
                                 both[:, :, 0:NOPE]).then_inc(raw_full[s], 16)

            with sp.Fori(0, PAIRS) as p:
                load_head(p, N_PAIR, p * 2, True)
                load_head(p, N_PAIR + 1, p * 2 + 1, False)
            for j in range(4):
                load(N_WO + j, cols(a["mla_w_o"][0], 256 * j))

            def load_mlp(layer):
                n0 = N_MLP[layer]
                with sp.Fori(0, QUARTERS) as q:
                    for j in range(8):
                        n = n0 + j
                        slot_free(n, q, 8)
                        if j < 4:
                            src = a["mlp_w1"][layer, :, ds(q * D + 256 * j, 256)]
                        else:
                            src = a["mlp_w2"][layer, ds(q * D, D), 256 * (j - 4):256 * (j - 3)]
                        sp.dma_start(full(raw[n % 2]), src.rearrange("(k p) n -> p k n", p=P)) \
                            .then_inc(raw_full[n % 2], 16)

            load_mlp(0)
            w_in = a["mlstm_w_in"][0]
            slot_free(N_GATE)
            sp.dma_start(gate_raw(raw[N_GATE % 2]), cols(w_in, 3 * D, 2 * MH)).then_inc(raw_full[N_GATE % 2], 16)
            for j in range(4):
                load(N_QK + j, cols(w_in, 256 * j))
            sp.wait_ge(g_m, 1)
            sp.dma_start(m_dram, Mc[:, :]).then_inc(m_out, 16)
            for j in range(4):
                load(N_V + j, cols(w_in, D + 256 * j))
            sp.wait_ge(m_out, 16)
            sp.wait_ge(gcol_ready, 2)
            for e in range(2):
                sp.dma_start(mb[:, e, :], m_dram[e:e + 1, :].broadcast_to([P, S])).then_inc(mb_in[e], 16)
            for j in range(4):
                load(N_O + j, cols(w_in, 2 * D + 256 * j))
            for j in range(2):
                load(N_WO2 + j, cols(a["mlstm_w_o"][0], 256 * j))
            with sp.Fori(1, MPAIRS) as pr:
                for e in range(2):
                    sp.wait_ge(w_exp, pr * 8 + (4 * e - 4))
                    sp.dma_start(mb[:, e, :], m_dram[ds(pr * 2 + e, 1), :].broadcast_to([P, S])) \
                        .then_inc(mb_in[e], 16)
            for j in range(2, 4):
                load(N_WO2 + j, cols(a["mlstm_w_o"][0], 256 * j))
            load_mlp(1)
            for t in range(TT):
                sp.wait_ge(out_ready, t + 1)
                sp.dma_start(out[0, P * t:P * t + P, :], o_tok[:, t, :]).then_inc(stored, 16)
            sp.wait_ge(stored, 16 * TT)

        @block.gpsimd
        def _(pool):
            own = Own(pool, pool_own)
            g = nc.gpsimd
            g.memset(ones[:], 1.0)
            g.memset(mhalf[:], -0.5)
            g.memset(mask_s[:], 0.0)
            g.memset(mask_w[:], 0.0)
            own.link(g.memset(ident[:], 0.0))
            g.affine_select(out=ident[:], in_=ident[:], compare_op=ALU.not_equal, fill=1.0, base=0,
                            pattern=[[-1, P]], channel_multiplier=1)
            g.affine_select(out=mask_s[:], in_=mask_s[:], compare_op=ALU.is_ge, fill=NEG, base=0,
                            pattern=[[-1, P]], channel_multiplier=1)
            own.link(g.affine_select(out=mask_w[:], in_=mask_w[:], compare_op=ALU.is_ge, fill=-NEG, base=0,
                                     pattern=[[1, P]], channel_multiplier=-1))
            g.tensor_copy(onesr[:], ones[:, 0:2])
            g.tensor_copy(identr[:], ident[:])
            g.tensor_copy(maskr[:], mask_s[:]).then_inc(consts, 1)

            def norm_adds(norm, end=False):
                first = sum(NORM_TILES[:norm])
                for m in range(1, NORM_TILES[norm] - end):
                    k = adds_before(norm) + m - 1
                    pool.wait_ge(sq_new, first + m + 1)
                    if m > 1:
                        pool.wait_ge(acc_add, k)
                    g.tensor_tensor(acc[:], acc[:], sq[:, k % 2, :], ALU.add).then_inc(acc_add, 1)

            def norm_pow(norm):
                pool.wait_ge(var_ready, norm + 1)
                g.tensor_tensor(rcol[:], var[:], mhalf[:, 0:4], ALU.pow).then_inc(rcol_ready, 1)

            norm_adds(NORM_MIX0)
            norm_pow(NORM_MIX0)
            def strip_low(n, kind, p=0):
                pool.wait_ge(whi_ready, p * 2 + (n + 1))
                for src, hi, lo in split_parts(kind, n % 2):
                    last = g.tensor_tensor(lo, src, hi.bitcast(F32), ALU.subtract)
                last.then_inc(wlo_ready, 1)

            norm_adds(NORM_KV)
            pool.wait_ge(wlo_ready, N_Q + 1)
            strip_low(N_Q + 1, "full")
            norm_pow(NORM_KV)
            norm_adds(NORM_CQ)
            norm_pow(NORM_CQ)

            def v_low(p):
                fixed(pool)
                pool.wait_ge(v_hi, p + 1)
                g.tensor_tensor(vl[:, :, :], v_slot(p), vh[:, :, :].bitcast(F32), ALU.subtract).then_inc(v_lo, 1)

            pool.wait_ge(wlo_ready, N_PAIR)
            strip_low(N_PAIR, "kq")
            strip_low(N_PAIR + 1, "q")
            with pool.Fori(0, PAIRS - 1) as p:
                strip_low(N_PAIR + 2, "kq", p)
                v_low(p)
                strip_low(N_PAIR + 3, "q", p)
            strip_low(N_WO, "full")
            v_low(PAIRS - 1)
            strip_low(N_WO + 1, "full")

            def low_hidden(layer, q, lead, per):
                for j in range(8):
                    pool.wait_ge(u_hi, q * per + (lead + j + 1))
                    g.tensor_tensor(ul[:, j, :], sq[:, j % 2, :], uh[:, j, :].bitcast(F32), ALU.subtract) \
                        .then_inc(u_ready, 1)

            def mlp(layer):
                norm_adds(NORM_MLP0 if layer == 0 else NORM_MLP1)
                norm_pow(NORM_MLP0 if layer == 0 else NORM_MLP1)
                with pool.Fori(0, QUARTERS) as q:
                    low_hidden(layer, q, 8 * QUARTERS * layer, 8)

            mlp(0)
            norm_adds(NORM_MIX1)
            norm_pow(NORM_MIX1)
            pool.wait_ge(wlo_ready, N_QK + 1)
            for m in range(8):
                if m == 3:
                    pool.wait_ge(wlo_ready, N_QK + 3)
                if m in (0, 3, 6):
                    strip_low(N_QK + 1 + (m + 1) // 2, "full")
                pool.wait_ge(y_hi, m + 1)
                g.tensor_tensor(ul[:, m, :], ys[:, m % 2, :], uh[:, m, :].bitcast(F32), ALU.subtract) \
                    .then_inc(y_lo, 1)
            def head_parts(i, lead, early=False):
                for j in range(TT):
                    z = 4 * lead + j
                    pool.wait_ge(sw_hi, i * 8 + (z + 1))
                    g.tensor_tensor(swl(lead % 2, j), sw[:, z % 2, 0:LEN[j]], swh(lead % 2, j).bitcast(F32),
                                    ALU.subtract).then_inc(sw_lo, 1)
                    if j == 0 and not early:
                        head_pow(i, lead - 2)

            def head_pow(i, lead):
                c = slice(4 * (lead % 2), 4 * (lead % 2) + 4)
                pool.wait_ge(var2_ready, i * 2 + (lead + 1))
                g.tensor_tensor(rc2[:, c], var2[:, c], mhalf[:, 0:4], ALU.pow).then_inc(rc2_ready, 1)

            pool.wait_ge(y_lo, 8)
            for e in range(2):
                rows = slice(64 * (1 - e), 64 * (1 - e) + 64)
                g.memset(mkh[rows, e, :].bitcast(F32), 0.0)
                own.link(g.memset(mkl[rows, e, :].bitcast(F32), 0.0))
            g.nop().then_inc(mk_zero, 1)
            def gain(m):
                pool.wait_ge(sig_new, m + 1)
                g.tensor_scalar(sg[:, m, :], sg[:, m, :], pcol[:, G_HEAD + m:G_HEAD + m + 1], None, ALU.mult) \
                    .then_inc(sg_ready, 1)

            for m in range(7):
                gain(m)
            head_parts(0, 0, early=True)
            gain(7)
            head_parts(0, 1, early=True)
            head_parts(0, 2)
            with pool.Fori(1, MPAIRS - 1) as i:
                head_parts(i, 1)
                head_parts(i, 2)
            head_parts(MPAIRS - 1, 1)
            for lead in range(2):
                head_pow(MPAIRS - 1, lead)
            strip_low(N_WO2 + 1, "full")
            mlp(1)
            norm_adds(NORM_FIN, end=True)
            norm_pow(NORM_FIN)

        @block.scalar
        def _(act):
            own = Own(act, act_own)
            sc = nc.scalar
            for at, src in ((G_MIX, a["norm_mix_g"].rearrange("l (m p) -> (l m) p", p=P)),
                            (G_MLP, a["norm_mlp_g"].rearrange("l (m p) -> (l m) p", p=P)),
                            (G_FIN, a["final_g"].rearrange("(m p) -> m p", p=P)),
                            (G_Q, a["mla_q_norm_g"].rearrange("l (m p) -> (l m) p", p=P)),
                            (G_KV, a["mla_kv_norm_g"].rearrange("l (m p) -> (l m) p", p=P)),
                            (CONV_W, a["mlstm_conv_w"].rearrange("l c (m p) -> (l c m) p", p=P)),
                            (CONV_B, a["mlstm_conv_b"].rearrange("l (m p) -> (l m) p", p=P)),
                            (G_HEAD, a["mlstm_head_norm_g"].rearrange("l (m p) -> (l m) p", p=P))):
                act.dma_start(prow[at:at + src.shape[0], :], src).then_inc(par_in, 16)
            act.dma_start(rope_c[:], a["rope_const"]).then_inc(pos_in, 16)
            act.dma_start(pos_i[:], a["positions"].broadcast_to([P, S])).then_inc(pos_in, 16)
            act.dma_start(gate_b[:, 0:1], a["mlstm_i_b"].rearrange("l h -> h l")).then_inc(pos_in, 16)
            act.dma_start(gate_b[:, 1:2], a["mlstm_f_b"].rearrange("l h -> h l")).then_inc(pos_in, 16)

            def split(n, kind="full", i=0, over=0, arrived=0):
                act.wait_ge(raw_full[n % 2], i * arrived + raw_count(n))
                if n >= 2:
                    which, value = strip_over(n - 2, gemm_done, q_mm)
                    act.wait_ge(which, i * over + value)
                parts = split_parts(kind, n % 2)
                for src, hi, _ in parts:
                    last = sc.copy(hi, src)
                if kind != "half 0":
                    last.then_inc(whi_ready, 1)

            def square(norm, m, src):
                if m == 0:
                    if norm:
                        act.wait_ge(stat_col, norm)
                    sc.activation(acc[:], src, ACT.Square).then_inc(sq_new, 1)
                else:
                    k = adds_before(norm) + m - 1
                    if k >= 2:
                        act.wait_ge(acc_add, k - 1)
                    sc.activation(sq[:, k % 2, :], src, ACT.Square).then_inc(sq_new, 1)

            def update(t0, norm, gain, m):
                act.wait_ge(gemm_evac, t0 + m + 1)
                square(norm, m, h[:, m, :])
                sc.activation(xh[:, m, :], h[:, m, :], ACT.Copy, scale=pcol[:, gain + m:gain + m + 1]) \
                    .then_inc(xh_new, 1)

            act.wait_ge(par_ready, 1)
            for m in range(KD):
                if m == 4:
                    split(N_KV)
                update(0, NORM_MIX0, G_MIX, m)
            split(N_KR, "kr")
            split(N_Q)
            for m in range(2):
                act.wait_ge(gemm_evac, T_IN + m + 1)
                square(NORM_KV, m, ckv[:, m, :])

            split(N_Q + 1)
            act.wait_ge(ang_ready, 1)
            sc.activation(sin[:], ang[:], ACT.Sin, scale=rope_c[:, 1:2]).then_inc(trig_ready, 1)
            sc.activation(cos[:], turn[:], ACT.Sin).then_inc(trig_ready, 1)

            def c_high(n_before, src, hi, gain, tiles):
                for m in range(tiles):
                    act.wait_ge(c_norm, n_before + m + 1)
                    sc.activation(hi[:, m, :], src[:, m, :], ACT.Copy, scale=pcol[:, gain + m:gain + m + 1]) \
                        .then_inc(c_hi, 1)

            c_high(0, ckv, ckvh, G_KV, 2)
            split(N_VA)
            for m in range(4):
                act.wait_ge(gemm_evac, T_IN + 4 + m + 1)
                square(NORM_CQ, m, cq[:, m, :])
            split(N_PAIR, "kq")
            act.wait_ge(kr_new, 1)
            for e in range(2):
                sc.copy(kh[e][64:128, :], krot[64:128, :]).then_inc(kr_hi, 1)

            def k_high(e, i, lead):
                act.wait_ge(k_mm, i + (lead + 1))
                if e and lead:
                    act.wait_ge(s_mm, i * 8 + 8)
                sc.copy(kh[e][0:64, :], ps[64 * e:64 * e + 64, B_KV, :]).then_inc(k_hi, 1)

            def q_high(e, i, lead):
                act.wait_ge(q_tab, i * 2 + (lead + 1))
                sc.copy(qh[e], qtmp[:]).then_inc(q_hi, 1)

            def exp(i, lead, b):
                w = P * (b + 1)
                s = 4 * lead + b
                act.wait_ge(s_max, i * 8 + (s + 1))
                if s >= 2:
                    act.wait_ge(t_mm, i * 8 + (s - 1))
                sc.activation(prob[:, b % 2, 0:w], ps[:, B_S + b % 2, 0:w], ACT.Exp, bias=nmax[:, b:b + 1],
                              accum_out=rsum[:, b:b + 1]).then_inc(s_exp, 1)

            def pt_high(i, lead, b):
                s = 4 * lead + b
                act.wait_ge(t_mm, i * 8 + (s + 1))
                sc.copy(pth[lead % 2][:, 0:b + 1, P * b:P * b + P],
                        ps[:, B_PT + b % 2, 0:P * (b + 1)].rearrange("p (j q) -> p j q", q=P)).then_inc(t_hi, 1)

            def o_high(i, lead):
                e, pair = lead % 2, i + lead // 2
                fixed(act)
                act.wait_ge(pv_mm, i * 2 + (lead + 1))
                sc.copy(uh[64 * e:64 * e + 64, ds(pair, 1), :].rearrange("p a s -> p (a s)"),
                        ps[64 * e:64 * e + 64, B_PV + e, :]).then_inc(o_hi, 1)

            c_high(2, cq, cqh, G_Q, 4)
            for e in range(2):
                k_high(e, 0, 0)
            split(N_PAIR + 1, "q")
            q_high(0, 0, 0)
            exp(0, 0, 0)
            exp(0, 0, 1)

            def attention(i, first=False, last=False):
                pt_high(i, 0, 0)
                exp(i, 0, 2)
                if last:
                    split(N_WO, "half 0")
                else:
                    split(N_PAIR + 2, "kq", i, 2, 48)
                pt_high(i, 0, 1)
                q_high(1, i, 1)
                exp(i, 0, 3)
                if last:
                    split(N_WO, "half 1")
                pt_high(i, 0, 2)
                exp(i, 1, 0)
                if not first:
                    o_high(i, -1)
                sc.copy(vh[:, :, :], v_slot(i)).then_inc(v_hi, 1)
                pt_high(i, 0, 3)
                exp(i, 1, 1)
                if not last:
                    k_high(0, i, 1)
                pt_high(i, 1, 0)
                exp(i, 1, 2)
                if not last:
                    q_high(0, i, 2)
                pt_high(i, 1, 1)
                exp(i, 1, 3)
                if not last:
                    split(N_PAIR + 3, "q", i, 2, 16)
                    k_high(1, i, 1)
                pt_high(i, 1, 2)
                if not last:
                    exp(i, 2, 0)
                pt_high(i, 1, 3)
                if not last:
                    exp(i, 2, 1)
                o_high(i, 0)

            attention(0, first=True)
            with act.Fori(1, PAIRS - 1) as i:
                attention(i)
            attention(PAIRS - 1, last=True)
            split(N_WO + 1)
            o_high(PAIRS, -1)

            def residual_stage(n0, t0, norm, gain):
                for j in range(4):
                    if j:
                        split(n0 + j + 1)
                    for m in (2 * j, 2 * j + 1):
                        update(t0, norm, gain, m)

            residual_stage(N_WO, T_WO, NORM_MLP0, G_MLP)

            def final_tile(m):
                act.wait_ge(gemm_evac, T_MLP[1] + 16 * QUARTERS - 8 + m + 1)
                square(NORM_FIN, m, h[:, m, :])
                if m >= 2:
                    act.wait_ge(out_t, m - 1)
                sc.activation(hg[:, m % 2, :], h[:, m, :], ACT.Copy, scale=pcol[:, G_FIN + m:G_FIN + m + 1]) \
                    .then_inc(hg_new, 1)

            def final_evac(m):
                act.wait_ge(out_t, m + 1)
                sc.copy(o_tok[:, :, P * m:P * m + P],
                        ps[:, B_OUT + m % 2, :].rearrange("p (t n) -> p t n", t=TT)).then_inc(out_evac, 1)

            def mlp_quarter(layer, i, q, last=False):
                n0 = N_MLP[layer] + 8 * q
                for j in range(4):
                    split(n0 + j + 1, "full", i, 16, 64)
                    for m in (2 * j, 2 * j + 1):
                        act.wait_ge(a_new, i * 8 + (8 * QUARTERS * layer + 8 * q + m + 1))
                        sc.copy(uh[:, m, :], sq[:, m % 2, :]).then_inc(u_hi, 1)
                for j in range(4):
                    if not last:
                        split(n0 + j + 5, "full", i, 16, 64)
                    elif j < 3:
                        split(n0 + j + 5)
                    elif layer == 0:
                        split(n0 + 8, "gate")
                    if last:
                        for m in (2 * j, 2 * j + 1):
                            if layer == 0:
                                update(T_MLP[0] + 16 * QUARTERS - 8, NORM_MIX1, G_MIX + 8, m)
                            else:
                                final_tile(m)
                                if m:
                                    final_evac(m - 1)

            def mlp(layer):
                with act.Fori(0, QUARTERS - 1) as i:
                    mlp_quarter(layer, i, 0)
                mlp_quarter(layer, 0, QUARTERS - 1, last=True)

            mlp(0)

            split(N_QK)
            split(N_QK + 1)
            act.wait_ge(gemm_evac, T_GATE + 1)
            sc.activation(gi[:], gi[:], ACT.Tanh, bias=gate_b[:, 2:3], scale=1.0 / CAP)
            own.link(sc.activation(gf[:], gf[:], ACT.Tanh, bias=gate_b[:, 3:4], scale=1.0 / CAP))
            own.link(sc.activation(gf[:], gf[:], ACT.Exp, scale=-CAP))
            sc.activation(gf[:], gf[:], ACT.Ln, bias=1.0).then_inc(g_ln, 1)
            for j in range(4):
                if j:
                    split(N_QK + j + 1)
                for m in (2 * j, 2 * j + 1):
                    act.wait_ge(y_new, m + 1)
                    if m >= 2:
                        act.wait_ge(y_lo, m - 1)
                    own.link(sc.activation(ys[:, m % 2, :], yc[:, m % 2, :], ACT.Silu))
                    sc.copy(uh[:, m, :], ys[:, m % 2, :]).then_inc(y_hi, 1)
            def weights(i, lead, j):
                z, e, pair = 4 * lead + j, lead % 2, i + lead // 2
                fixed(act)
                if j == 0:
                    act.wait_ge(mb_in[e], pair * 16 + 16)
                    act.wait_ge(md_ready, i * 2 + (lead + 1))
                if z >= 2:
                    act.wait_ge(sw_mul, i * 8 + (z - 1))
                bias = gcol[:, ds(pair * 2 + (MH * j + e), 1)]
                last = sc.activation(wt[:, z % 2, 0:P], md[:, e, P * j:P * j + P], ACT.Exp, bias=bias, scale=-1.0)
                if j < TT - 1:
                    last = sc.activation(wt[:, z % 2, P:LEN[j]], mb[:, e, P * (j + 1):S], ACT.Exp,
                                         bias=bias, scale=-1.0)
                last.then_inc(w_exp, 1)

            def high(i, lead, j):
                z = 4 * lead + j
                act.wait_ge(sw_mul, i * 8 + (z + 1))
                sc.copy(swh(lead % 2, j), sw[:, z % 2, 0:LEN[j]]).then_inc(sw_hi, 1)

            def v_high(i, lead):
                e, pair = lead % 2, i + lead // 2
                sc.copy(mvh[:, :, P * e:P * e + P], v_tok[:, :, ds(pair * 256 + P * e, P)]).then_inc(mv_hi, 1)

            def square_num(i, lead):
                e = lead % 2
                act.wait_ge(num_mm, i * 2 + (lead + 1))
                sc.activation(numsq[:, e, :], bank(B_NUM[e]), ACT.Square).then_inc(num_sq, 1)

            def row_copy(i, lead):
                act.wait_ge(den_mm, i * 2 + (lead + 1))
                sc.copy(den_row, ps[0:1, B_DEN, :]).then_inc(den_read, 1)

            def gated_high(i, lead):
                e, pair = lead % 2, i + lead // 2
                fixed(act)
                act.wait_ge(hs_ready, i * 2 + (lead + 1))
                sc.copy(uh[:, ds(pair + 4 * e, 1), :].rearrange("p a s -> p (a s)"), rb[:, e, :]) \
                    .then_inc(g_hi, 1)

            def head_step(i, lead, early=False, last=False):
                if not last:
                    weights(i, lead + 1, 0)
                    weights(i, lead + 1, 1)
                if not early:
                    gated_high(i, lead - 2)
                if not last:
                    high(i, lead + 1, 0)
                    v_high(i, lead + 1)
                    weights(i, lead + 1, 2)
                    high(i, lead + 1, 1)
                    weights(i, lead + 1, 3)
                    high(i, lead + 1, 2)
                else:
                    act.wait_ge(g_ready, MH - 2)
                square_num(i, lead)
                if not last:
                    high(i, lead + 1, 3)
                row_copy(i, lead)

            for j in range(4):
                split(N_V + j + 1)
                if j == 0:
                    act.wait_ge(g_m, 1)
                    sc.activation(en[:], en[:], ACT.Exp, scale=-1.0).then_inc(g_en, 1)
            for j in range(4):
                split(N_O + j + 1)
                if j == 3:
                    for block in range(TT):
                        weights(0, 0, block)
                for m in (2 * j, 2 * j + 1):
                    if m == 7:
                        act.wait_ge(gemm_done, T_O + 8)
                        high(0, 0, 0)
                        high(0, 0, 1)
                        v_high(0, 0)
                    act.wait_ge(gemm_evac, T_O + m + 1)
                    sc.activation(sg[:, m, :], otmp[:, m % 2, :], ACT.Sigmoid).then_inc(sig_new, 1)
            high(0, 0, 2)
            high(0, 0, 3)
            for u in range(3):
                head_step(0, u, early=(u < 2))
            with act.Fori(1, MPAIRS - 1) as i:
                head_step(i, 1)
                head_step(i, 2)
            head_step(MPAIRS - 1, 1, last=True)
            gated_high(MPAIRS - 1, 0)
            split(N_WO2 + 1)
            gated_high(MPAIRS - 1, 1)
            residual_stage(N_WO2, T_WO2, NORM_MLP1, G_MLP + 8)
            mlp(1)
            final_evac(KD - 1)

        @block.vector
        def _(dve):
            own = Own(dve, dve_own)
            v = nc.vector

            def split(n, kind="full", i=0, per=0):
                dve.wait_ge(whi_ready, i * per + (n + 1))
                for src, hi, lo in split_parts(kind, n % 2):
                    last = v.tensor_tensor(lo, src, hi.bitcast(F32), ALU.subtract)
                last.then_inc(wlo_ready, 1)

            def low(t_lo_, src, hi, gain=None):
                if gain is None:
                    return v.tensor_tensor(t_lo_, src, hi.bitcast(F32), ALU.subtract)
                return v.scalar_tensor_tensor(out=t_lo_, in0=src, scalar=gain, in1=hi.bitcast(F32),
                                              op0=ALU.mult, op1=ALU.subtract)

            def x_low(group, gain, m):
                dve.wait_ge(xh_new, 8 * group + m + 1)
                low(xl[:, m, :], h[:, m, :], xh[:, m, :], pcol[:, gain + m:gain + m + 1]).then_inc(x_ready, 1)

            def stat_diag(norm, width):
                dve.wait_ge(stat_col, norm + 1)
                v.tensor_scalar(var[:], ps[:, B_COL, 0:4], 1.0 / width, EPS, ALU.mult, ALU.add) \
                    .then_inc(var_ready, 1)
                dve.wait_ge(rcol_ready, norm + 1)
                for t in range(TT):
                    last = v.tensor_scalar(diag[:, 0, P * t:P * t + P], ident[:], rcol[:, t:t + 1], None,
                                           ALU.mult)
                last.then_inc(diag_ready, 1)

            def stat_row(norm, r):
                dve.wait_ge(stat_bc, norm + 1)
                v.tensor_copy(r[:], bank(B_BC)).then_inc(rbc_ready, 1)
                dve.wait_ge(rbc_ready, norm + 1)

            for m in range(KD):
                dve.wait_ge(gemm_done, m + 1)
                v.tensor_copy(h[:, m, :], bank(m % RING)).then_inc(gemm_evac, 1)
                if m == RING - 1:
                    dve.wait_ge(par_t, 1)
                    v.tensor_copy(pcol[:], ps[:, B_COL, 0:PCOLS]).then_inc(par_ready, 1)
                    dve.wait_ge(par_ready, 1)
                    for lead in range(m):
                        x_low(0, G_MIX, lead)
                elif m >= RING:
                    x_low(0, G_MIX, m - 1)
            x_low(0, G_MIX, KD - 1)
            split(N_KV)
            split(N_KR, "kr")

            stat_diag(NORM_MIX0, D)
            stat_row(NORM_MIX0, r_a)

            def scaled(t, dst, r):
                dve.wait_ge(gemm_done, t + 1)
                return v.tensor_tensor(dst, bank(t % RING), r[:], ALU.mult)

            for m in range(2):
                scaled(T_IN + m, ckv[:, m, :], r_a).then_inc(gemm_evac, 1)
            split(N_Q)

            dve.wait_ge(pos_in, 64)
            own.link(v.tensor_copy(ang[:], pos_i[:]))
            own.link(v.tensor_scalar(ang[:], ang[:], rope_c[:, 0:1], None, ALU.mult))
            own.link(v.tensor_scalar(turn[:], ang[:], 1.0 / (2 * np.pi), MAGIC, ALU.mult, ALU.add))
            own.link(v.tensor_scalar(turn[:], turn[:], MAGIC, None, ALU.subtract))
            for part in (TWO_PI_1, TWO_PI_2, TWO_PI_3):
                own.link(v.scalar_tensor_tensor(out=ang[:], in0=turn[:], scalar=-part, in1=ang[:],
                                                op0=ALU.mult, op1=ALU.add))
            own.link(v.tensor_scalar(ang[:], ang[:], PI_IN, -PI_IN, ALU.min, ALU.max))
            own.link(v.tensor_scalar(turn[:], ang[:], np.pi / 2, -2 * np.pi, ALU.is_gt, ALU.mult))
            own.link(v.scalar_tensor_tensor(out=turn[:], in0=ang[:], scalar=np.pi / 2, in1=turn[:],
                                            op0=ALU.add, op1=ALU.add))
            own.link(v.tensor_scalar(turn[:], turn[:], PI_IN, -PI_IN, ALU.min, ALU.max))
            v.tensor_scalar(gate_b[:, 2:4], gate_b[:, 0:2], 1.0 / CAP, None, ALU.mult).then_inc(ang_ready, 1)

            stat_diag(NORM_KV, KVRANK)
            v.memset(tab[0:64, :], SCALE)
            dve.wait_ge(trig_ready, 2)
            v.tensor_scalar(tab[64:96, :], cos[64:96, :], SCALE, None, ALU.mult)
            own.link(v.tensor_scalar(tab[96:128, :], sin[96:128, :], SCALE, None, ALU.mult))
            dve.wait_ge(gemm_done, T_IN + 4)
            for table, dst, src in ((cos, krot, 64), (sin, krot2, 64 + ROPE)):
                for at in (64, 64 + ROPE):
                    last = v.tensor_tensor(dst[at:at + ROPE, :], ps[src:src + ROPE, (T_IN + 2) % RING, :],
                                           table[at:at + ROPE, :], ALU.mult)
                last.then_inc(gemm_evac, 1)
            dve.wait_ge(gemm_evac, T_IN + 4)
            own.link(v.tensor_tensor(krot[64:128, :], krot[64:128, :], krot2[64:128, :], ALU.add))
            v.tensor_tensor(krot[64:128, :], krot[64:128, :], r_a[64:128, :], ALU.mult).then_inc(kr_new, 1)
            scaled(T_IN + 4, cq[:, 0, :], r_a).then_inc(gemm_evac, 1)
            stat_row(NORM_KV, r_b)

            dve.wait_ge(gemm_evac, T_IN + 2)
            for m in range(2):
                v.tensor_tensor(ckv[:, m, :], ckv[:, m, :], r_b[:], ALU.mult).then_inc(c_norm, 1)
            for m in range(2):
                dve.wait_ge(c_hi, m + 1)
                low(ckvl[:, m, :], ckv[:, m, :], ckvh[:, m, :], pcol[:, G_KV + m:G_KV + m + 1]).then_inc(c_ready, 1)
            scaled(T_IN + 5, cq[:, 1, :], r_a).then_inc(gemm_evac, 1)
            dve.wait_ge(wlo_ready, N_VA)
            split(N_VA)
            scaled(T_IN + 6, cq[:, 2, :], r_a).then_inc(gemm_evac, 1)
            scaled(T_IN + 7, cq[:, 3, :], r_a).then_inc(gemm_evac, 1)
            def v_evac(t):
                half, tt = t // TT, t % TT
                dve.wait_ge(gemm_done, T_VA + t + 1)
                v.tensor_copy(v_all[:, 4 * half:4 * half + 4, P * tt:P * tt + P],
                              bank((T_VA + t) % RING).rearrange("p (m n) -> p m n", n=P)).then_inc(gemm_evac, 1)

            for t in range(2):
                v_evac(t)
            stat_diag(NORM_CQ, QRANK)
            for t in range(2, 5):
                v_evac(t)
            for e in range(2):
                dve.wait_ge(kr_hi, e + 1)
                low(kl[e][64:128, :], krot[64:128, :], kh[e][64:128, :]).then_inc(kr_lo, 1)
            stat_row(NORM_CQ, r_b)
            for m in range(4):
                v.tensor_tensor(cq[:, m, :], cq[:, m, :], r_b[:], ALU.mult).then_inc(c_norm, 1)
            for m in range(4):
                if m < 3:
                    v_evac(5 + m)
                dve.wait_ge(c_hi, 2 + m + 1)
                low(cql[:, m, :], cq[:, m, :], cqh[:, m, :], pcol[:, G_Q + m:G_Q + m + 1]).then_inc(c_ready, 1)

            def k_low(e, i, lead):
                dve.wait_ge(k_hi, i * 2 + (2 * lead + e + 1))
                low(kl[e][0:64, :], ps[64 * e:64 * e + 64, B_KV, :], kh[e][0:64, :]).then_inc(k_lo, 1)

            def q_table(i, lead):
                dve.wait_ge(q_mm, i * 2 + (lead + 1))
                if lead:
                    dve.wait_ge(q_lo, i * 2 + lead)
                v.tensor_tensor(qtmp[:], bank(B_Q), tab[:], ALU.mult).then_inc(q_tab, 1)

            def q_low(i, lead):
                dve.wait_ge(q_hi, i * 2 + (lead + 1))
                low(ql[lead % 2], qtmp[:], qh[lead % 2]).then_inc(q_lo, 1)

            def row_max(i, lead, b):
                dve.wait_ge(s_mm, i * 8 + (4 * lead + b + 1))
                v.tensor_reduce(nmax[:, b:b + 1], ps[:, B_S + b % 2, 0:P * (b + 1)], op=ALU.max, axis=AX.X,
                                negate=True).then_inc(s_max, 1)

            def normalise(i, lead, b):
                dve.wait_ge(s_exp, i * 8 + (4 * lead + b + 1))
                own.link(v.reciprocal(rinv[:, b:b + 1], rsum[:, b:b + 1]))
                w = P * (b + 1)
                v.tensor_scalar(prob[:, b % 2, 0:w], prob[:, b % 2, 0:w], rinv[:, b:b + 1], None, ALU.mult) \
                    .then_inc(p_norm, 1)

            def pt_low(i, lead, b):
                dve.wait_ge(t_hi, i * 8 + (4 * lead + b + 1))
                part, e = slice(P * b, P * b + P), lead % 2
                low(ptl[e][:, 0:b + 1, part], ps[:, B_PT + b % 2, 0:P * (b + 1)].rearrange("p (j q) -> p j q", q=P),
                    pth[e][:, 0:b + 1, part]).then_inc(t_lo, 1)

            def o_low(i, lead):
                e, pair = lead % 2, i + lead // 2
                dve.wait_ge(o_hi, i * 2 + (lead + 1))
                rows = slice(64 * e, 64 * e + 64)
                low(ul[rows, ds(pair, 1), :].rearrange("p a s -> p (a s)"), ps[rows, B_PV + e, :],
                    uh[rows, ds(pair, 1), :].rearrange("p a s -> p (a s)")).then_inc(o_lo, 1)

            for e in range(2):
                k_low(e, 0, 0)
            q_table(0, 0)
            q_low(0, 0)
            row_max(0, 0, 0)
            row_max(0, 0, 1)
            normalise(0, 0, 0)

            def attention(i, first=False, last=False):
                normalise(i, 0, 1)
                row_max(i, 0, 2)
                pt_low(i, 0, 0)
                normalise(i, 0, 2)
                q_table(i, 1)
                row_max(i, 0, 3)
                pt_low(i, 0, 1)
                q_low(i, 1)
                normalise(i, 0, 3)
                row_max(i, 1, 0)
                pt_low(i, 0, 2)
                if not first:
                    o_low(i, -1)
                normalise(i, 1, 0)
                row_max(i, 1, 1)
                pt_low(i, 0, 3)
                if not last:
                    k_low(0, i, 1)
                normalise(i, 1, 1)
                row_max(i, 1, 2)
                pt_low(i, 1, 0)
                if not last:
                    q_table(i, 2)
                normalise(i, 1, 2)
                row_max(i, 1, 3)
                if not last:
                    q_low(i, 2)
                pt_low(i, 1, 1)
                normalise(i, 1, 3)
                if not last:
                    k_low(1, i, 1)
                    row_max(i, 2, 0)
                pt_low(i, 1, 2)
                if not last:
                    normalise(i, 2, 0)
                    row_max(i, 2, 1)
                pt_low(i, 1, 3)
                o_low(i, 0)

            attention(0, first=True)
            with dve.Fori(1, PAIRS - 1) as i:
                own.enter(i, 1, 8)
                attention(i)
                own.leave(1, PAIRS - 1)
            attention(PAIRS - 1, last=True)
            o_low(PAIRS, -1)
            dve.wait_ge(wlo_ready, N_WO + 2)

            def onto_residual(t, m, i=0, per=0):
                dve.wait_ge(gemm_done, i * per + (t + 1))
                return v.tensor_tensor(h[:, m, :], bank(t % RING), h[:, m, :], ALU.add)

            def residual_stage(n0, t0, group, gain):
                for j in range(4):
                    if j:
                        split(n0 + j + 1)
                    for m in (2 * j, 2 * j + 1):
                        onto_residual(t0 + m, m).then_inc(gemm_evac, 1)
                        if m:
                            x_low(group, gain, m - 1)
                x_low(group, gain, KD - 1)

            residual_stage(N_WO, T_WO, 1, G_MLP)

            def mlp_quarter(layer, i, q, first=False, last=False):
                n0, t0 = N_MLP[layer] + 8 * q, T_MLP[layer] + 16 * q
                u0 = 8 * QUARTERS * layer + 8 * q
                for j in range(4):
                    split(n0 + j + 1, "full", i, 8)
                    if first and j == 0:
                        norm = NORM_MLP0 if layer == 0 else NORM_MLP1
                        stat_diag(norm, D)
                        stat_row(norm, r_a)
                    for m in (2 * j, 2 * j + 1):
                        dve.wait_ge(gemm_done, i * 16 + (t0 + m + 1))
                        v.tensor_tensor(diag[:, m % 2, :], bank((t0 + m) % RING), r_a[:], ALU.mult) \
                            .then_inc(gemm_evac, 1)
                        dve.wait_ge(gemm_evac, i * 16 + (t0 + m + 1))
                        if u0 or m > 1 or not first:
                            dve.wait_ge(u_ready, i * 8 + (u0 + max(m - 1, 0)))
                        v.scalar_tensor_tensor(out=sq[:, m % 2, :], in0=diag[:, m % 2, :], scalar=0.0,
                                               in1=diag[:, m % 2, :], op0=ALU.max, op1=ALU.mult) \
                            .then_inc(a_new, 1)
                for j in range(4):
                    if not last:
                        split(n0 + j + 5, "full", i, 8)
                    elif j < 3:
                        split(n0 + j + 5)
                    elif layer == 0:
                        split(n0 + 8, "gate")
                    for m in (2 * j, 2 * j + 1):
                        onto_residual(t0 + 8 + m, m, i, 16).then_inc(gemm_evac, 1)
                        if last and layer == 0 and m:
                            x_low(2, G_MIX + 8, m - 1)
                if last and layer == 0:
                    x_low(2, G_MIX + 8, KD - 1)

            def mlp(layer):
                mlp_quarter(layer, 0, 0, first=True)
                with dve.Fori(1, QUARTERS - 1) as i:
                    mlp_quarter(layer, i, 0)
                mlp_quarter(layer, 0, QUARTERS - 1, last=True)

            mlp(0)

            split(N_QK)
            stat_diag(NORM_MIX1, D)
            stat_row(NORM_MIX1, r_a)
            v.memset(zrow[:], 0.0)
            v.memset(cpad[:, 0:CONV - 1], 0.0)
            dve.wait_ge(gemm_done, T_GATE + 1)
            b = bank(T_GATE % RING)
            own.link(v.tensor_tensor(gi[:], b[0:MH, :], r_a[0:MH, :], ALU.mult))
            v.tensor_tensor(gf[:], b[32:32 + MH, :], r_a[32:32 + MH, :], ALU.mult).then_inc(gemm_evac, 1)

            def gates():
                dve.wait_ge(g_ln, 1)
                own.link(v.tensor_tensor_scan(Fc[:], gf[:], zrow[:], 0.0, ALU.add, ALU.add))
                own.link(v.scalar_tensor_tensor(out=Gc[:], in0=gi[:], scalar=CAP, in1=Fc[:], op0=ALU.mult,
                                                op1=ALU.add))
                own.link(v.tensor_tensor_scan(Mc[:], Gc[:], Gc[:], 0.0, ALU.max, ALU.max))
                v.tensor_tensor(en[:], Mc[:], Fc[:], ALU.subtract).then_inc(g_m, 1)

            def gate_columns():
                dve.wait_ge(g_t, 1)
                v.tensor_copy(gcol[:], ps[:, 5, 0:32]).then_inc(gcol_ready, 1)
                v.tensor_copy(encol[:, :].rearrange("p (e j) -> p e j", e=MH),
                              ps[:, 5, 32:64].rearrange("p (j e) -> p e j", e=MH)).then_inc(gcol_ready, 1)

            def conv(m):
                if m:
                    dve.wait_ge(y_new, m)
                scaled(T_QK + m, cpad[:, CONV - 1:CONV - 1 + S], r_a).then_inc(gemm_evac, 1)
                if m >= 2:
                    dve.wait_ge(y_hi, m - 1)
                dve.wait_ge(gemm_evac, T_QK + m + 1)
                w = [pcol[:, CONV_W + 8 * c + m:CONV_W + 8 * c + m + 1] for c in range(CONV)]
                y = yc[:, m % 2, :]
                own.link(v.tensor_scalar(y, cpad[:, 0:S], w[0], pcol[:, CONV_B + m:CONV_B + m + 1],
                                         ALU.mult, ALU.add))
                for c in range(1, CONV):
                    ins = v.scalar_tensor_tensor(out=y, in0=cpad[:, c:c + S], scalar=w[c], in1=y,
                                                 op0=ALU.mult, op1=ALU.add)
                    if c < CONV - 1:
                        own.link(ins)
                ins.then_inc(y_new, 1)

            for j in range(4):
                conv(2 * j)
                if j == 1:
                    dve.wait_ge(wlo_ready, N_QK + 2)
                    split(N_QK + 2)
                conv(2 * j + 1)
                if j == 1:
                    gates()
            dve.wait_ge(wlo_ready, N_V + 1)
            for j in range(4):
                split(N_V + j + 1)
                for i in range(2):
                    t = T_V + 2 * j + i
                    dve.wait_ge(gemm_done, t + 1)
                    for half in range(2):
                        tt = 2 * i + half
                        last = v.tensor_scalar(v_tok[:, tt, 256 * j:256 * j + 256],
                                               ps[:, t % RING, 256 * half:256 * half + 256],
                                               rcol[:, tt:tt + 1], None, ALU.mult)
                    last.then_inc(gemm_evac, 1)
                if j == 1:
                    gate_columns()
            def k_copy(i, lead):
                e, pair = lead % 2, i + lead // 2
                rows = slice(64 * e, 64 * e + 64)
                for dst, src in ((mkh, uh), (mkl, ul)):
                    last = v.tensor_copy(dst[rows, e, :], src[rows, ds(pair + 4, 1), :]
                                         .rearrange("p a s -> p (a s)").bitcast(F32))
                last.then_inc(mk_ready, 1)

            def masked(i, lead):
                e, pair = lead % 2, i + lead // 2
                dve.wait_ge(mb_in[e], pair * 16 + 16)
                v.tensor_tensor(md[:, e, :].rearrange("p (j q) -> p j q", q=P),
                                mb[:, e, :].rearrange("p (j q) -> p j q", q=P),
                                mask_w[:].unsqueeze(1).broadcast_to([P, TT, P]), ALU.add).then_inc(md_ready, 1)

            def weighted(i, lead, j):
                z, n = 4 * lead + j, LEN[j]
                dve.wait_ge(st_mm, i * 8 + (z + 1))
                dve.wait_ge(w_exp, i * 8 + (z + 1))
                if z >= 2:
                    dve.wait_ge(sw_lo, i * 8 + (z - 1))
                v.scalar_tensor_tensor(out=sw[:, z % 2, 0:n], in0=ps[:, B_ST + z % 2, 0:n],
                                       scalar=float(64 ** -0.5), in1=wt[:, z % 2, 0:n],
                                       op0=ALU.mult, op1=ALU.mult).then_inc(sw_mul, 1)

            def v_low(i, lead):
                e, pair = lead % 2, i + lead // 2
                dve.wait_ge(mv_hi, i * 2 + (lead + 1))
                part = mvh[:, :, P * e:P * e + P]
                low(mvl[:, :, P * e:P * e + P], v_tok[:, :, ds(pair * 256 + P * e, P)], part).then_inc(mv_lo, 1)

            for j in range(4):
                if j == 2:
                    dve.wait_ge(y_lo, 8)
                    for e in range(2):
                        k_copy(0, e)
                        masked(0, e)
                split(N_O + j + 1)
                if j == 3:
                    weighted(0, 0, 0)
                    weighted(0, 0, 1)
                for m in (2 * j, 2 * j + 1):
                    if m < 2:
                        dve.wait_ge(y_hi, 8)
                    else:
                        dve.wait_ge(sig_new, m - 1)
                    scaled(T_O + m, otmp[:, m % 2, :], r_a).then_inc(gemm_evac, 1)

            def head_norm(i, lead):
                e, pair = lead % 2, i + lead // 2
                c = slice(4 * e, 4 * e + 4)
                dve.wait_ge(ms_mm, i * 2 + (lead + 1))
                v.tensor_copy(stat[:, e, :], ps[:, B_STAT, 0:8]).then_inc(stat_read, 1)
                dve.wait_ge(stat_read, i * 2 + (lead + 1))
                den = stat[:, e, 0:4]
                own.link(v.scalar_tensor_tensor(out=dd[:, c], in0=den, scalar=-1.0, in1=den,
                                                op0=ALU.mult, op1=ALU.max))
                own.link(v.tensor_tensor(dd[:, c], dd[:, c], encol[:, ds(pair * 8 + 4 * e, 4)], ALU.max))
                own.link(v.scalar_tensor_tensor(out=dd[:, c], in0=dd[:, c], scalar=EPS, in1=dd[:, c],
                                                op0=ALU.mult, op1=ALU.mult))
                v.scalar_tensor_tensor(out=var2[:, c], in0=stat[:, e, 4:8], scalar=1.0 / P, in1=dd[:, c],
                                       op0=ALU.mult, op1=ALU.add).then_inc(var2_ready, 1)

            def head_diag(i, lead):
                e, c = lead % 2, slice(4 * (lead % 2), 4 * (lead % 2) + 4)
                dve.wait_ge(rc2_ready, i * 2 + (lead + 1))
                v.tensor_tensor(diag[:, e, :].rearrange("p (t q) -> p t q", q=P),
                                ident[:].unsqueeze(1).broadcast_to([P, TT, P]),
                                rc2[:, c].unsqueeze(2).broadcast_to([P, TT, P]), ALU.mult).then_inc(diag2_ready, 1)

            def gated(i, lead):
                e, pair = lead % 2, i + lead // 2
                dve.wait_ge(bc2_mm, i * 2 + (lead + 1))
                v.tensor_tensor(rb[:, e, :], bank(B_BCH),
                                sg[:, ds(pair * 2 + e, 1), :].rearrange("p a s -> p (a s)"), ALU.mult) \
                    .then_inc(rb_ready, 1)
                dve.wait_ge(rb_ready, i * 2 + (lead + 1))
                v.tensor_tensor(rb[:, e, :], rb[:, e, :], bank(B_NUM[e]), ALU.mult).then_inc(hs_ready, 1)

            def gated_low(i, lead):
                e, pair = lead % 2, i + lead // 2
                dve.wait_ge(g_hi, i * 2 + (lead + 1))
                low(ul[:, ds(pair + 4 * e, 1), :].rearrange("p a s -> p (a s)"), rb[:, e, :],
                    uh[:, ds(pair + 4 * e, 1), :].rearrange("p a s -> p (a s)")).then_inc(g_ready, 1)

            def head_step(i, lead, first=False, early=False, last=False):
                if not last and not first:
                    k_copy(i, lead + 1)
                    masked(i, lead + 1)
                if not early:
                    gated(i, lead - 2)
                if not last:
                    weighted(i, lead + 1, 0)
                    weighted(i, lead + 1, 1)
                if not first:
                    head_norm(i, lead - 1)
                if not early:
                    gated_low(i, lead - 2)
                if not last:
                    v_low(i, lead + 1)
                    weighted(i, lead + 1, 2)
                if not first:
                    head_diag(i, lead - 1)
                if not last:
                    weighted(i, lead + 1, 3)

            v_low(0, 0)
            weighted(0, 0, 2)
            weighted(0, 0, 3)
            for u in range(3):
                if u == 2:
                    dve.wait_ge(sg_ready, MH)
                head_step(0, u, first=(u == 0), early=(u < 2))
            with dve.Fori(1, MPAIRS - 1) as i:
                own.enter(i, 1, 6)
                head_step(i, 1)
                head_step(i, 2)
                own.leave(1, MPAIRS - 1)
            head_step(MPAIRS - 1, 1, last=True)
            gated(MPAIRS - 1, 0)
            gated_low(MPAIRS - 1, 0)
            head_norm(MPAIRS - 1, 1)
            head_diag(MPAIRS - 1, 1)
            gated(MPAIRS - 1, 1)
            gated_low(MPAIRS - 1, 1)
            dve.wait_ge(wlo_ready, N_WO2 + 2)
            residual_stage(N_WO2, T_WO2, 3, G_MLP + 8)
            mlp(1)
            dve.wait_ge(stat_col, NORM_FIN + 1)
            v.tensor_scalar(var[:], ps[:, B_COL, 0:4], 1.0 / D, EPS, ALU.mult, ALU.add).then_inc(var_ready, 1)
            dve.wait_ge(rcol_ready, NORM_FIN + 1)
            dve.wait_ge(out_evac, KD)
            for t in range(TT):
                v.tensor_scalar(o_tok[:, t, :], o_tok[:, t, :], rcol[:, t:t + 1], None, ALU.mult) \
                    .then_inc(out_ready, 1)

        @block.tensor
        def _(pe):
            mm, tr = nc.tensor.matmul, nc.tensor.transpose

            def product(o, pairs, wait=None):
                for k, ((ah, al), (bh, bl)) in enumerate(pairs):
                    if wait is not None:
                        wait(k)
                    first, last = k == 0, k == len(pairs) - 1
                    mm(o, ah, bl, start=first, stop=False)
                    mm(o, ah, bh, start=False, stop=False)
                    ins = mm(o, al, bh, start=False, stop=last)
                return ins

            def free_bank(t, i=0, per=0):
                if t >= RING:
                    pe.wait_ge(gemm_evac, i * per + (t - RING + 1))

            def strip_ready(n, i=0, per=0):
                pe.wait_ge(wlo_ready, i * per + (n + 1))

            def tile(t, n, c, rh, rl, wait=None, i=0, per=0, width=P, order=None):
                free_bank(t, i, per)
                s = n % 2
                ks = range(8)
                o = ps[0:width, t % RING, :]
                order = order or (lambda k: k)
                return product(o, [((full(whi[s])[:, k, c:c + width], full(wlo[s])[:, k, c:c + width]),
                                    (rh[:, order(k), :], rl[:, order(k), :])) for k in ks], wait) \
                    .then_inc(gemm_done, 1)

            def stat_sum(norm, end=False):
                n = adds_before(norm + 1)
                pe.wait_ge(acc_add, n - end)
                if end:
                    pe.wait_ge(sq_new, sum(NORM_TILES))
                for t in range(TT):
                    part = slice(P * t, P * t + P)
                    last = mm(ps[:, B_COL, t:t + 1], acc[:, part], ones[:, 0:1], start=True, stop=not end)
                    if end:
                        last = mm(ps[:, B_COL, t:t + 1], sq[:, (n - 1) % 2, part], ones[:, 0:1],
                                  start=False, stop=True)
                last.then_inc(stat_col, 1)

            def stat_spread(norm):
                pe.wait_ge(diag_ready, norm + 1)
                if norm:
                    pe.wait_ge(rbc_ready, norm)
                mm(bank(B_BC), ones[:], diag[:, 0, :], start=True, stop=True).then_inc(stat_bc, 1)

            pe.wait_ge(consts, 1)
            for m in range(KD):
                if m == RING:
                    pe.wait_ge(par_in, 128)
                    tr(ps[:, B_COL, 0:PCOLS], prow[:, :], ident[0:PCOLS, 0:PCOLS]).then_inc(par_t, 1)
                pe.wait_ge(x_in[m // 2], 16)
                free_bank(m)
                for t in range(TT):
                    last = tr(ps[:, m % RING, P * t:P * t + P], x_tok[:, t, P * m:P * m + P], ident[:])
                last.then_inc(gemm_done, 1)

            def x_wait(group):
                return lambda k: pe.wait_ge(x_ready, 8 * group + k + 1)

            pe.wait_ge(whi_ready, N_KV + 1)
            for m in range(2):
                free_bank(T_IN + m)
            wh, wl = full(whi[N_KV % 2]), full(wlo[N_KV % 2])
            for k in range(8):
                x_wait(0)(k)
                for m in range(2):
                    o, cols = bank((T_IN + m) % RING), slice(P * m, P * m + P)
                    mm(o, wh[:, k, cols], xl[:, k, :], start=k == 0, stop=False)
                    mm(o, wh[:, k, cols], xh[:, k, :], start=False, stop=False)
            strip_ready(N_KV)
            for m in range(2):
                for k in range(8):
                    last = mm(bank((T_IN + m) % RING), wl[:, k, P * m:P * m + P], xh[:, k, :],
                              start=False, stop=k == 7)
                last.then_inc(gemm_done, 1)
                if m == 0:
                    stat_sum(NORM_MIX0)
            stat_spread(NORM_MIX0)
            strip_ready(N_KR)
            t = T_IN + 2
            free_bank(t + 1)
            wh, wl = [kr_split(w[N_KR % 2]).rearrange("p k r n -> p k (r n)") for w in (whi, wlo)]
            product(bank(t % RING), [((wh[:, k, :], wl[:, k, :]), (xh[:, k, :], xl[:, k, :]))
                                     for k in range(8)]).then_inc(gemm_done, 2)
            strip_ready(N_Q)
            tile(T_IN + 4, N_Q, 0, xh, xl)
            stat_sum(NORM_KV)
            tile(T_IN + 5, N_Q, P, xh, xl)
            stat_spread(NORM_KV)
            strip_ready(N_Q + 1)
            pe.wait_ge(gemm_evac, T_IN + 4)
            tile(T_IN + 6, N_Q + 1, 0, xh, xl)
            tile(T_IN + 7, N_Q + 1, P, xh, xl)

            def k_product(s, wait=None):
                product(bank(B_KV), [((pkv(whi[s])[:, k, :], pkv(wlo[s])[:, k, :]), (ckvh[:, k, :], ckvl[:, k, :]))
                                     for k in range(2)], wait).then_inc(k_mm, 1)

            def q_half(half, s, wait=None):
                for k in (0, 1) if half == 0 else (2, 3):
                    if wait is not None:
                        wait(k)
                    ah, al, bh, bl = pq(whi[s])[:, k, :], pq(wlo[s])[:, k, :], cqh[:, k, :], cql[:, k, :]
                    mm(bank(B_Q), ah, bl, start=(k == 0), stop=False)
                    mm(bank(B_Q), ah, bh, start=False, stop=False)
                    last = mm(bank(B_Q), al, bh, start=False, stop=(k == 3))
                if half:
                    last.then_inc(q_mm, 1)

            def scores(i, lead, b):
                e = lead % 2
                s = 4 * lead + b
                if s >= 2:
                    pe.wait_ge(s_exp, i * 8 + (s - 1))
                if b == 0:
                    pe.wait_ge(q_hi, i * 2 + (lead + 1))
                    pe.wait_ge(k_lo, i * 2 + (lead + 1))
                w = P * (b + 1)
                o = ps[:, B_S + b % 2, 0:w]
                part = slice(P * b, P * b + P)
                mm(o, qh[e][:, part], kl[e][:, 0:w], start=True, stop=False)
                mm(o, qh[e][:, part], kh[e][:, 0:w], start=False, stop=False)
                if b == 0:
                    pe.wait_ge(q_lo, i * 2 + (lead + 1))
                mm(o, ql[e][:, part], kh[e][:, 0:w], start=False, stop=False)
                mm(ps[:, B_S + b % 2, P * b:w], identr[:], maskr[:], start=False, stop=True).then_inc(s_mm, 1)

            def turn_p(i, lead, b, first=False):
                s = 4 * lead + b
                pe.wait_ge(p_norm, i * 8 + (s + 1))
                if s >= 2 or not first:
                    pe.wait_ge(t_lo, i * 8 + (s - 1))
                for j in range(b + 1):
                    last = tr(ps[:, B_PT + b % 2, P * j:P * j + P], prob[:, b % 2, P * j:P * j + P], ident[:])
                last.then_inc(t_mm, 1)

            def weigh(i, lead, steps=(0, 1)):
                e = lead % 2
                for j in range(TT) if 0 in steps else ():
                    if j == 0:
                        pe.wait_ge(t_hi, i * 8 + (4 * lead + 4))
                        pe.wait_ge(v_hi, i + (lead // 2 + 1))
                    mm(ps[:, B_PV + e, P * j:S], vh[:, j, :], pth[e][:, j, P * j:S], start=(j == 0), stop=False)
                for j in range(TT) if 1 in steps else ():
                    o = ps[:, B_PV + e, P * j:S]
                    if j == 0:
                        pe.wait_ge(v_lo, i + (lead // 2 + 1))
                        pe.wait_ge(t_lo, i * 8 + (4 * lead + 4))
                    mm(o, vl[:, j, :], pth[e][:, j, P * j:S], start=False, stop=False)
                    last = mm(o, vh[:, j, :], ptl[e][:, j, P * j:S], start=False, stop=(j == TT - 1))
                if 1 in steps:
                    last.then_inc(pv_mm, 1)

            strip_ready(N_VA)
            pe.wait_ge(c_ready, 2)
            wv = [w[N_VA % 2][:, :].rearrange("p (k n) -> p k n", k=2) for w in (whi, wlo)]
            for t in range(8):
                half, part = t // TT, slice(P * (t % TT), P * (t % TT) + P)
                cols = slice(512 * half, 512 * half + 512)
                free_bank(T_VA + t)
                product(bank((T_VA + t) % RING), [((ckvh[:, k, part], ckvl[:, k, part]),
                                                   (wv[0][:, k, cols], wv[1][:, k, cols]))
                                                  for k in range(2)]).then_inc(gemm_done, 1)
                if t == 1:
                    stat_sum(NORM_CQ)
                if t == 4:
                    stat_spread(NORM_CQ)
            pe.wait_ge(gemm_evac, T_VA + 6)
            strip_ready(N_PAIR)
            k_product(N_PAIR % 2)
            for half in range(2):
                q_half(half, N_PAIR % 2, lambda k: pe.wait_ge(c_ready, 2 + k + 1))
            pe.wait_ge(kr_lo, 2)
            pe.wait_ge(gemm_evac, T_VA + 8)
            scores(0, 0, 0)
            scores(0, 0, 1)
            strip_ready(N_PAIR + 1)
            pe.wait_ge(q_tab, 1)
            q_half(0, (N_PAIR + 1) % 2)

            def attention(i, first=False, last=False):
                turn_p(i, 0, 0, first)
                scores(i, 0, 2)
                q_half(1, (N_PAIR + 1) % 2)
                turn_p(i, 0, 1, first)
                scores(i, 0, 3)
                if not first:
                    weigh(i, -1)
                turn_p(i, 0, 2)
                scores(i, 1, 0)
                if not last:
                    strip_ready(N_PAIR + 2, i, 2)
                    pe.wait_ge(k_lo, i * 2 + 2)
                    k_product(N_PAIR % 2)
                turn_p(i, 0, 3)
                scores(i, 1, 1)
                if not last:
                    pe.wait_ge(q_tab, i * 2 + 2)
                    q_half(0, N_PAIR % 2)
                turn_p(i, 1, 0)
                scores(i, 1, 2)
                if not last:
                    q_half(1, N_PAIR % 2)
                else:
                    out_products(range(0, 2))
                turn_p(i, 1, 1)
                scores(i, 1, 3)
                if last:
                    out_products(range(2, 4))
                weigh(i, 0, (0,))
                turn_p(i, 1, 2)
                if not last:
                    scores(i, 2, 0)
                weigh(i, 0, (1,))
                if last:
                    out_products(range(4, 6))
                turn_p(i, 1, 3)
                if last:
                    out_products(range(6, 7))
                if not last:
                    scores(i, 2, 1)
                    strip_ready(N_PAIR + 3, i, 2)
                    pe.wait_ge(q_tab, i * 2 + 3)
                    q_half(0, (N_PAIR + 1) % 2)

            def side_by_side(n0, t0, ks, wait, order=lambda k: k):
                s = n0 % 2
                for k in ks:
                    if k == 0:
                        strip_ready(n0)
                        for m in range(2):
                            free_bank(t0 + m)
                    wait(k)
                    bh, bl = uh[:, order(k), :], ul[:, order(k), :]
                    for m in range(2):
                        c, o = slice(P * m, P * m + P), bank((t0 + m) % RING)
                        ah, al = full(whi[s])[:, k, c], full(wlo[s])[:, k, c]
                        mm(o, ah, bl, start=(k == 0), stop=False)
                        mm(o, ah, bh, start=False, stop=False)
                        last = mm(o, al, bh, start=False, stop=(k == KD - 1))
                        if k == KD - 1:
                            last.then_inc(gemm_done, 1)

            def out_products(ks):
                side_by_side(N_WO, T_WO, ks, lambda k: pe.wait_ge(o_lo, 2 * k + 2))

            attention(0, first=True)
            with pe.Fori(1, PAIRS - 1) as i:
                attention(i)
            attention(PAIRS - 1, last=True)

            def strips(n0, t0, js, rh, rl, order=None):
                for j in js:
                    strip_ready(n0 + j)
                    for m in range(2):
                        tile(t0 + 2 * j + m, n0 + j, P * m, rh, rl, order=order)

            weigh(PAIRS, -1)
            out_products(range(KD - 1, KD))
            strips(N_WO, T_WO, range(1, 4), uh, ul)

            def mlp_quarter(layer, i, q, first=False, last=False):
                n0, t0 = N_MLP[layer] + 8 * q, T_MLP[layer] + 16 * q
                u0 = 8 * QUARTERS * layer + 8 * q
                norm = NORM_MLP0 if layer == 0 else NORM_MLP1
                for j in range(4):
                    strip_ready(n0 + j, i, 8)
                    for m in range(2):
                        tile(t0 + 2 * j + m, n0 + j, P * m, xh, xl,
                             x_wait(1 + 2 * layer) if first and j + m == 0 else None, i, 16)
                        if first and j == 0:
                            (stat_sum, stat_spread)[m](norm)
                for j in range(4):
                    strip_ready(n0 + 4 + j, i, 8)
                    for m in range(2):
                        tile(t0 + 8 + 2 * j + m, n0 + 4 + j, P * m, uh, ul,
                             (lambda k: pe.wait_ge(u_ready, i * 8 + (u0 + k + 1))) if j + m == 0 else None, i, 16)
                        if last and layer == 1 and 2 * j + m:
                            turn_out(2 * j + m - 1)

            def turn_out(m):
                pe.wait_ge(hg_new, m + 1)
                if m >= 2:
                    pe.wait_ge(out_evac, m - 1)
                for t in range(TT):
                    ins = tr(ps[:, B_OUT + m % 2, P * t:P * t + P], hg[:, m % 2, P * t:P * t + P], ident[:])
                ins.then_inc(out_t, 1)

            def mlp(layer):
                mlp_quarter(layer, 0, 0, first=True)
                with pe.Fori(1, QUARTERS - 1) as i:
                    mlp_quarter(layer, i, 0)
                mlp_quarter(layer, 0, QUARTERS - 1, last=True)

            mlp(0)

            strip_ready(N_GATE)
            tile(T_GATE, N_GATE, 0, xh, xl, x_wait(2), width=32 + MH)
            stat_sum(NORM_MIX1)
            for j in range(4):
                strip_ready(N_QK + j)
                for m in range(2):
                    tile(T_QK + 2 * j + m, N_QK + j, P * m, xh, xl)
                    if j + m == 0:
                        stat_spread(NORM_MIX1)
            for j in range(4):
                strip_ready(N_V + j)
                s = (N_V + j) % 2
                for i in range(2):
                    t = T_V + 2 * j + i
                    free_bank(t)
                    for half in range(2):
                        part = slice(P * (2 * i + half), P * (2 * i + half) + P)
                        last = product(ps[:, t % RING, 256 * half:256 * half + 256],
                                       [((xh[:, k, part], xl[:, k, part]), (full(whi[s])[:, k, :], full(wlo[s])[:, k, :]))
                                        for k in range(8)])
                    last.then_inc(gemm_done, 1)
                if j == 1:
                    pe.wait_ge(g_m, 1)
                    pe.wait_ge(g_en, 1)
                    for c, row in ((0, Gc), (32, en)):
                        for t in range(TT):
                            last = tr(ps[:, 5, c + MH * t:c + MH * t + MH], row[:, P * t:P * t + P],
                                      ident[0:MH, 0:MH])
                    last.then_inc(g_t, 1)
            strips(N_O, T_O, range(3), xh, xl)

            def st_product(i, lead, js):
                e, pair = lead % 2, i + lead // 2
                for j in js:
                    z = 4 * lead + j
                    if z >= 2:
                        pe.wait_ge(sw_mul, i * 8 + (z - 1))
                    if j == 0:
                        pe.wait_ge(mk_ready, i * 2 + (lead + 1))
                    o = ps[:, B_ST + z % 2, 0:LEN[j]]
                    part = slice(P * j, P * j + P)
                    qt = [x[:, ds(pair, 1), P * j:S].rearrange("p a s -> p (a s)") for x in (uh, ul)]
                    product(o, [((mkh[:, e, part], mkl[:, e, part]), qt)]).then_inc(st_mm, 1)

            def numerator(i, lead):
                e = lead % 2
                part = slice(P * e, P * e + P)
                pe.wait_ge(mv_lo, i * 2 + (lead + 1))
                pe.wait_ge(sw_hi, i * 8 + (4 * lead + 4))
                for j in range(TT):
                    o = ps[:, B_NUM[e], P * j:S]
                    mm(o, mvh[:, j, part], swh(e, j), start=(j == 0), stop=False)
                    mm(o, mvl[:, j, part], swh(e, j), start=False, stop=False)
                pe.wait_ge(sw_lo, i * 8 + (4 * lead + 4))
                for j in range(TT):
                    last = mm(ps[:, B_NUM[e], P * j:S], mvh[:, j, part], swl(e, j), start=False,
                              stop=(j == TT - 1))
                last.then_inc(num_mm, 1)

            def row_sums(i, lead):
                e = lead % 2
                for j in range(TT):
                    o = ps[0:2, B_DEN, P * j:S]
                    mm(o, onesr[:], swl(e, j), start=(j == 0), stop=False)
                    last = mm(o, onesr[:], swh(e, j), start=False, stop=(j == TT - 1))
                last.then_inc(den_mm, 1)

            def head_sums(i, lead, first=False):
                e = lead % 2
                if not first:
                    pe.wait_ge(stat_read, i * 2 + lead)
                pe.wait_ge(num_sq, i * 2 + (lead + 1))
                pe.wait_ge(den_read, i * 2 + (lead + 1))
                for b in range(TT):
                    mm(ps[:, B_STAT, 4 + b:5 + b], numsq[:, e, P * b:P * b + P], ones[:, 0:1],
                       start=True, stop=True)
                for b in range(TT):
                    last = tr(ps[:, B_STAT, b:b + 1], den_row[:, P * b:P * b + P], ident[0:1, 0:1])
                last.then_inc(ms_mm, 1)

            def norm_spread(i, lead, first=False):
                pe.wait_ge(diag2_ready, i * 2 + (lead + 1))
                if not first:
                    pe.wait_ge(rb_ready, i * 2 + lead)
                mm(bank(B_BCH), ones[:], diag[:, lead % 2, :], start=True, stop=True).then_inc(bc2_mm, 1)

            def out_products2(ks):
                side_by_side(N_WO2, T_WO2, ks, lambda k: pe.wait_ge(g_ready, k + 1), order=by_head)

            def by_head(k):
                return k // 2 + 4 * (k % 2)

            def head_step(i, lead, first=False, last=False, second=False):
                if not last:
                    st_product(i, lead + 1, (0, 1))
                if not first:
                    head_sums(i, lead - 1, second)
                if not last:
                    st_product(i, lead + 1, (2,))
                else:
                    pe.wait_ge(hs_ready, MH - 2)
                numerator(i, lead)
                if not last:
                    st_product(i, lead + 1, (3,))
                row_sums(i, lead)
                if not first:
                    norm_spread(i, lead - 1, second)

            pe.wait_ge(mk_zero, 1)
            st_product(0, 0, (0, 1))
            strip_ready(N_O + 3)
            tile(T_O + 6, N_O + 3, 0, xh, xl)
            st_product(0, 0, (2, 3))
            tile(T_O + 7, N_O + 3, P, xh, xl)
            pe.wait_ge(gemm_evac, T_WO2)
            head_step(0, 0, first=True)
            head_step(0, 1, second=True)
            head_step(0, 2)
            with pe.Fori(1, MPAIRS - 1) as i:
                head_step(i, 1)
                head_step(i, 2)
            head_step(MPAIRS - 1, 1, last=True)
            head_sums(MPAIRS - 1, 1)
            out_products2(range(0, 4))
            norm_spread(MPAIRS - 1, 1)
            out_products2(range(4, 8))
            pe.wait_ge(hs_ready, MH)
            strips(N_WO2, T_WO2, range(1, 4), uh, ul, by_head)
            mlp(1)
            stat_sum(NORM_FIN, end=True)
            turn_out(KD - 1)


_INS = ["x", "positions", "norm_mix_g", "norm_mlp_g", "final_g",
        "mla_w_in", "mla_q_norm_g", "mla_kv_norm_g", "mla_w_uq", "mla_w_ukv", "mla_w_o",
        "mlstm_w_in", "mlstm_conv_w", "mlstm_conv_b", "mlstm_i_b", "mlstm_f_b", "mlstm_head_norm_g", "mlstm_w_o",
        "mlp_w1", "mlp_w2"]


def kernel(**inputs):
    import numpy as _np
    import concourse.bacc as _bacc
    from concourse import mybir as _mybir
    from concourse.bass_utils import run_bass_kernel_spmd as _run

    nc = _bacc.Bacc("TRN2", target_bir_lowering=False, num_devices=1)
    arrays, args = {}, {}
    for name in _INS:
        arr = _np.ascontiguousarray(inputs[name])
        arrays[f"in_{name}"] = arr
        args[name] = nc.dram_tensor(f"in_{name}", arr.shape, _mybir.dt.from_np(arr.dtype), kind="ExternalInput").ap()
    half = ROPE // 2
    lane = _np.arange(P) % ROPE
    freq = _np.float32(THETA) ** (-_np.arange(0, ROPE, 2, dtype=_np.float32) / _np.float32(ROPE))
    rope = _np.stack([freq[lane % half], _np.where(lane < half, -1.0, 1.0)], axis=1).astype(_np.float32)
    arrays["rope_const"] = rope
    args["rope_const"] = nc.dram_tensor("rope_const", rope.shape, _mybir.dt.float32, kind="ExternalInput").ap()
    out = nc.dram_tensor("out_h", (1, S, D), _mybir.dt.float32, kind="ExternalOutput").ap()
    trunk(nc, args, out)
    r = _run(nc, [arrays], core_ids=[0])
    return r.results[0]["out_h"]
```
